# Optimizing a Trainium2 kernel written in Bass

```python
import math
import jax, jax.numpy as jnp
from jax import lax
import numpy as np

D_MODEL = 1024
BATCH = 1
SEQ = 256
DEPTH = 1

HEAD_DIM = 64
SCALE = HEAD_DIM ** -0.5
NSA_HEADS = 8
NSA_GROUPS = 2
NSA_HPG = NSA_HEADS // NSA_GROUPS
CMP_LEN = 32
CMP_STRIDE = 16
CMP_HIDDEN = 128
SEL_BLOCK = 64
SEL_TOPN = 8
WINDOW = 256
WIN_QBLOCK = 128
MOBA_HEADS = 4
MOBA_BLOCK = 256
MOBA_TOPK = 3
MEM_LEN = 256
MEM_HEADS = 4
GATHER_QCHUNK = 32
N_BRANCHES = 3
D_FF = -(-8 * D_MODEL // (3 * 256)) * 256
REL_BUCKETS = 32
REL_MAX_DIST = 128
N_BIAS_HEADS = NSA_HEADS + MOBA_HEADS
RMS_EPS = 1e-6
NEG_INF = -1e30
FORCE_SCORE = 1e4

NSA_Q_W = NSA_HEADS * HEAD_DIM
NSA_KV_W = NSA_GROUPS * HEAD_DIM
NSA_GATE_W = NSA_HEADS * 3
MOBA_W = MOBA_HEADS * HEAD_DIM
MEM_W = MEM_HEADS * HEAD_DIM
SPLIT_SIZES = (NSA_Q_W,) + (NSA_KV_W,) * 6 + (NSA_GATE_W,) + (MOBA_W,) * 3 + (MEM_W,) + (D_MODEL,) * N_BRANCHES
IN_WIDTH = sum(SPLIT_SIZES)

kernel_name = 'hybrid_nsa_moba_memory_block'

def rms_norm(x, g):
    xf = x.astype(jnp.float32)
    y = xf * lax.rsqrt(jnp.mean(xf * xf, axis=-1, keepdims=True) + RMS_EPS)
    return (y * g.astype(jnp.float32)).astype(x.dtype)

def t5_bucket(dist):
    dist = jnp.maximum(dist, 0)
    max_exact = REL_BUCKETS // 2
    logd = jnp.log(jnp.maximum(dist, 1).astype(jnp.float32) / max_exact) / math.log(REL_MAX_DIST / max_exact)
    large = jnp.minimum(max_exact + (logd * (REL_BUCKETS - max_exact)).astype(jnp.int32), REL_BUCKETS - 1)
    return jnp.where(dist < max_exact, dist, large)

def masked_softmax(logits, mask):
    p = jax.nn.softmax(jnp.where(mask, logits, NEG_INF), axis=-1)
    return p * jnp.any(mask, axis=-1, keepdims=True)

def split_columns(t):
    points, acc = [], 0
    for size in SPLIT_SIZES[:-1]:
        acc += size
        points.append(acc)
    return jnp.split(t, points, axis=-1)

def to_heads(t, n_heads):
    b, s, _ = t.shape
    return t.reshape(b, s, n_heads, HEAD_DIM).transpose(0, 2, 1, 3)

def nsa_compressed(q, k, v, pos_k, w1_k, w2_k, pos_v, w1_v, w2_v, bias_tab):
    b, g, hpg, s, dh = q.shape
    n_cmp = (s - CMP_LEN) // CMP_STRIDE + 1
    idx = jnp.arange(n_cmp)[:, None] * CMP_STRIDE + jnp.arange(CMP_LEN)[None, :]

    def compress(t, pos, w1, w2):
        blocks = (t[:, :, idx] + pos).reshape(b, g, n_cmp, CMP_LEN * dh)
        return jax.nn.gelu(blocks @ w1) @ w2

    kc = compress(k, pos_k, w1_k, w2_k)
    vc = compress(v, pos_v, w1_v, w2_v)
    t = jnp.arange(s)
    dist = t[:, None] - (jnp.arange(n_cmp) * CMP_STRIDE + CMP_LEN - 1)[None, :]
    bias = bias_tab[t5_bucket(dist)].reshape(s, n_cmp, g, hpg).transpose(2, 3, 0, 1)
    logits = jnp.einsum('bghtd,bgcd->bghtc', q, kc).astype(jnp.float32) * SCALE + bias
    p = masked_softmax(logits, dist >= 0)
    o = jnp.einsum('bghtc,bgcd->bghtd', p.astype(vc.dtype), vc)
    return o, p

def nsa_selected(q, k, v, p_cmp, bias_tab):
    b, g, hpg, s, dh = q.shape
    n_blk = s // SEL_BLOCK
    n_cmp = p_cmp.shape[-1]
    cs = jnp.arange(n_cmp) * CMP_STRIDE
    ss = jnp.arange(n_blk) * SEL_BLOCK
    overlap = jnp.clip(jnp.minimum(cs[:, None] + CMP_LEN, ss[None, :] + SEL_BLOCK)
                       - jnp.maximum(cs[:, None], ss[None, :]), 0).astype(jnp.float32) / CMP_LEN
    imp = jnp.einsum('bghtc,cn->bgtn', p_cmp, overlap)
    t = jnp.arange(s)
    cur = (t // SEL_BLOCK)[:, None]
    blk = jnp.arange(n_blk)[None, :]
    forced = (blk == 0) | (blk == cur) | (blk == cur - 1)
    score = jnp.where(forced, FORCE_SCORE, jnp.where(blk <= cur, imp, NEG_INF))
    n_top = min(SEL_TOPN, n_blk)
    top_val, top_idx = lax.top_k(score, n_top)
    top_ok = top_val > NEG_INF / 2

    k_blk = k.reshape(b, g, n_blk, SEL_BLOCK, dh)
    v_blk = v.reshape(b, g, n_blk, SEL_BLOCK, dh)
    tab_g = bias_tab.reshape(REL_BUCKETS, g, hpg)
    qc_len = GATHER_QCHUNK
    n_chunks = s // qc_len
    bi = jnp.arange(b)[:, None, None, None]
    gi = jnp.arange(g)[None, :, None, None]
    n_keys = n_top * SEL_BLOCK

    def chunk(args):
        qc, ic, okc, t0 = args
        kg = k_blk[bi, gi, ic].reshape(b, g, qc_len, n_keys, dh)
        vg = v_blk[bi, gi, ic].reshape(b, g, qc_len, n_keys, dh)
        kpos = (ic[..., None] * SEL_BLOCK + jnp.arange(SEL_BLOCK)).reshape(b, g, qc_len, n_keys)
        dist = (t0 + jnp.arange(qc_len))[None, None, :, None] - kpos
        mask = (dist >= 0) & jnp.repeat(okc, SEL_BLOCK, axis=-1)
        bias = jnp.moveaxis(tab_g[t5_bucket(dist), gi], -1, 2)
        logits = jnp.einsum('bghqd,bgqkd->bghqk', qc, kg).astype(jnp.float32) * SCALE + bias
        p = masked_softmax(logits, mask[:, :, None])
        return jnp.einsum('bghqk,bgqkd->bghqd', p.astype(vg.dtype), vg)

    qs = jnp.moveaxis(q.reshape(b, g, hpg, n_chunks, qc_len, dh), 3, 0)
    idx_s = jnp.moveaxis(top_idx.reshape(b, g, n_chunks, qc_len, n_top), 2, 0)
    ok_s = jnp.moveaxis(top_ok.reshape(b, g, n_chunks, qc_len, n_top), 2, 0)
    t0s = jnp.arange(n_chunks, dtype=jnp.int32) * qc_len
    out = lax.map(chunk, (qs, idx_s, ok_s, t0s))
    return jnp.moveaxis(out, 0, 3).reshape(b, g, hpg, s, dh)

def nsa_window(q, k, v, bias_tab):
    b, g, hpg, s, dh = q.shape
    n_qb = s // WIN_QBLOCK
    span = WIN_QBLOCK + WINDOW
    kp = jnp.pad(k, ((0, 0), (0, 0), (WINDOW, 0), (0, 0)))
    vp = jnp.pad(v, ((0, 0), (0, 0), (WINDOW, 0), (0, 0)))
    idx = jnp.arange(n_qb)[:, None] * WIN_QBLOCK + jnp.arange(span)[None, :]
    kb = kp[:, :, idx]
    vb = vp[:, :, idx]
    qb = q.reshape(b, g, hpg, n_qb, WIN_QBLOCK, dh)
    dist = jnp.arange(WIN_QBLOCK)[:, None] - jnp.arange(span)[None, :] + WINDOW
    mask = ((dist >= 0) & (dist < WINDOW))[None] & ((idx - WINDOW) >= 0)[:, None, :]
    bias = bias_tab[t5_bucket(dist)].reshape(WIN_QBLOCK, span, g, hpg).transpose(2, 3, 0, 1)
    logits = jnp.einsum('bghnqd,bgnkd->bghnqk', qb, kb).astype(jnp.float32) * SCALE + bias[:, :, None]
    p = masked_softmax(logits, mask)
    o = jnp.einsum('bghnqk,bgnkd->bghnqd', p.astype(vb.dtype), vb)
    return o.reshape(b, g, hpg, s, dh)

def moba_attention(q, k, v, bias_tab):
    b, h, s, dh = q.shape
    n_blk = -(-s // MOBA_BLOCK)
    pad = n_blk * MOBA_BLOCK - s
    kp = jnp.pad(k, ((0, 0), (0, 0), (0, pad), (0, 0)))
    vp = jnp.pad(v, ((0, 0), (0, 0), (0, pad), (0, 0)))
    k_blk = kp.reshape(b, h, n_blk, MOBA_BLOCK, dh)
    v_blk = vp.reshape(b, h, n_blk, MOBA_BLOCK, dh)
    n_top = min(MOBA_TOPK, n_blk - 1)
    qc_len = GATHER_QCHUNK
    n_chunks = s // qc_len
    bi = jnp.arange(b)[:, None, None, None]
    hi = jnp.arange(h)[None, :, None, None]
    n_keys = n_top * MOBA_BLOCK

    def chunk(args):
        qc, t0 = args[0], args[1]
        tq = t0 + jnp.arange(qc_len)
        own = t0 // MOBA_BLOCK
        k_own = lax.dynamic_slice_in_dim(kp, own * MOBA_BLOCK, MOBA_BLOCK, axis=2)
        v_own = lax.dynamic_slice_in_dim(vp, own * MOBA_BLOCK, MOBA_BLOCK, axis=2)
        dist_own = tq[:, None] - (own * MOBA_BLOCK + jnp.arange(MOBA_BLOCK))[None, :]
        logits = (jnp.einsum('bhqd,bhkd->bhqk', qc, k_own).astype(jnp.float32) * SCALE
                  + bias_tab[t5_bucket(dist_own)].transpose(2, 0, 1))
        mask = jnp.broadcast_to(dist_own >= 0, logits.shape)
        if n_top > 0:
            ic, okc = args[2], args[3]
            kg = k_blk[bi, hi, ic].reshape(b, h, qc_len, n_keys, dh)
            vg = v_blk[bi, hi, ic].reshape(b, h, qc_len, n_keys, dh)
            kpos = (ic[..., None] * MOBA_BLOCK + jnp.arange(MOBA_BLOCK)).reshape(b, h, qc_len, n_keys)
            dist = tq[None, None, :, None] - kpos
            sel_logits = (jnp.einsum('bhqd,bhqkd->bhqk', qc, kg).astype(jnp.float32) * SCALE
                          + bias_tab[t5_bucket(dist), hi])
            logits = jnp.concatenate([sel_logits, logits], axis=-1)
            mask = jnp.concatenate([jnp.repeat(okc, MOBA_BLOCK, axis=-1), mask], axis=-1)
        p = masked_softmax(logits, mask).astype(v.dtype)
        o = jnp.einsum('bhqk,bhkd->bhqd', p[..., n_keys:], v_own)
        if n_top > 0:
            o = o + jnp.einsum('bhqk,bhqkd->bhqd', p[..., :n_keys], vg)
        return o

    qs = jnp.moveaxis(q.reshape(b, h, n_chunks, qc_len, dh), 2, 0)
    t0s = jnp.arange(n_chunks, dtype=jnp.int32) * qc_len
    if n_top > 0:
        k_mean = jnp.mean(k_blk, axis=3)
        gate = jnp.einsum('bhtd,bhnd->bhtn', q, k_mean).astype(jnp.float32)
        past = jnp.arange(n_blk)[None, :] < (jnp.arange(s) // MOBA_BLOCK)[:, None]
        top_val, top_idx = lax.top_k(jnp.where(past, gate, NEG_INF), n_top)
        top_ok = top_val > NEG_INF / 2
        idx_s = jnp.moveaxis(top_idx.reshape(b, h, n_chunks, qc_len, n_top), 2, 0)
        ok_s = jnp.moveaxis(top_ok.reshape(b, h, n_chunks, qc_len, n_top), 2, 0)
        out = lax.map(chunk, (qs, t0s, idx_s, ok_s))
    else:
        out = lax.map(chunk, (qs, t0s))
    return jnp.moveaxis(out, 0, 2).reshape(b, h, s, dh)

def memory_attention(q, mk, mv):
    logits = jnp.einsum('bhtd,bhmd->bhtm', q, mk).astype(jnp.float32) * SCALE
    p = jax.nn.softmax(logits, axis=-1).astype(mv.dtype)
    return jnp.einsum('bhtm,bhmd->bhtd', p, mv)

def merge_heads(o):
    b, h, s, dh = o.shape
    return o.transpose(0, 2, 1, 3).reshape(b, s, h * dh)

def hybrid_mixer(h, mem_n, rel_bias, w_in, cmp_pos_k, cmp_w1_k, cmp_w2_k, cmp_pos_v, cmp_w1_v, cmp_w2_v,
                 w_mem_kv, w_nsa_o, w_moba_o, w_mem_o, w_mix_out):
    b, s, _ = h.shape
    (q_n, k_c, v_c, k_s, v_s, k_w, v_w, g_n, q_m, k_m, v_m, q_x,
     gate_nsa, gate_moba, gate_mem) = split_columns(h @ w_in)

    tab_nsa = rel_bias[:, :NSA_HEADS]
    qn = to_heads(q_n, NSA_HEADS).reshape(b, NSA_GROUPS, NSA_HPG, s, HEAD_DIM)
    o_c, p_c = nsa_compressed(qn, to_heads(k_c, NSA_GROUPS), to_heads(v_c, NSA_GROUPS),
                              cmp_pos_k, cmp_w1_k, cmp_w2_k, cmp_pos_v, cmp_w1_v, cmp_w2_v, tab_nsa)
    o_s = nsa_selected(qn, to_heads(k_s, NSA_GROUPS), to_heads(v_s, NSA_GROUPS), p_c, tab_nsa)
    o_w = nsa_window(qn, to_heads(k_w, NSA_GROUPS), to_heads(v_w, NSA_GROUPS), tab_nsa)
    gb = jax.nn.sigmoid(g_n).reshape(b, s, NSA_GROUPS, NSA_HPG, 3).transpose(0, 2, 3, 1, 4)
    o_nsa = gb[..., 0:1] * o_c + gb[..., 1:2] * o_s + gb[..., 2:3] * o_w
    y_nsa = merge_heads(o_nsa.reshape(b, NSA_HEADS, s, HEAD_DIM)) @ w_nsa_o

    o_m = moba_attention(to_heads(q_m, MOBA_HEADS), to_heads(k_m, MOBA_HEADS), to_heads(v_m, MOBA_HEADS),
                         rel_bias[:, NSA_HEADS:])
    y_moba = merge_heads(o_m) @ w_moba_o

    mk, mv = jnp.split(mem_n @ w_mem_kv, 2, axis=-1)
    o_x = memory_attention(to_heads(q_x, MEM_HEADS), to_heads(mk, MEM_HEADS), to_heads(mv, MEM_HEADS))
    y_mem = merge_heads(o_x) @ w_mem_o

    merged = (jax.nn.sigmoid(gate_nsa) * y_nsa + jax.nn.sigmoid(gate_moba) * y_moba
              + jax.nn.sigmoid(gate_mem) * y_mem)
    return merged @ w_mix_out

def setup_inputs(seed: int = 0) -> dict:
    key = jax.random.key(seed)
    ks = jax.random.split(key, 24)

    def nrm(k, shape, scale):
        return jax.random.normal(k, shape, jnp.float32) * scale

    def gain(k):
        return 1.0 + 0.05 * jax.random.normal(k, (DEPTH, D_MODEL), jnp.float32)

    return {
        'x': nrm(ks[0], (BATCH, SEQ, D_MODEL), 1.0),
        'mem': nrm(ks[1], (BATCH, MEM_LEN, D_MODEL), 1.0),
        'rel_bias': nrm(ks[2], (REL_BUCKETS, N_BIAS_HEADS), 0.1),
        'pre_mix_g': gain(ks[3]),
        'mem_norm_g': gain(ks[4]),
        'post_mix_g': gain(ks[5]),
        'w_in': nrm(ks[6], (DEPTH, D_MODEL, IN_WIDTH), D_MODEL ** -0.5),
        'cmp_pos_k': nrm(ks[7], (DEPTH, CMP_LEN, HEAD_DIM), 0.02),
        'cmp_w1_k': nrm(ks[8], (DEPTH, CMP_LEN * HEAD_DIM, CMP_HIDDEN), (CMP_LEN * HEAD_DIM) ** -0.5),
        'cmp_w2_k': nrm(ks[9], (DEPTH, CMP_HIDDEN, HEAD_DIM), CMP_HIDDEN ** -0.5),
        'cmp_pos_v': nrm(ks[10], (DEPTH, CMP_LEN, HEAD_DIM), 0.02),
        'cmp_w1_v': nrm(ks[11], (DEPTH, CMP_LEN * HEAD_DIM, CMP_HIDDEN), (CMP_LEN * HEAD_DIM) ** -0.5),
        'cmp_w2_v': nrm(ks[12], (DEPTH, CMP_HIDDEN, HEAD_DIM), CMP_HIDDEN ** -0.5),
        'w_mem_kv': nrm(ks[13], (DEPTH, D_MODEL, 2 * MEM_W), D_MODEL ** -0.5),
        'w_nsa_o': nrm(ks[14], (DEPTH, NSA_Q_W, D_MODEL), NSA_Q_W ** -0.5),
        'w_moba_o': nrm(ks[15], (DEPTH, MOBA_W, D_MODEL), MOBA_W ** -0.5),
        'w_mem_o': nrm(ks[16], (DEPTH, MEM_W, D_MODEL), MEM_W ** -0.5),
        'w_mix_out': nrm(ks[17], (DEPTH, D_MODEL, D_MODEL), D_MODEL ** -0.5),
        'pre_ffn_g': gain(ks[18]),
        'post_ffn_g': gain(ks[19]),
        'w_ffn_gate': nrm(ks[20], (DEPTH, D_MODEL, D_FF), D_MODEL ** -0.5),
        'w_ffn_up': nrm(ks[21], (DEPTH, D_MODEL, D_FF), D_MODEL ** -0.5),
        'w_ffn_down': nrm(ks[22], (DEPTH, D_FF, D_MODEL), D_FF ** -0.5),
    }

def reference(x, mem, rel_bias, pre_mix_g, mem_norm_g, post_mix_g, w_in,
              cmp_pos_k, cmp_w1_k, cmp_w2_k, cmp_pos_v, cmp_w1_v, cmp_w2_v,
              w_mem_kv, w_nsa_o, w_moba_o, w_mem_o, w_mix_out,
              pre_ffn_g, post_ffn_g, w_ffn_gate, w_ffn_up, w_ffn_down):
    for l in range(DEPTH):
        h = rms_norm(x, pre_mix_g[l])
        mem_n = rms_norm(mem, mem_norm_g[l])
        y = hybrid_mixer(h, mem_n, rel_bias, w_in[l], cmp_pos_k[l], cmp_w1_k[l], cmp_w2_k[l],
                         cmp_pos_v[l], cmp_w1_v[l], cmp_w2_v[l], w_mem_kv[l],
                         w_nsa_o[l], w_moba_o[l], w_mem_o[l], w_mix_out[l])
        x = x + rms_norm(y, post_mix_g[l])
        h = rms_norm(x, pre_ffn_g[l])
        f = (jax.nn.silu(h @ w_ffn_gate[l]) * (h @ w_ffn_up[l])) @ w_ffn_down[l]
        x = x + rms_norm(f, post_ffn_g[l])
    return x


_drawn_inputs = setup_inputs


def setup_inputs(seed=0):
    import zlib

    import numpy as np

    out = dict(_drawn_inputs(seed))
    spreads = {}
    factors = {'mem_norm_g': 2.885, 'cmp_pos_k': 64.0, 'cmp_pos_v': 14.984, 'rel_bias': 3.505}
    for name, (base, spread) in spreads.items():
        noise = np.random.default_rng([zlib.crc32(name.encode()), seed]).standard_normal(out[name].shape)
        drawn = base * np.exp(spread * noise) if base else spread * noise
        out[name] = __import__('jax').numpy.asarray(drawn.astype(out[name].dtype))
    for name, factor in factors.items():
        out[name] = (out[name] * factor).astype(out[name].dtype)
    return out
```

```python
from contextlib import ExitStack

import concourse.bass as bass
from concourse import mybir

F32 = mybir.dt.float32
F32R = mybir.dt.float32r
ALU = mybir.AluOpType
ACT = mybir.ActivationFunctionType
AX = mybir.AxisListType.X

P = 128
SEQ = 256
TILES = SEQ // P
D = 1024
KD = D // P
HD = 64
SCALE = HD ** -0.5
NSA_H, GROUPS, HPG = 8, 2, 4
MOBA_H, MEM_H = 4, 4
BIAS_H = NSA_H + MOBA_H
MEM_LEN = 256
CMP_LEN, CMP_STRIDE, CMP_HID = 32, 16, 128
NCMP = (SEQ - CMP_LEN) // CMP_STRIDE + 1
PAIRS = CMP_LEN // 2
BUCKETS, MAX_DIST = 32, 128
D_FF = 2816
KF = D_FF // P
EPS = 1e-6
MASKED = -1e30

C_Q, C_KC, C_VC, C_KS, C_VS, C_KW, C_VW, C_GN = 0, 512, 640, 768, 896, 1024, 1152, 1280
C_QM, C_KM, C_VM, C_QX, C_GATES = 1304, 1560, 1816, 2072, 2328
ATT_W = C_GATES

SLICE = 512
ATT_TAIL = ATT_W - 4 * SLICE
RAW, SUBS = 4, 4
AHEAD = SUBS - 1

B_MEMKV, B_ATT, B_GATE, B_MOBA, B_MEM, B_NSA, B_MIX, B_GU, B_DOWN = 0, 1, 6, 12, 14, 16, 18, 20, 31
GU_BLOCKS, GU_W = 11, 256
U_GU, U_DOWN = 32, 54
UNITS = U_DOWN + 2 * KF // 4
V_GATE, V_MOBA, V_MEM, V_NSA, V_MIX, V_GU, V_DOWN = 24, 48, 50, 52, 56, 2 * U_GU, 2 * U_DOWN

JOBS = 24
BLK = KD * 256

QK_MK, QK_Q, QK_KC, QK_VC, QK_KS, QK_KW, QK_QM, QK_KM, QK_QX = 0, 2, 6, 7, 8, 9, 10, 12, 14

G_W, BP_W = 512, 384


def job_plan():
    jobs = []
    for m in range(MOBA_H):
        jobs.append(("moba", m, QK_QM + m // 2, m % 2, QK_KM + m // 2, NSA_H + m))
    for m in range(MEM_H):
        jobs.append(("mem", m, QK_QX + m // 2, m % 2, QK_MK + m // 2, None))
    for h in range(NSA_H):
        for kind, kb in (("sel", QK_KS), ("win", QK_KW)):
            jobs.append((kind, h, QK_Q + h % HPG, h // HPG, kb, h))
    return jobs


def pair_of(job):
    return job // 2 if job < 8 else 4 + (job - 8) // 4


def ends_pair(job):
    return job % 2 == 1 if job < 8 else (job - 8) % 4 == 3


def t_count(job):
    return 1 if job == 0 else job + 2


def build_layer(nc, a, out, g_scratch):
    jobs = job_plan()
    xf = a["x"][0].rearrange("(t p) d -> p t d", p=P)
    memf = a["mem"][0].rearrange("(t p) d -> p t d", p=P)
    outf = out[0].rearrange("(t p) d -> p t d", p=P)

    def rows(name):
        return a[name][0].rearrange("(k p) n -> p k n", p=P)

    w_in, w_memkv = rows("w_in"), rows("w_mem_kv")
    w_nsa, w_moba, w_mem, w_mix = rows("w_nsa_o"), rows("w_moba_o"), rows("w_mem_o"), rows("w_mix_out")
    w_gate, w_up, w_down = rows("w_ffn_gate"), rows("w_ffn_up"), rows("w_ffn_down")

    with ExitStack() as ctx:
        def sb(name, shape, dt=F32, stack=ctx):
            return stack.enter_context(nc.sbuf_tensor(name, shape, dt))

        def psum(name, shape):
            return ctx.enter_context(nc.psum_tensor(name, shape, F32))

        def sem(name):
            return ctx.enter_context(nc.semaphore(name))

        raw = sb("raw", [P, RAW, 4, SLICE])
        wh = sb("wh", [P, SUBS, 2, SLICE], F32R)
        wl = sb("wl", [P, SUBS, 2, SLICE], F32R)
        xh = sb("xh", [P, KD, SEQ], F32R)
        xl = sb("xl", [P, KD, SEQ], F32R)
        xs = sb("xs", [P, TILES, D])
        ident = sb("ident", [P, P])
        flip = sb("flip", [P, P])
        row_any = sb("row_any", [P, TILES])
        grows = sb("grows", [3 * KD, P])
        gcol = sb("gcol", [P, 3 * KD])
        gpost = sb("gpost", [P, D])
        eps = sb("eps", [P, 1])
        ssq = sb("ssq", [P, 8, TILES])
        rstd = sb("rstd", [P, 8, TILES])
        small = sb("small", [P, 64])
        with ExitStack() as s:
            memh = sb("memh", [P, KD, SEQ], F32R, s)
            meml = sb("meml", [P, KD, SEQ], F32R, s)
            mems = sb("mems", [P, TILES, D], F32, s)
        gates = sb("gates", [P, TILES, 3 * D])
        with ExitStack() as s:
            w1 = sb("w1", [P, 2, PAIRS, CMP_HID], F32, s)
        oh = sb("oh", [P, 8, SEQ], F32R)
        ol = sb("ol", [P, 8, SEQ], F32R)
        late = ExitStack()
        with ExitStack() as s:
            bp = sb("bp", [P, BIAS_H, BP_W], F32, s)
        with ExitStack() as s:
            pat = sb("pat", [P, TILES, ATT_W], F32, s)
            kvm = sb("kvm", [P, TILES, 2 * 256], F32, s)
            qkt = sb("qkt", [P, 16, SEQ], F32, s)
            tb = sb("tb", [P, BIAS_H, 256], F32, s)
            tbc = sb("tbc", [P, TILES, NSA_H, 16], F32, s)
            with ExitStack() as early:
                rel = sb("rel", [BUCKETS, BIAS_H], F32, early)
                onehot = sb("onehot", [BUCKETS, G_W], F32, early)
                grow = sb("grow", [BIAS_H, G_W], F32, early)
                pos2 = sb("pos2", [CMP_LEN, 2, 2, HD], F32, early)
            sx = sb("sx", [P, 2, 512], F32, s)
            pts = sb("pts", [P, 2, 512], F32, s)
            post = sb("post", [P, 2, CMP_LEN], F32, s)
            with ExitStack() as early:
                gcmp = sb("gcmp", [P, 2, PAIRS, GROUPS * NCMP], F32, early)
            pcz = sb("pcz", [P, TILES, GROUPS, HPG, 32], F32, s)
            pct = sb("pct", [P, GROUPS, SEQ], F32, s)
            w2k = sb("w2k", [CMP_HID, 2, HD], F32, s)
            w2v = sb("w2v", [CMP_HID, HD], F32, s)
            hx = sb("hx", [P, 3, 4 * NCMP], F32, s)
            hidk = sb("hidk", [P, GROUPS * NCMP], F32, s)
            hidv = sb("hidv", [P, GROUPS, HPG, 32], F32, s)
            kct = sb("kct", [P, NCMP], F32, s)
            vcz = sb("vcz", [P, GROUPS, HPG, HD], F32, s)
            xc = sb("xc", [P, TILES, NSA_H, 16], F32, s)
            cst = sb("cst", [P, 4, TILES * NSA_H], F32, s)
            gsig = sb("gsig", [P, TILES, 3 * NSA_H], F32, s)
            jst = sb("jst", [P, 5, JOBS, TILES], F32, s)
        with late:
            ah = sb("ah", [P, KF, SEQ], F32R, late)
            al = sb("al", [P, KF, SEQ], F32R, late)
            yb = sb("yb", [P, TILES, D], F32, late)
            tmp = sb("tmp", [P, TILES, SLICE], F32, late)
            silu = sb("silu", [P, TILES, GU_W], F32, late)
            act_tok = sb("act_tok", [P, TILES, GU_W], F32, late)

        acc = psum("acc", [P, 2, TILES, 512])
        sbank = psum("sbank", [P, 2, 512])
        ptb = psum("ptb", [P, 512])
        ob = psum("ob", [P, 512])
        quad = [sbank[:, 0], sbank[:, 1], ptb[:], ob[:]]

        loaded = [sem(f"loaded{i}") for i in range(RAW)]
        hi_done = sem("hi_done")
        lo_done = sem("lo_done")
        mm_done = sem("mm_done")
        acc0_done = sem("acc0_done")
        ev = [sem("ev0"), sem("ev1")]
        xd, memd, constd = sem("xd"), sem("memd"), sem("constd")
        reld, cmpd, gpostd, g_stored, bp_d, out_d = (sem("reld"), sem("cmpd"), sem("gpostd"), sem("g_stored"),
                                                     sem("bp_d"), sem("out_d"))
        dve_c, act_c = sem("dve_c"), sem("act_c")
        ssq_done = sem("ssq_done")
        root_done = sem("root_done")
        rstd_done = sem("rstd_done")
        tp_done, th_done, tl_done = sem("tp_done"), sem("th_done"), sem("tl_done")
        pre_pe, pre_dve, pre_act = sem("pre_pe"), sem("pre_dve"), sem("pre_act")
        grow_done = sem("grow_done")
        tb_pe, tb_ev = sem("tb_pe"), [sem("tb_ev0"), sem("tb_ev1")]
        qk_pe, qk_ev = sem("qk_pe"), [sem("qk_ev0"), sem("qk_ev1")]
        cmp_g, cmp_pe, cmp_dve, cmp_act = sem("cmp_g"), sem("cmp_pe"), sem("cmp_dve"), sem("cmp_act")
        s_done, x_done, e_done, r_done, p_done = (sem("s_done"), sem("x_done"), sem("e_done"), sem("r_done"),
                                                  sem("p_done"))
        t_done, te_done, pv_done = sem("t_done"), sem("te_done"), sem("pv_done")
        oh_done, ol_done = sem("oh_done"), sem("ol_done")
        silu_done, prod_done, at_done, ah_done, al_done = (sem("silu_done"), sem("prod_done"), sem("at_done"),
                                                           sem("ah_done"), sem("al_done"))
        y_done, x1_done, fin_done = sem("y_done"), sem("x1_done"), sem("fin_done")

        block = ctx.enter_context(nc.Block())

        def width(v):
            return ATT_TAIL if v // 4 == B_ATT + 4 else SLICE

        def prob_cols(kind, t):
            if kind == "mem":
                return 256 * t, 256 * t + 256
            return (0, 128) if t == 0 else (128, 384)

        def pair_queries(dst, src):
            return (dst.rearrange("p (i g d) -> p g i d", g=GROUPS, i=HPG),
                    src.rearrange("p (g i d) -> p g i d", g=GROUPS, i=HPG))

        @block.sync
        def _(sp):
            def free_slot(u):
                if isinstance(u, int) and u < RAW:
                    return
                sp.wait_ge(lo_done, 2 * (u - RAW) + 2)

            def unit(u, slot, parts):
                free_slot(u)
                for dst, src in parts:
                    sp.dma_start(dst, src).then_inc(loaded[slot], 32 // len(parts))

            def plain(u, src, k0, c0, w=SLICE):
                unit(u, u % RAW, [(raw[:, u % RAW, :, 0:w], src[:, k0:k0 + 4, c0:c0 + w])])

            u = 0
            for half in range(2):
                plain(u, w_memkv, 4 * half, 0)
                u += 1
            for b in range(5):
                for half in range(2):
                    plain(u, w_in, 4 * half, SLICE * b, SLICE if b < 4 else ATT_TAIL)
                    u += 1
            for b in range(6):
                for half in range(2):
                    plain(u, w_in, 4 * half, C_GATES + SLICE * b)
                    u += 1
            for w in (w_moba, w_mem):
                unit(u, u % RAW, [(raw[:, u % RAW, 2 * n:2 * n + 2, :], w[:, :, SLICE * n:SLICE * n + SLICE])
                                  for n in range(2)])
                u += 1
            for n in range(2):
                plain(u, w_nsa, 0, SLICE * n)
                u += 1
            for n in range(2):
                for half in range(2):
                    plain(u, w_mix, 4 * half, SLICE * n)
                    u += 1

            def gate_up(i, j):
                for half in range(2):
                    u, slot = U_GU + 2 * i + half, (2 * j + half) % RAW
                    unit(u, slot, [(raw[:, slot, :, GU_W * c:GU_W * c + GU_W],
                                    w[:, 4 * half:4 * half + 4, bass.ds(i * GU_W, GU_W)])
                                   for c, w in enumerate((w_gate, w_up))])

            gate_up(0, 0)
            with nc.sync.Fori(0, (GU_BLOCKS - 1) // 2) as it:
                for j in range(2):
                    gate_up(it * 2 + (1 + j), 1 - j)
            for j in range(2 * KF // 4):
                u = U_DOWN + j
                cut = []
                for c in (0, 2):
                    n, k = divmod(4 * j + c, KF)
                    cut.append((raw[:, u % RAW, c:c + 2, :], w_down[:, k:k + 2, SLICE * n:SLICE * n + SLICE]))
                unit(u, u % RAW, cut)
            for t in range(TILES):
                sp.wait_ge(fin_done, t + 1)
                sp.dma_start(outf[:, t], xs[:, t]).then_inc(out_d, 16)
            sp.wait_ge(out_d, 16 * TILES)

        @block.gpsimd
        def _(pool):
            nc.gpsimd.dma_start(rel[:], a["rel_bias"]).then_inc(reld, 16)
            nc.gpsimd.dma_start(onehot[:], a["bucket_onehot"]).then_inc(reld, 16)
            for kv, name in enumerate(("cmp_pos_k", "cmp_pos_v")):
                for rep in range(2):
                    nc.gpsimd.dma_start(pos2[:, kv, rep, :], a[name][0]).then_inc(cmpd, 16)
            for kv, name in enumerate(("cmp_w1_k", "cmp_w1_v")):
                nc.gpsimd.dma_start(w1[:, kv], a[name][0].rearrange("(j p) n -> p j n", p=P)).then_inc(cmpd, 16)
            for rep in range(2):
                nc.gpsimd.dma_start(w2k[:, rep, :], a["cmp_w2_k"][0]).then_inc(cmpd, 16)
            nc.gpsimd.dma_start(w2v[:], a["cmp_w2_v"][0]).then_inc(cmpd, 16)
            pool.wait_ge(grow_done, 2)
            nc.gpsimd.dma_start(g_scratch, grow[:]).then_inc(g_stored, 16)
            pool.wait_ge(g_stored, 16)
            nc.gpsimd.dma_start(bp[:], bass.AP(g_scratch.tensor, 0, [[1, P], [G_W, BIAS_H], [1, BP_W]])).then_inc(bp_d, 16)
            nc.gpsimd.dma_start(gpost[:], bass.AP(a["post_mix_g"].tensor, 0, [[0, P], [1, D]])).then_inc(gpostd, 16)
            for n, (kind, *_r) in enumerate(jobs):
                pool.wait_ge(r_done, n + 1)
                for t in range(TILES):
                    lo, hi = prob_cols(kind, t)
                    ins = nc.gpsimd.tensor_scalar(sx[:, n % 2, lo:hi], sx[:, n % 2, lo:hi], jst[:, 4, n, t:t + 1], 1.0,
                                                  ALU.mult, ALU.mult)
                ins.then_inc(p_done, 1)
            pool.wait_ge(x1_done, TILES)
            nc.gpsimd.dma_start(gpost[:], bass.AP(a["post_ffn_g"].tensor, 0, [[0, P], [1, D]])).then_inc(gpostd, 16)

        @block.scalar
        def _(act):
            for name, dst in (("const_ident", ident), ("const_flip", flip), ("const_any", row_any)):
                nc.scalar.dma_start(dst[:], a[name]).then_inc(constd, 16)
            for i, name in enumerate(("pre_mix_g", "mem_norm_g", "pre_ffn_g")):
                nc.scalar.dma_start(grows[KD * i:KD * i + KD, :], a[name][0].rearrange("(k p) -> k p", p=P)).then_inc(constd, 16)
            nc.scalar.dma_start(mems[:], memf).then_inc(memd, 16)
            nc.scalar.dma_start(xs[:], xf).then_inc(xd, 16)

            split = [0]

            def hi(v, slot, half, w, first_load):
                act.wait_ge(loaded[slot], first_load)
                if not (isinstance(v, int) and v < SUBS):
                    act.wait_ge(mm_done, v - SUBS + 1)
                k = (2 * slot + half) % SUBS
                nc.scalar.activation(wh[:, k, :, 0:w], raw[:, slot, 2 * half:2 * half + 2, 0:w], ACT.Copy).then_inc(hi_done, 1)

            def hi_to(v_end):
                while split[0] <= min(v_end, 2 * UNITS - 1):
                    v = split[0]
                    u = v // 2
                    hi(v, u % RAW, v % 2, width(v), 32 * (u // RAW + 1))
                    split[0] += 1

            chain = [0]

            def link(ins):
                chain[0] += 1
                ins.then_inc(act_c, 1)
                act.wait_ge(act_c, chain[0])

            def wait_block(b, t, v_last):
                if t == 0:
                    act.wait_ge(acc0_done, b + 1)
                else:
                    act.wait_ge(mm_done, v_last + 1)

            def round_hi(r, j):
                act.wait_ge(tp_done, 4 * r + j + 1)
                bank = (acc[:, j // 2, j % 2] if r == 1 else quad[j])
                dst = memh if r == 0 else xh
                for kk in range(2):
                    k = 2 * j + kk
                    g = {0: KD + k, 1: k, 3: 2 * KD + k}.get(r)
                    scale = 0.5 if r == 2 else gcol[:, g:g + 1]
                    ins = nc.scalar.activation(dst[:, k, :], bank[:, 256 * kk:256 * kk + 256], ACT.Copy, scale=scale)
                ins.then_inc(th_done, 1)

            act.wait_ge(pre_dve, 1)
            act.wait_ge(pre_dve, 2)
            for j in range(4):
                round_hi(0, j)
            for j in range(4):
                round_hi(1, j)
            for i in range(2):
                act.wait_ge(ssq_done, 4 * (i + 1) // 2)
                nc.scalar.activation(small[:, 2 * i:2 * i + 2], ssq[:, i, :], ACT.Sqrt, bias=eps[:], scale=1.0 / D).then_inc(root_done, 1)
            hi_to(AHEAD)

            def evac_cols(b):
                v_last = 4 * b + 3
                hi_to(v_last + AHEAD)
                act.wait_ge(rstd_done, 1 if b == 0 else 2)
                wait_block(b, 0, v_last)
                if b == 0:
                    dst, i, w = kvm[:, 0, :], 0, SLICE
                else:
                    w = ATT_TAIL if b == 5 else SLICE
                    dst, i = pat[:, 0, SLICE * (b - 1):SLICE * (b - 1) + w], 1
                src = acc[:, b % 2, 0, 0:w]
                if b == B_ATT:
                    dst, src = pair_queries(dst, src)
                nc.scalar.activation(dst, src, ACT.Copy, scale=rstd[:, i, 0:1]).then_inc(ev[0], 1)

            def evac_qk(beta):
                act.wait_ge(qk_pe, beta + 1)
                nc.scalar.activation(qkt[:, 2 * beta:2 * beta + 2, :], sbank[:, beta % 2], ACT.Copy).then_inc(qk_ev[0], 1)

            evac_cols(0)
            for i in (0, 2, 4):
                act.wait_ge(tb_pe, i + 1)
                nc.scalar.activation(tb[:, 2 * i:2 * i + 2, :], ptb[:], ACT.Copy).then_inc(tb_ev[0], 1)
            evac_cols(1)
            evac_qk(0)
            evac_cols(2)
            evac_qk(2)
            evac_cols(3)
            evac_cols(4)
            evac_qk(4)
            act.wait_ge(cmp_dve, 1)
            nc.scalar.activation(hx[:, 2, :], hx[:, 1, :], ACT.Tanh, scale=0.7978845608028654).then_inc(cmp_act, 1)
            evac_cols(5)
            evac_qk(6)
            act.wait_ge(ev[0], B_ATT + 3)
            act.wait_ge(ev[1], B_ATT + 3)
            nc.scalar.activation(gsig[:], pat[:, :, C_GN:C_GN + 3 * NSA_H], ACT.Tanh, scale=0.5).then_inc(cmp_act, 1)

            def evac_gate(b):
                for t in range(TILES):
                    wait_block(b, t, 4 * b + 3)
                    c = SLICE * (b - B_GATE)
                    nc.scalar.activation(gates[:, t, c:c + SLICE], acc[:, b % 2, t], ACT.Tanh,
                                         scale=rstd[:, 4, t:t + 1]).then_inc(ev[t], 1)

            def evac_pt(n):
                act.wait_ge(t_done, t_count(n))
                if n >= 2:
                    act.wait_ge(pv_done, n - 1)
                w = 512 if jobs[n][0] == "mem" else 384
                nc.scalar.activation(pts[:, n % 2, 0:w], ptb[:, 0:w], ACT.Copy).then_inc(te_done, 1)

            def evac_o(n):
                if ends_pair(n):
                    act.wait_ge(pv_done, n + 1)
                    nc.scalar.activation(oh[:, pair_of(n), :], ob[:, 0:256], ACT.Copy).then_inc(oh_done, 1)

            for n in range(JOBS + 2):
                hi_to(V_GATE + n + AHEAD)
                if n < JOBS:
                    kind = jobs[n][0]
                    act.wait_ge(x_done, n + 1)
                    src = sbank if kind == "mem" else sx
                    if n >= 2:
                        act.wait_ge(t_done, t_count(n - 2))
                    for t in range(TILES):
                        lo, hic = prob_cols(kind, t)
                        ins = nc.scalar.activation(sx[:, n % 2, lo:hic], src[:, n % 2, lo:hic], ACT.Exp,
                                                   bias=jst[:, 1, n, t:t + 1], scale=SCALE,
                                                   accum_out=jst[:, 2, n, t:t + 1])
                    ins.then_inc(e_done, 1)
                    if n == 1:
                        act.wait_ge(cmp_dve, 4)
                        nc.scalar.activation(xc[:, :, :, 0:NCMP], xc[:, :, :, 0:NCMP], ACT.Exp, scale=SCALE).then_inc(cmp_act, 1)
                    if n % 4 == 3:
                        evac_gate(B_GATE + n // 4)
                if n == 2:
                    act.wait_ge(t_done, 2)
                    nc.scalar.activation(pct[:], ptb[:], ACT.Copy).then_inc(te_done, 1)
                if 1 <= n <= JOBS:
                    evac_pt(n - 1)
                if n >= 2:
                    evac_o(n - 2)

            hi_to(V_NSA + 3 + AHEAD)
            for j in range(4):
                round_hi(2, j)

            def evac_y(b, v_last):
                c = SLICE * ((b - B_MIX) % 2 if b < B_GU else b - B_DOWN)
                for t in range(TILES):
                    wait_block(b, t, v_last)
                    nc.scalar.activation(yb[:, t, c:c + SLICE], acc[:, b % 2, t], ACT.Copy).then_inc(ev[t], 1)

            for n in range(2):
                v_last = V_MIX + 4 * n + 3
                hi_to(v_last + AHEAD)
                evac_y(B_MIX + n, v_last)

            def root(i):
                for t in range(TILES):
                    act.wait_ge(ssq_done, 2 * i + t + 1)
                    nc.scalar.activation(small[:, 2 * i + t:2 * i + t + 1], ssq[:, i, t:t + 1], ACT.Sqrt, bias=eps[:],
                                         scale=1.0 / D).then_inc(root_done, 1)

            root(2)
            for j in range(4):
                round_hi(3, j)
            root(3)

            nc.scalar.preload_act_table(ACT.Silu)

            def ffn_hi(i, j, s):
                v = V_GU + AHEAD + s + 4 * i
                vj = AHEAD + s + 4 * j
                hi(v, (vj // 2) % RAW, vj % 2, SLICE, ((V_GU + vj) // 2 // RAW + 1) * 32 + (i - j) * 16)

            def ffn_ah(i):
                act.wait_ge(at_done, i + 1)
                nc.scalar.activation(ah[:, bass.ds(i * 2, 2), :], ptb[:], ACT.Copy).then_inc(ah_done, 1)

            def ffn_act(i, j, first):
                for s in range(4):
                    ffn_hi(i, j, s)
                    if s == 2 and not first:
                        ffn_ah(i - 1)
                for t in range(TILES):
                    if t == 0:
                        act.wait_ge(acc0_done, i + (B_GU + 1))
                    else:
                        act.wait_ge(mm_done, i * 4 + (V_GU + 4))
                    if not first:
                        act.wait_ge(prod_done, i * 2 + (t - 1))
                    nc.scalar.activation(silu[:, t], acc[:, j % 2, t, 0:GU_W], ACT.Silu, scale=rstd[:, 3, t:t + 1]).then_inc(silu_done, 1)

            act.wait_ge(rstd_done, 4)
            ffn_act(0, 0, True)
            with nc.scalar.Fori(0, (GU_BLOCKS - 1) // 2) as it:
                for j in range(2):
                    ffn_act(it * 2 + (1 + j), 1 - j, False)
            split[0] = V_GU + 4 * GU_BLOCKS + AHEAD
            hi_to(V_DOWN + 2 + AHEAD)
            ffn_ah(GU_BLOCKS - 1)
            for n in range(2):
                v_last = V_DOWN + 11 * n + 10
                hi_to(v_last + AHEAD)
                evac_y(B_DOWN + n, v_last)
            root(4)

        @block.vector
        def _(dve):
            split = [0]

            def lo(v, slot, half, w):
                dve.wait_ge(hi_done, v + 1)
                k = (2 * slot + half) % SUBS
                nc.vector.tensor_tensor(wl[:, k, :, 0:w], raw[:, slot, 2 * half:2 * half + 2, 0:w],
                                        wh[:, k, :, 0:w].bitcast(F32), ALU.subtract).then_inc(lo_done, 1)

            def lo_to(v_end):
                while split[0] <= min(v_end, 2 * UNITS - 1):
                    v = split[0]
                    lo(v, v // 2 % RAW, v % 2, width(v))
                    split[0] += 1

            chain = [0]

            def link(ins):
                chain[0] += 1
                ins.then_inc(dve_c, 1)
                dve.wait_ge(dve_c, chain[0])

            def wait_block(b, t, v_last):
                if t == 0:
                    dve.wait_ge(acc0_done, b + 1)
                else:
                    dve.wait_ge(mm_done, v_last + 1)

            def round_lo(r, j):
                dve.wait_ge(th_done, 4 * r + j + 1)
                bank = (acc[:, j // 2, j % 2] if r == 1 else quad[j])
                h, l = (memh, meml) if r == 0 else (xh, xl)
                for kk in range(2):
                    k = 2 * j + kk
                    g = {0: KD + k, 1: k, 3: 2 * KD + k}.get(r)
                    scale = 0.5 if r == 2 else gcol[:, g:g + 1]
                    ins = nc.vector.scalar_tensor_tensor(l[:, k, :], bank[:, 256 * kk:256 * kk + 256], scale,
                                                         h[:, k, :].bitcast(F32), ALU.mult, ALU.subtract)
                ins.then_inc(tl_done, 1)

            nc.vector.memset(eps[:], EPS).then_inc(pre_dve, 1)
            dve.wait_ge(pre_pe, 1)
            link(nc.vector.tensor_copy(gcol[:], ob[:, 0:3 * KD]))
            nc.vector.tensor_copy(post[:], ob[:, 32:32 + 2 * CMP_LEN].rearrange("p (a j) -> p a j", a=2)).then_inc(pre_dve, 1)
            dve.wait_ge(pre_pe, 2)
            nc.vector.tensor_scalar(grow[:, 0:256], ptb[0:BIAS_H, 0:256], 1.0 / SCALE, None, ALU.mult).then_inc(grow_done, 1)
            nc.vector.memset(grow[:, 256:G_W], MASKED / SCALE).then_inc(grow_done, 1)
            nc.vector.memset(hidv[:], 0.0)
            link(nc.vector.memset(vcz[:], 0.0))

            def sum_squares(i, t, src, junk):
                return nc.vector.tensor_tensor_reduce(out=junk, in0=src, in1=src, scale=1.0, scalar=0.0, op0=ALU.mult,
                                                      op1=ALU.add, accum_out=ssq[:, i, t:t + 1])

            junk = qkt[:].rearrange("p (j a) n -> p j (a n)", j=4)
            dve.wait_ge(memd, 16)
            for t in range(TILES):
                sum_squares(0, t, mems[:, t], junk[:, t]).then_inc(ssq_done, 1)
            for j in range(4):
                round_lo(0, j)
            dve.wait_ge(xd, 16)
            for t in range(TILES):
                sum_squares(1, t, xs[:, t], junk[:, 2 + t]).then_inc(ssq_done, 1)
            for j in range(4):
                round_lo(1, j)
            lo_to(AHEAD)
            for i in range(2):
                dve.wait_ge(root_done, i + 1)
                nc.vector.reciprocal(rstd[:, i, :], small[:, 2 * i:2 * i + 2]).then_inc(rstd_done, 1)
            dve.wait_ge(rstd_done, 2)
            link(nc.vector.tensor_scalar(rstd[:, 4, :], rstd[:, 1, :], 0.5, None, ALU.mult))

            def evac_cols(b):
                v_last = 4 * b + 3
                lo_to(v_last + AHEAD)
                wait_block(b, 1, v_last)
                if b == 0:
                    dst, i, w = kvm[:, 1, :], 0, SLICE
                else:
                    w = ATT_TAIL if b == 5 else SLICE
                    dst, i = pat[:, 1, SLICE * (b - 1):SLICE * (b - 1) + w], 1
                src = acc[:, b % 2, 1, 0:w]
                if b == B_ATT:
                    dst, src = pair_queries(dst, src)
                nc.vector.tensor_scalar(dst, src, rstd[:, i, 1:2], None, ALU.mult).then_inc(ev[1], 1)

            def evac_qk(beta):
                dve.wait_ge(qk_pe, beta + 1)
                nc.vector.tensor_copy(qkt[:, 2 * beta:2 * beta + 2, :], sbank[:, beta % 2].rearrange("p (a n) -> p a n", a=2)).then_inc(qk_ev[1], 1)

            evac_cols(0)
            for i in (1, 3, 5):
                dve.wait_ge(tb_pe, i + 1)
                nc.vector.tensor_copy(tb[:, 2 * i:2 * i + 2, :], ob[:].rearrange("p (a n) -> p a n", a=2)).then_inc(tb_ev[1], 1)
            dve.wait_ge(tb_pe, 7)
            nc.vector.tensor_copy(tbc[:, :, :, 0:NCMP], ob[:, 0:256].rearrange("p (t h c) -> p t h c", t=2, h=NSA_H)[:, :, :, 0:NCMP]).then_inc(tb_ev[1], 1)
            evac_cols(1)
            evac_cols(2)
            evac_qk(1)
            evac_cols(3)
            evac_qk(3)
            dve.wait_ge(qk_ev[1], 2)
            for kv in range(2):
                for g in range(GROUPS):
                    for jj in range(2):
                        src = qkt[HD * g:HD * g + HD, QK_KC + kv, jj:jj + 1]
                        pos = post[HD * g:HD * g + HD, kv, jj:jj + 1]
                        ins = nc.vector.tensor_tensor(
                            gcmp[HD * jj:HD * jj + HD, kv, :, NCMP * g:NCMP * g + NCMP],
                            bass.AP(src.tensor, src.offset, [src.ap[0], [2, PAIRS], [CMP_STRIDE, NCMP]]),
                            bass.AP(pos.tensor, pos.offset, [pos.ap[0], [2, PAIRS], [0, NCMP]]), ALU.add)
            ins.then_inc(cmp_g, 1)
            evac_cols(4)
            dve.wait_ge(cmp_pe, 1)
            nc.vector.memset(pcz[:], 0.0)
            link(nc.vector.tensor_copy(hx[:, 0, :], ob[:, 0:4 * NCMP]))
            link(nc.vector.tensor_tensor(hx[:, 1, :], hx[:, 0, :], hx[:, 0, :], ALU.mult))
            link(nc.vector.tensor_scalar(hx[:, 1, :], hx[:, 1, :], 0.044715, 1.0, ALU.mult, ALU.add))
            nc.vector.tensor_tensor(hx[:, 1, :], hx[:, 1, :], hx[:, 0, :], ALU.mult).then_inc(cmp_dve, 1)
            dve.wait_ge(cmp_act, 1)
            link(nc.vector.scalar_tensor_tensor(hx[:, 2, :], hx[:, 2, :], 1.0, hx[:, 0, :], ALU.add, ALU.mult))
            nc.vector.tensor_scalar(hidk[:], hx[:, 2, 0:2 * NCMP], 0.5, None, ALU.mult)
            for i in range(HPG):
                ins = nc.vector.tensor_scalar(hidv[:, :, i, 0:NCMP],
                                              hx[:, 2, 2 * NCMP:4 * NCMP].rearrange("p (g c) -> p g c", g=GROUPS),
                                              0.5, None, ALU.mult)
            ins.then_inc(cmp_dve, 1)
            evac_cols(5)
            evac_qk(5)
            dve.wait_ge(cmp_pe, 2)
            for g in range(GROUPS):
                nc.vector.tensor_copy(kct[HD * g:HD * g + HD, :], ob[HD * g:HD * g + HD, 64 + NCMP * g:64 + NCMP * g + NCMP])
            for i in range(HPG):
                ins = nc.vector.tensor_copy(vcz[32 * i:32 * i + 32, :, i, :],
                                            ob[32 * i:32 * i + 32, 128:256].rearrange("p (g d) -> p g d", g=GROUPS))
            ins.then_inc(cmp_dve, 1)
            dve.wait_ge(cmp_act, 2)
            link(nc.vector.tensor_scalar(gsig[:], gsig[:], 0.5, 0.5, ALU.mult, ALU.add))
            gview = gsig[:].rearrange("p t (h b) -> p t h b", b=3)

            for n in range(JOBS + 2):
                if n < JOBS:
                    kind, h, _qb, _qh, _kb, bh = jobs[n]
                    dve.wait_ge(s_done, n + 1)
                    if kind == "mem":
                        link(nc.vector.tensor_reduce(jst[:, 0, n, :], sbank[:, n % 2].rearrange("p (t k) -> p t k", t=2), AX, ALU.max))
                    else:
                        if n >= 2:
                            dve.wait_ge(t_done, t_count(n - 2))
                        for t in range(TILES):
                            c0, c1 = prob_cols(kind, t)
                            nc.vector.tensor_tensor(sx[:, n % 2, c0:c1], sbank[:, n % 2, c0:c1], tb[:, bh, 128 * (1 - t):256], ALU.add).then_inc(dve_c, 1)
                            chain[0] += 1
                        dve.wait_ge(dve_c, chain[0] - 1)
                        for t in range(TILES):
                            c0, c1 = prob_cols(kind, t)
                            if t == 1:
                                dve.wait_ge(dve_c, chain[0])
                            ins = nc.vector.reduce_max(jst[:, 0, n, t:t + 1], sx[:, n % 2, c0:c1], axis=AX)
                        link(ins)
                    nc.vector.tensor_scalar(jst[:, 1, n, :], jst[:, 0, n, :], -SCALE, None, ALU.mult).then_inc(x_done, 1)
                lo_to(V_GATE + n + AHEAD)
                if n < JOBS:
                    dve.wait_ge(e_done, n + 1)
                    if kind in ("sel", "win"):
                        link(nc.vector.reciprocal(jst[:, 3, n, :], jst[:, 2, n, :]))
                        nc.vector.tensor_tensor(jst[:, 4, n, :], jst[:, 3, n, :], gview[:, :, h, 1 if kind == "sel" else 2], ALU.mult).then_inc(r_done, 1)
                    else:
                        nc.vector.reciprocal(jst[:, 4, n, :], jst[:, 2, n, :]).then_inc(r_done, 1)
                if n == 0:
                    x16 = xc[:].rearrange("p t h c -> p (t h) c")[:, :, 0:NCMP]
                    dve.wait_ge(cmp_pe, 3)
                    for g, bank in enumerate((ob, ptb)):
                        hs = slice(HPG * g, HPG * g + HPG)
                        ins = nc.vector.tensor_tensor(xc[:, :, hs, 0:NCMP],
                                                      bank[:, 0:P].rearrange("p (t h c) -> p t h c", t=2, h=HPG)[:, :, :, 0:NCMP],
                                                      tbc[:, :, hs, 0:NCMP], ALU.add)
                    link(ins)
                    link(nc.vector.tensor_reduce(cst[:, 0, :], x16, AX, ALU.max))
                    m16 = cst[:, 0, :]
                    nc.vector.tensor_tensor(x16, x16, bass.AP(m16.tensor, m16.offset, [m16.ap[0], [1, 16], [0, NCMP]]), ALU.subtract).then_inc(cmp_dve, 1)
                    evac_qk(7)
                if n == 1:
                    dve.wait_ge(cmp_act, 3)
                    link(nc.vector.tensor_reduce(cst[:, 1, :], x16, AX, ALU.add))
                    link(nc.vector.reciprocal(cst[:, 2, :], cst[:, 1, :]))
                    link(nc.vector.tensor_tensor(cst[:, 3, :].rearrange("p (t h) -> p t h", t=2), cst[:, 2, :].rearrange("p (t h) -> p t h", t=2), gview[:, :, :, 0], ALU.mult))
                    for t in range(TILES):
                        f8 = cst[:, 3, NSA_H * t:NSA_H * t + NSA_H]
                        ins = nc.vector.scalar_tensor_tensor(
                            pcz[:, t].rearrange("p g i c -> p (g i) c")[:, :, 0:NCMP], xc[:, t, :, 0:NCMP], row_any[:, t:t + 1],
                            bass.AP(f8.tensor, f8.offset, [f8.ap[0], [1, NSA_H], [0, NCMP]]), ALU.mult, ALU.mult)
                    ins.then_inc(cmp_dve, 1)
                if n >= 2 and ends_pair(n - 2):
                    p = pair_of(n - 2)
                    dve.wait_ge(oh_done, p + 1)
                    nc.vector.tensor_tensor(ol[:, p, :], ob[:, 0:256], oh[:, p, :].bitcast(F32), ALU.subtract).then_inc(ol_done, 1)

            for b in range(B_MOBA, B_MIX):
                c = SLICE * (b % 2)
                branch = {B_MOBA: 1, B_MEM: 2, B_NSA: 0}[b - b % 2]
                v_last = V_MOBA + b - B_MOBA if b < B_NSA else V_NSA + 2 * (b - B_NSA) + 1
                lo_to(v_last + AHEAD)
                for t in range(TILES):
                    wait_block(b, t, v_last)
                    g = gates[:, t, D * branch + c:D * branch + c + SLICE]
                    if b < B_MEM:
                        nc.vector.scalar_tensor_tensor(yb[:, t, c:c + SLICE], g, 1.0, acc[:, b % 2, t], ALU.add, ALU.mult).then_inc(ev[t], 1)
                    else:
                        nc.vector.scalar_tensor_tensor(tmp[:, t], g, 1.0, acc[:, b % 2, t], ALU.add, ALU.mult).then_inc(ev[t], 1)
                        dve.wait_ge(ev[t], b + 1)
                        ins = nc.vector.tensor_tensor(yb[:, t, c:c + SLICE], yb[:, t, c:c + SLICE], tmp[:, t], ALU.add)
                        if b >= B_NSA:
                            ins.then_inc(y_done, 1)
                        else:
                            link(ins)
            for j in range(4):
                round_lo(2, j)
            for n in range(2):
                lo_to(V_MIX + 4 * n + 3 + AHEAD)

            def norm_sum(b, i, first_ev):
                for t in range(TILES):
                    dve.wait_ge(ev[t], first_ev + 2)
                    dve.wait_ge(ssq_done, 2 * i + t)
                    sum_squares(i, t, yb[:, t], tmp_all[:, 0:D]).then_inc(ssq_done, 1)

            tmp_all = tmp[:].rearrange("p t n -> p (t n)")
            dve.wait_ge(gpostd, 16)
            norm_sum(B_MIX, 2, B_MIX)
            for t in range(TILES):
                dve.wait_ge(root_done, 3 + t)
                link(nc.vector.reciprocal(rstd[:, 2, t:t + 1], small[:, 4 + t:5 + t]))
                link(nc.vector.scalar_tensor_tensor(yb[:, t], yb[:, t], rstd[:, 2, t:t + 1], gpost[:], ALU.mult, ALU.mult))
                nc.vector.tensor_tensor(xs[:, t], xs[:, t], yb[:, t], ALU.add).then_inc(x1_done, 1)
            for t in range(TILES):
                dve.wait_ge(x1_done, t + 1)
                dve.wait_ge(ssq_done, 6 + t)
                sum_squares(3, t, xs[:, t], tmp_all[:, 0:D]).then_inc(ssq_done, 1)
            for j in range(4):
                round_lo(3, j)
            for t in range(TILES):
                dve.wait_ge(root_done, 5 + t)
                nc.vector.reciprocal(rstd[:, 3, t:t + 1], small[:, 6 + t:7 + t]).then_inc(rstd_done, 1)
            dve.wait_ge(rstd_done, 4)

            def ffn_lo(i, j, s):
                vj = AHEAD + s + 4 * j
                lo(V_GU + AHEAD + s + 4 * i, (vj // 2) % RAW, vj % 2, SLICE)

            def ffn_al(i):
                dve.wait_ge(ah_done, i + 1)
                nc.vector.tensor_tensor(al[:, bass.ds(i * 2, 2), :], ptb[:].rearrange("p (k n) -> p k n", k=2),
                                        ah[:, bass.ds(i * 2, 2), :].bitcast(F32), ALU.subtract).then_inc(al_done, 1)

            def ffn_dve(i, j, first):
                for s in range(4):
                    ffn_lo(i, j, s)
                    if s == 2 and not first:
                        ffn_al(i - 1)
                for t in range(TILES):
                    dve.wait_ge(silu_done, i * 2 + (t + 1))
                    if not first:
                        dve.wait_ge(at_done, i)
                    nc.vector.scalar_tensor_tensor(act_tok[:, t], acc[:, j % 2, t, GU_W:2 * GU_W], rstd[:, 3, t:t + 1],
                                                   silu[:, t], ALU.mult, ALU.mult).then_inc(prod_done, 1)

            ffn_dve(0, 0, True)
            with nc.vector.Fori(0, (GU_BLOCKS - 1) // 2) as it:
                for j in range(2):
                    ffn_dve(it * 2 + (1 + j), 1 - j, False)
            split[0] = V_GU + 4 * GU_BLOCKS + AHEAD
            lo_to(V_DOWN + 2 + AHEAD)
            ffn_al(GU_BLOCKS - 1)
            for n in range(2):
                lo_to(V_DOWN + 11 * n + 10 + AHEAD)
            dve.wait_ge(gpostd, 32)
            norm_sum(B_DOWN, 4, B_MIX + 2)
            for t in range(TILES):
                dve.wait_ge(root_done, 7 + t)
                link(nc.vector.reciprocal(rstd[:, 5, t:t + 1], small[:, 8 + t:9 + t]))
                link(nc.vector.scalar_tensor_tensor(yb[:, t], yb[:, t], rstd[:, 5, t:t + 1], gpost[:], ALU.mult, ALU.mult))
                nc.vector.tensor_tensor(xs[:, t], xs[:, t], yb[:, t], ALU.add).then_inc(fin_done, 1)

        @block.tensor
        def _(pe):
            def product(bank, h, l, k, t, slot, s, w, first, last):
                c = slice(P * t, P * t + P)
                nc.tensor.matmul(bank[:, 0:w], h[:, k, c], wh[:, slot, s, 0:w], start=first, stop=False)
                nc.tensor.matmul(bank[:, 0:w], h[:, k, c], wl[:, slot, s, 0:w], start=False, stop=False)
                return nc.tensor.matmul(bank[:, 0:w], l[:, k, c], wh[:, slot, s, 0:w], start=False, stop=last)

            def sub(v, slot, parity, h, l, k0, w, first, last):
                pe.wait_ge(lo_done, v + 1)
                for t in range(TILES):
                    for s in range(2):
                        ins = product(acc[:, parity, t], h, l, k0 + s, t, slot, s, w,
                                      first and s == 0, last and s == 1)
                    if t == 0 and last:
                        ins.then_inc(acc0_done, 1)
                ins.then_inc(mm_done, 1)

            def free_acc(b, static=True):
                if static and b < 2:
                    return
                for t in range(TILES):
                    pe.wait_ge(ev[t], b - 1)

            def whole_block(b, v0, subs, h, l, k0=0, w=SLICE):
                free_acc(b)
                for i in range(subs):
                    sub(v0 + i, (v0 + i) % SUBS, b % 2, h, l, k0 + 2 * i, w, i == 0, i == subs - 1)

            def transpose_bank(r, j, src):
                bank = (acc[:, j // 2, j % 2] if r == 1 else quad[j])
                for kk in range(2):
                    for t in range(TILES):
                        ins = nc.tensor.transpose(bank[:, 256 * kk + P * t:256 * kk + P * t + P],
                                                  src[:, t, P * (2 * j + kk):P * (2 * j + kk) + P], ident[:])
                ins.then_inc(tp_done, 1)

            pe.wait_ge(constd, 6 * 16)
            pe.wait_ge(cmpd, 9 * 16)
            pe.wait_ge(reld, 2 * 16)
            nc.tensor.transpose(ob[:, 0:3 * KD], grows[:], ident[0:3 * KD, 0:3 * KD])
            for kv in range(2):
                ins = nc.tensor.transpose(ob[:, 32 + CMP_LEN * kv:32 + CMP_LEN * kv + CMP_LEN],
                                          pos2[:, kv].rearrange("j r d -> j (r d)"), ident[0:CMP_LEN, 0:CMP_LEN])
            ins.then_inc(pre_pe, 1)
            nc.tensor.matmul(ptb[0:BIAS_H, :], rel[:], onehot[:], start=True, stop=True).then_inc(pre_pe, 1)
            pe.wait_ge(memd, 16)
            pe.wait_ge(pre_dve, 2)
            pe.wait_ge(grow_done, 1)
            for j in range(4):
                transpose_bank(0, j, mems)
            pe.wait_ge(xd, 16)
            for j in range(4):
                transpose_bank(1, j, xs)

            pe.wait_ge(tl_done, 8)
            whole_block(B_MEMKV, 0, 4, memh, meml)
            pe.wait_ge(bp_d, 16)
            for i in range(6):
                if i >= 2:
                    pe.wait_ge(tb_ev[i % 2], i // 2)
                dst = (ptb, ob)[i % 2]
                nc.tensor.matmul(dst[:].rearrange("p (a n) -> p a n", a=2), flip[:], bp[:, 2 * i:2 * i + 2, 0:256], start=True, stop=True).then_inc(tb_pe, 1)
            pe.wait_ge(tb_ev[1], 3)
            for t in range(TILES):
                off = 31 + P * (1 - t)
                src = bp[:, 0:NSA_H, off:off + 1]
                ins = nc.tensor.matmul(ob[:, P * t:P * t + P].rearrange("p (h c) -> p h c", h=NSA_H)[:, :, 0:NCMP], flip[:],
                                       bass.AP(src.tensor, src.offset, [src.ap[0], [BP_W, NSA_H], [CMP_STRIDE, NCMP]]),
                                       start=True, stop=True)
            ins.then_inc(tb_pe, 1)
            pe.wait_ge(tb_ev[0], 3)
            pe.wait_ge(tb_ev[1], 4)

            def qk_batch(beta, blocks_ready, sources):
                for t in range(TILES):
                    pe.wait_ge(ev[t], blocks_ready)
                if beta >= 2:
                    pe.wait_ge(qk_ev[beta % 2], beta // 2)
                for i, src in enumerate(sources):
                    for t in range(TILES):
                        ins = nc.tensor.transpose(sbank[:, beta % 2, 256 * i + P * t:256 * i + P * t + P], src(t), ident[:])
                ins.then_inc(qk_pe, 1)

            def col(c):
                return lambda t: pat[:, t, c:c + P]

            whole_block(1, 4, 4, xh, xl)
            qk_batch(0, 1, [lambda t: kvm[:, t, 0:P], lambda t: kvm[:, t, P:2 * P]])
            whole_block(2, 8, 4, xh, xl)
            qk_batch(1, 2, [col(0), col(P)])
            qk_batch(2, 2, [col(2 * P), col(3 * P)])
            whole_block(3, 12, 4, xh, xl)
            qk_batch(3, 3, [col(C_KC), col(C_VC)])
            whole_block(4, 16, 4, xh, xl)
            qk_batch(4, 4, [col(C_KS), col(C_KW)])
            pe.wait_ge(cmp_g, 1)
            for kv in range(2):
                for j in range(PAIRS):
                    ins = nc.tensor.matmul(ob[:, 2 * NCMP * kv:2 * NCMP * (kv + 1)], w1[:, kv, j, :], gcmp[:, kv, j, :],
                                           start=(j == 0), stop=(j == PAIRS - 1))
            ins.then_inc(cmp_pe, 1)
            whole_block(5, 20, 4, xh, xl, w=ATT_TAIL)
            qk_batch(5, 5, [col(C_QM), col(C_QM + P)])
            qk_batch(6, 5, [col(C_KM), col(C_KM + P)])
            pe.wait_ge(cmp_dve, 2)
            nc.tensor.matmul(ob[:, 64:64 + 2 * NCMP], w2k[:].rearrange("p r d -> p (r d)"), hidk[:], start=True, stop=True)
            for g in range(GROUPS):
                ins = nc.tensor.matmul(ob[:, 128 + HD * g:128 + HD * g + HD], hidv[:, g].rearrange("p i c -> p (i c)"), w2v[:],
                                       start=True, stop=True)
            ins.then_inc(cmp_pe, 1)

            def scores(n):
                kind, h, qb, qh, kb, _bh = jobs[n]
                half = slice(HD * qh, HD * qh + HD)
                if n == 0:
                    pe.wait_ge(qk_ev[1], 3)
                    pe.wait_ge(qk_ev[0], 4)
                elif n == 1:
                    pe.wait_ge(qk_ev[1], 4)
                else:
                    pe.wait_ge(e_done, n - 1)
                for t in range(TILES):
                    c0, c1 = prob_cols(kind, t)
                    ins = nc.tensor.matmul(sbank[:, n % 2, c0:c1], qkt[half, qb, P * t:P * t + P], qkt[half, kb, 0:c1 - c0],
                                           start=True, stop=True)
                ins.then_inc(s_done, 1)

            def turn(n):
                kind = jobs[n][0]
                pe.wait_ge(p_done, n + 1)
                if n:
                    pe.wait_ge(te_done, t_count(n) - 1)
                else:
                    pe.wait_ge(cmp_dve, 4)
                pieces = [(0, 0), (P, P), (2 * P, 2 * P)] if kind != "mem" else [(0, 0), (2 * P, P), (P, 2 * P), (3 * P, 3 * P)]
                for src, dst in pieces:
                    ins = nc.tensor.transpose(ptb[:, dst:dst + P], sx[:, n % 2, src:src + P], ident[:])
                ins.then_inc(t_done, 1)

            def values(n):
                kind, h = jobs[n][0:2]
                starts = kind != "win"
                ends = kind != "sel"
                if n == 0:
                    pe.wait_ge(cmp_dve, 4)
                elif ends_pair(n - 1):
                    pe.wait_ge(ol_done, pair_of(n))
                dst = ob[HD * (h % 2):HD * (h % 2) + HD]
                if kind == "sel":
                    g = h // HPG
                    nc.tensor.matmul(dst[:, 0:256], vcz[:, g, h % HPG, :], pct[:, g, :], start=True, stop=False)
                    starts = False
                if kind == "moba":
                    v = [pat[:, t, C_VM + HD * h:C_VM + HD * h + HD] for t in range(2)]
                elif kind == "mem":
                    v = [kvm[:, t, 256 + HD * h:256 + HD * h + HD] for t in range(2)]
                else:
                    c = (C_VS if kind == "sel" else C_VW) + HD * (h // HPG)
                    v = [pat[:, t, c:c + HD] for t in range(2)]
                pe.wait_ge(te_done, t_count(n))
                nc.tensor.matmul(dst[:, 0:256], v[0], pts[:, n % 2, 0:256], start=starts, stop=False)
                c0 = 0 if kind == "mem" else P
                nc.tensor.matmul(dst[:, c0:256], v[1], pts[:, n % 2, 256:512 - c0], start=False, stop=ends).then_inc(pv_done, 1)

            for n in range(JOBS + 2):
                if n < JOBS:
                    scores(n)
                if n == 0:
                    pe.wait_ge(cmp_dve, 3)
                    for h in range(NSA_H):
                        for t in range(TILES):
                            g = h // HPG
                            c = 16 * (HPG * t + h % HPG)
                            ins = nc.tensor.matmul((ob, ptb)[g][:, c:c + NCMP], qkt[HD * g:HD * g + HD, QK_Q + h % HPG, P * t:P * t + P],
                                                   kct[HD * g:HD * g + HD, :], start=True, stop=True)
                    ins.then_inc(cmp_pe, 1)
                if n < JOBS:
                    if n % 4 == 0:
                        free_acc(B_GATE + n // 4)
                    sub(V_GATE + n, n % SUBS, (n // 4) % 2, xh, xl, 2 * (n % 4), SLICE, n % 4 == 0, n % 4 == 3)
                elif n == JOBS:
                    whole_block(B_MOBA, V_MOBA, 1, oh, ol, 0)
                    whole_block(B_MOBA + 1, V_MOBA + 1, 1, oh, ol, 0)
                if n == 0:
                    qk_batch(7, 6, [col(C_QX), col(C_QX + P)])
                if n == 2:
                    pe.wait_ge(cmp_dve, 5)
                    pe.wait_ge(te_done, 1)
                    for g in range(GROUPS):
                        for t in range(TILES):
                            ins = nc.tensor.transpose(ptb[:, 256 * g + P * t:256 * g + P * t + P],
                                                      pcz[:, t, g].rearrange("p i c -> p (i c)"), ident[:])
                    ins.then_inc(t_done, 1)
                if 1 <= n <= JOBS:
                    turn(n - 1)
                if n >= 2:
                    values(n - 2)
            for n in range(2):
                whole_block(B_MEM + n, V_MEM + n, 1, oh, ol, 2)
            pe.wait_ge(ol_done, 8)
            for n in range(2):
                whole_block(B_NSA + n, V_NSA + 2 * n, 2, oh, ol, 4)
            for j in range(4):
                pe.wait_ge(y_done, 2 + 2 * (j // 2))
                transpose_bank(2, j, yb)
            pe.wait_ge(tl_done, 12)
            for n in range(2):
                whole_block(B_MIX + n, V_MIX + 4 * n, 4, xh, xl)
            pe.wait_ge(x1_done, 2)
            for j in range(4):
                transpose_bank(3, j, xs)
            pe.wait_ge(tl_done, 16)

            for t in range(TILES):
                pe.wait_ge(ev[t], B_GU)
            for s in range(4):
                sub(V_GU + s, s, 0, xh, xl, 2 * s, SLICE, s == 0, s == 3)

            def ffn_body(i, j, first):
                if not first:
                    pe.wait_ge(prod_done, i * 2 - 2)
                for s in range(4):
                    sub(i * 4 + (V_GU + s), s, j, xh, xl, 2 * s, SLICE, s == 0, s == 3)
                    if s == 1:
                        ffn_turn_at(i)

            def ffn_turn_at(i):
                pe.wait_ge(prod_done, i * 2)
                pe.wait_ge(al_done, i - 1) if not isinstance(i, int) or i > 1 else None
                for kk in range(2):
                    for t in range(TILES):
                        ins = nc.tensor.transpose(ptb[:, 256 * kk + P * t:256 * kk + P * t + P],
                                                  act_tok[:, t, P * kk:P * kk + P], ident[:])
                ins.then_inc(at_done, 1)

            ffn_body(1, 1, True)
            ffn_body(2, 0, False)
            with nc.tensor.Fori(0, (GU_BLOCKS - 3) // 2) as it:
                for j in range(2):
                    ffn_body(it * 2 + (3 + j), 1 - j, False)
            for n in range(2):
                pe.wait_ge(prod_done, 2 * (GU_BLOCKS - 1 + n))
                for i in range(11):
                    v = V_DOWN + 11 * n + i
                    sub(v, v % SUBS, (B_DOWN + n) % 2, ah, al, 2 * i, SLICE, i == 0, i == 10)
                    if n == 0 and i == 1:
                        ffn_turn_at(GU_BLOCKS)
                    if n == 0 and i == 8:
                        pe.wait_ge(al_done, GU_BLOCKS)


def bucket_onehot():
    import numpy as np
    dist = 255 - np.arange(G_W)
    exact = BUCKETS // 2
    safe = np.maximum(dist, 1).astype(np.float32)
    logd = np.log(safe / np.float32(exact)).astype(np.float32) / np.float32(np.log(MAX_DIST / exact))
    large = np.minimum(exact + (logd * np.float32(BUCKETS - exact)).astype(np.int32), BUCKETS - 1)
    bucket = np.where(dist < exact, np.maximum(dist, 0), large)
    hot = (bucket[None, :] == np.arange(BUCKETS)[:, None]) & (dist >= 0)[None, :]
    return hot.astype(np.float32)


NAMES = ["x", "mem", "rel_bias", "pre_mix_g", "mem_norm_g", "post_mix_g", "w_in", "cmp_pos_k", "cmp_w1_k", "cmp_w2_k",
         "cmp_pos_v", "cmp_w1_v", "cmp_w2_v", "w_mem_kv", "w_nsa_o", "w_moba_o", "w_mem_o", "w_mix_out",
         "pre_ffn_g", "post_ffn_g", "w_ffn_gate", "w_ffn_up", "w_ffn_down"]


def kernel(**inputs):
    import numpy as np
    import concourse.bacc as bacc
    from concourse.bass_utils import run_bass_kernel_spmd

    nc = bacc.Bacc("TRN2", target_bir_lowering=False, num_devices=1)
    arrays = {f"in_{n}": np.ascontiguousarray(inputs[n]) for n in NAMES}
    arrays["in_bucket_onehot"] = bucket_onehot()
    arrays["in_const_ident"] = np.eye(P, dtype=np.float32)
    arrays["in_const_flip"] = np.ascontiguousarray(np.eye(P, dtype=np.float32)[::-1])
    rows = np.arange(SEQ).reshape(TILES, P).T
    arrays["in_const_any"] = np.ascontiguousarray((rows >= CMP_LEN - 1).astype(np.float32))
    a = {n[3:]: nc.dram_tensor(n, v.shape, F32, kind="ExternalInput").ap() for n, v in arrays.items()}
    out = nc.dram_tensor("out_0", (1, SEQ, D), F32, kind="ExternalOutput").ap()
    g_scratch = nc.dram_tensor("g_scratch", (BIAS_H, G_W), F32, kind="Internal").ap()
    build_layer(nc, a, out, g_scratch)
    r = run_bass_kernel_spmd(nc, [arrays], core_ids=[0])
    return r.results[0]["out_0"]
```

```python
from contextlib import ExitStack

import concourse.bass as bass
from concourse import mybir

F32 = mybir.dt.float32
F32R = mybir.dt.float32r
ALU = mybir.AluOpType
ACT = mybir.ActivationFunctionType
AX = mybir.AxisListType.X

P = 128
SEQ = 256
TILES = SEQ // P
D = 1024
KD = D // P
HD = 64
SCALE = HD ** -0.5
NSA_H, GROUPS, HPG = 8, 2, 4
MOBA_H, MEM_H = 4, 4
BIAS_H = NSA_H + MOBA_H
MEM_LEN = 256
CMP_LEN, CMP_STRIDE, CMP_HID = 32, 16, 128
NCMP = (SEQ - CMP_LEN) // CMP_STRIDE + 1
PAIRS = CMP_LEN // 2
BUCKETS, MAX_DIST = 32, 128
D_FF = 2816
KF = D_FF // P
EPS = 1e-6
MASKED = -1e30

C_Q, C_KC, C_VC, C_KS, C_VS, C_KW, C_VW, C_GN = 0, 512, 640, 768, 896, 1024, 1152, 1280
C_QM, C_KM, C_VM, C_QX, C_GATES = 1304, 1560, 1816, 2072, 2328
ATT_W = C_GATES

SLICE = 512
ATT_TAIL = ATT_W - 4 * SLICE
RAW, SUBS = 4, 4
AHEAD = SUBS - 1

B_MEMKV, B_ATT, B_GATE, B_MOBA, B_MEM, B_NSA, B_MIX, B_GU, B_DOWN = 0, 1, 6, 12, 14, 16, 18, 20, 31
GU_BLOCKS, GU_W = 11, 256
U_GU, U_DOWN = 32, 54
UNITS = U_DOWN + 2 * KF // 4
V_GATE, V_MOBA, V_MEM, V_NSA, V_MIX, V_GU, V_DOWN = 24, 48, 50, 52, 56, 2 * U_GU, 2 * U_DOWN

JOBS = 24
BLK = KD * 256

QK_MK, QK_Q, QK_KC, QK_VC, QK_KS, QK_KW, QK_QM, QK_KM, QK_QX = 0, 2, 6, 7, 8, 9, 10, 12, 14

G_W, BP_W = 512, 384


def job_plan():
    jobs = []
    for m in range(MOBA_H):
        jobs.append(("moba", m, QK_QM + m // 2, m % 2, QK_KM + m // 2, NSA_H + m))
    for m in range(MEM_H):
        jobs.append(("mem", m, QK_QX + m // 2, m % 2, QK_MK + m // 2, None))
    for h in range(NSA_H):
        for kind, kb in (("sel", QK_KS), ("win", QK_KW)):
            jobs.append((kind, h, QK_Q + h % HPG, h // HPG, kb, h))
    return jobs


def pair_of(job):
    return job // 2 if job < 8 else 4 + (job - 8) // 4


def ends_pair(job):
    return job % 2 == 1 if job < 8 else (job - 8) % 4 == 3


def t_count(job):
    return 1 if job == 0 else job + 2


def build_layer(nc, a, out, g_scratch):
    jobs = job_plan()
    xf = a["x"][0].rearrange("(t p) d -> p t d", p=P)
    memf = a["mem"][0].rearrange("(t p) d -> p t d", p=P)
    outf = out[0].rearrange("(t p) d -> p t d", p=P)

    def rows(name):
        return a[name][0].rearrange("(k p) n -> p k n", p=P)

    w_in, w_memkv = rows("w_in"), rows("w_mem_kv")
    w_nsa, w_moba, w_mem, w_mix = rows("w_nsa_o"), rows("w_moba_o"), rows("w_mem_o"), rows("w_mix_out")
    w_gate, w_up, w_down = rows("w_ffn_gate"), rows("w_ffn_up"), rows("w_ffn_down")

    with ExitStack() as ctx:
        def sb(name, shape, dt=F32, stack=ctx):
            return stack.enter_context(nc.sbuf_tensor(name, shape, dt))

        def psum(name, shape):
            return ctx.enter_context(nc.psum_tensor(name, shape, F32))

        def sem(name):
            return ctx.enter_context(nc.semaphore(name))

        raw = sb("raw", [P, RAW, 4, SLICE])
        wh = sb("wh", [P, SUBS, 2, SLICE], F32R)
        wl = sb("wl", [P, SUBS, 2, SLICE], F32R)
        xh = sb("xh", [P, KD, SEQ], F32R)
        xl = sb("xl", [P, KD, SEQ], F32R)
        xs = sb("xs", [P, TILES, D])
        const0 = sb("const0", [P, P + TILES])
        ident, row_any = const0[:, 0:P], const0[:, P:P + TILES]
        grows = sb("grows", [3 * KD, P])
        gcol = sb("gcol", [P, 3 * KD])
        gpost = sb("gpost", [P, D])
        eps = sb("eps", [P, 1])
        ssq = sb("ssq", [P, 8, TILES])
        part = sb("part", [P, 2, 2, TILES])
        rstd = sb("rstd", [P, 8, TILES])
        small = sb("small", [P, 64])
        with ExitStack() as s:
            memh = sb("memh", [P, KD, SEQ], F32R, s)
            meml = sb("meml", [P, KD, SEQ], F32R, s)
            mems = sb("mems", [P, TILES, D], F32, s)
        gates = sb("gates", [P, TILES, 3 * D])
        with ExitStack() as s:
            w1 = sb("w1", [P, 2, PAIRS, CMP_HID], F32, s)
        oh = sb("oh", [P, 8, SEQ], F32R)
        ol = sb("ol", [P, 8, SEQ], F32R)
        late = ExitStack()
        with ExitStack() as s:
            bp = sb("bp", [P, BIAS_H, BP_W], F32, s)
        with ExitStack() as s:
            pat = sb("pat", [P, TILES, ATT_W], F32, s)
            kvm = sb("kvm", [P, TILES, 2 * 256], F32, s)
            qkt = sb("qkt", [P, 16, SEQ], F32, s)
            tb = sb("tb", [P, BIAS_H, 256], F32, s)
            tbc = sb("tbc", [P, TILES, NSA_H, 16], F32, s)
            with ExitStack() as early:
                rel = sb("rel", [BUCKETS, BIAS_H], F32, early)
                const1 = sb("const1", [P, P + G_W], F32, early)
                grow = sb("grow", [BIAS_H, G_W], F32, early)
                pos2 = sb("pos2", [CMP_LEN, 2, 2, HD], F32, early)
            flip, onehot = const1[:, 0:P], const1[0:BUCKETS, P:P + G_W]
            sx = sb("sx", [P, 2, 512], F32, s)
            pts = sb("pts", [P, 2, 512], F32, s)
            post = sb("post", [P, 2, CMP_LEN], F32, s)
            with ExitStack() as early:
                gcmp = sb("gcmp", [P, 2, PAIRS, GROUPS * NCMP], F32, early)
            pcz = sb("pcz", [P, TILES, GROUPS, HPG, 32], F32, s)
            pct = sb("pct", [P, GROUPS, SEQ], F32, s)
            w2k = sb("w2k", [CMP_HID, 2, HD], F32, s)
            w2v = sb("w2v", [CMP_HID, HD], F32, s)
            hx = sb("hx", [P, 3, 4 * NCMP], F32, s)
            hidk = sb("hidk", [P, GROUPS * NCMP], F32, s)
            hidv = sb("hidv", [P, GROUPS, HPG, 32], F32, s)
            kct = sb("kct", [P, NCMP], F32, s)
            vcz = sb("vcz", [P, GROUPS, HPG, HD], F32, s)
            xc = sb("xc", [P, TILES, NSA_H, 16], F32, s)
            cst = sb("cst", [P, 4, TILES * NSA_H], F32, s)
            gsig = sb("gsig", [P, TILES, 3 * NSA_H], F32, s)
            jst = sb("jst", [P, 5, JOBS, TILES], F32, s)
        with late:
            ah = sb("ah", [P, KF, SEQ], F32R, late)
            al = sb("al", [P, KF, SEQ], F32R, late)
            yb = sb("yb", [P, TILES, D], F32, late)
            tmp = sb("tmp", [P, TILES, SLICE], F32, late)
            silu = sb("silu", [P, TILES, GU_W], F32, late)
            act_tok = sb("act_tok", [P, TILES, GU_W], F32, late)

        acc = psum("acc", [P, 2, TILES, 512])
        sbank = psum("sbank", [P, 2, 512])
        ptb = psum("ptb", [P, 512])
        ob = psum("ob", [P, 512])
        quad = [sbank[:, 0], sbank[:, 1], ptb[:], ob[:]]

        loaded = [sem(f"loaded{i}") for i in range(RAW)]
        hi_done = sem("hi_done")
        lo_done = sem("lo_done")
        mm_done = sem("mm_done")
        acc0_done = sem("acc0_done")
        ev = [sem("ev0"), sem("ev1")]
        xd, memd, constd = sem("xd"), [sem("memd0"), sem("memd1")], sem("constd")
        gaind = [sem("gaind0"), sem("gaind1")]
        sub0d, posd, zeroed = sem("sub0d"), sem("posd"), sem("zeroed")
        reld, cmpd, gpostd, g_stored, bp_d, out_d = (sem("reld"), sem("cmpd"), sem("gpostd"), sem("g_stored"),
                                                     sem("bp_d"), sem("out_d"))
        dve_c, act_c = sem("dve_c"), sem("act_c")
        ssq_done = sem("ssq_done")
        root_done = sem("root_done")
        rstd_done = sem("rstd_done")
        tp_done, th_done, tl_done = sem("tp_done"), sem("th_done"), sem("tl_done")
        pre_pe, pre_dve, pre_act = sem("pre_pe"), sem("pre_dve"), sem("pre_act")
        grow_done = sem("grow_done")
        tb_pe, tb_ev = sem("tb_pe"), [sem("tb_ev0"), sem("tb_ev1")]
        qk_pe, qk_ev = sem("qk_pe"), [sem("qk_ev0"), sem("qk_ev1")]
        cmp_g, cmp_pe, cmp_dve, cmp_act = sem("cmp_g"), sem("cmp_pe"), sem("cmp_dve"), sem("cmp_act")
        s_done, x_done, e_done, r_done, p_done = (sem("s_done"), sem("x_done"), sem("e_done"), sem("r_done"),
                                                  sem("p_done"))
        t_done, te_done, pv_done = sem("t_done"), sem("te_done"), sem("pv_done")
        oh_done, ol_done = sem("oh_done"), sem("ol_done")
        silu_done, prod_done, at_done, ah_done, al_done = (sem("silu_done"), sem("prod_done"), sem("at_done"),
                                                           sem("ah_done"), sem("al_done"))
        y_done, x1_done, fin_done = sem("y_done"), sem("x1_done"), sem("fin_done")
        sq_done, sum_done = sem("sq_done"), sem("sum_done")

        junk = qkt[:].rearrange("p (j a) n -> p j (a n)", j=4)

        block = ctx.enter_context(nc.Block())

        def width(v):
            return ATT_TAIL if v // 4 == B_ATT + 4 else SLICE

        def prob_cols(kind, t):
            if kind == "mem":
                return 256 * t, 256 * t + 256
            return (0, 128) if t == 0 else (128, 384)

        def pair_queries(dst, src):
            return (dst.rearrange("p (i g d) -> p g i d", g=GROUPS, i=HPG),
                    src.rearrange("p (g i d) -> p g i d", g=GROUPS, i=HPG))

        @block.sync
        def _(sp):
            def free_slot(u):
                if isinstance(u, int) and u < RAW:
                    return
                sp.wait_ge(lo_done, 2 * (u - RAW) + 2)

            def unit(u, slot, parts):
                free_slot(u)
                for dst, src in parts:
                    sp.dma_start(dst, src).then_inc(loaded[slot], 32 // len(parts))

            def plain(u, src, k0, c0, w=SLICE):
                unit(u, u % RAW, [(raw[:, u % RAW, :, 0:w], src[:, k0:k0 + 4, c0:c0 + w])])

            for c in range(2):
                sp.dma_start(mems[:, :, SLICE * c:SLICE * c + SLICE], memf[:, :, SLICE * c:SLICE * c + SLICE]).then_inc(memd[c], 16)
            sp.dma_start(raw[:, 0, 0:2, :], w_memkv[:, 0:2, 0:SLICE]).then_inc(sub0d, 16)
            sp.dma_start(raw[:, 0, 2:4, :], w_memkv[:, 2:4, 0:SLICE]).then_inc(loaded[0], 32)
            plain(1, w_memkv, 4, 0)
            sp.dma_start(xs[:], xf).then_inc(xd, 16)
            plain(2, w_in, 0, 0)
            plain(3, w_in, 4, 0)
            sp.wait_ge(grow_done, 2)
            sp.dma_start(g_scratch, grow[:]).then_inc(g_stored, 16)
            sp.wait_ge(g_stored, 16)
            sp.dma_start(bp[:], bass.AP(g_scratch.tensor, 0, [[1, P], [G_W, BIAS_H], [1, BP_W]])).then_inc(bp_d, 16)
            u = 4
            for b in range(1, 5):
                for half in range(2):
                    plain(u, w_in, 4 * half, SLICE * b, SLICE if b < 4 else ATT_TAIL)
                    u += 1
            for b in range(6):
                for half in range(2):
                    plain(u, w_in, 4 * half, C_GATES + SLICE * b)
                    u += 1
            for w in (w_moba, w_mem):
                unit(u, u % RAW, [(raw[:, u % RAW, 2 * n:2 * n + 2, :], w[:, :, SLICE * n:SLICE * n + SLICE])
                                  for n in range(2)])
                u += 1
            for n in range(2):
                plain(u, w_nsa, 0, SLICE * n)
                u += 1
            for n in range(2):
                for half in range(2):
                    plain(u, w_mix, 4 * half, SLICE * n)
                    u += 1

            def gate_up(i, j):
                for half in range(2):
                    u, slot = U_GU + 2 * i + half, (2 * j + half) % RAW
                    unit(u, slot, [(raw[:, slot, :, GU_W * c:GU_W * c + GU_W],
                                    w[:, 4 * half:4 * half + 4, bass.ds(i * GU_W, GU_W)])
                                   for c, w in enumerate((w_gate, w_up))])

            gate_up(0, 0)
            with nc.sync.Fori(0, (GU_BLOCKS - 1) // 2) as it:
                for j in range(2):
                    gate_up(it * 2 + (1 + j), 1 - j)
            for j in range(2 * KF // 4):
                u = U_DOWN + j
                cut = []
                for c in (0, 2):
                    n, k = divmod(4 * j + c, KF)
                    cut.append((raw[:, u % RAW, c:c + 2, :], w_down[:, k:k + 2, SLICE * n:SLICE * n + SLICE]))
                unit(u, u % RAW, cut)
            for i in range(4):
                t, c = i % 2, SLICE * (i // 2)
                sp.wait_ge(fin_done, i + 1)
                sp.dma_start(outf[:, t, c:c + SLICE], xs[:, t, c:c + SLICE]).then_inc(out_d, 16)
            sp.wait_ge(out_d, 16 * 4)

        @block.gpsimd
        def _(pool):
            nc.gpsimd.memset(hidv[:], 0.0).then_inc(zeroed, 1)
            nc.gpsimd.memset(vcz[:], 0.0).then_inc(zeroed, 1)
            pool.wait_ge(bp_d, 16)
            for kv, name in enumerate(("cmp_w1_k", "cmp_w1_v")):
                nc.gpsimd.dma_start(w1[:, kv], a[name][0].rearrange("(j p) n -> p j n", p=P)).then_inc(cmpd, 16)
            for rep in range(2):
                nc.gpsimd.dma_start(w2k[:, rep, :], a["cmp_w2_k"][0]).then_inc(cmpd, 16)
            nc.gpsimd.dma_start(w2v[:], a["cmp_w2_v"][0]).then_inc(cmpd, 16)
            nc.gpsimd.dma_start(gpost[:], bass.AP(a["post_mix_g"].tensor, 0, [[0, P], [1, D]])).then_inc(gpostd, 16)
            pool.wait_ge(cmp_pe, 1)
            nc.gpsimd.memset(pcz[:], 0.0).then_inc(zeroed, 1)
            for n, (kind, *_r) in enumerate(jobs):
                pool.wait_ge(r_done, n + 1)
                for t in range(TILES):
                    lo, hi = prob_cols(kind, t)
                    ins = nc.gpsimd.tensor_scalar(sx[:, n % 2, lo:hi], sx[:, n % 2, lo:hi], jst[:, 4, n, t:t + 1], 1.0,
                                                  ALU.mult, ALU.mult)
                ins.then_inc(p_done, 1)
            pool.wait_ge(x1_done, 4)
            nc.gpsimd.dma_start(gpost[:], bass.AP(a["post_ffn_g"].tensor, 0, [[0, P], [1, D]])).then_inc(gpostd, 16)

        @block.scalar
        def _(act):
            nc.scalar.dma_start(const0[:], a["const0"]).then_inc(constd, 16)
            for i, name in enumerate(("mem_norm_g", "pre_mix_g", "pre_ffn_g")):
                nc.scalar.dma_start(grows[KD * i:KD * i + KD, :], a[name][0].rearrange("(k p) -> k p", p=P)).then_inc(gaind[min(i, 1)], 16)
                if i == 0:
                    nc.scalar.dma_start(rel[:], a["rel_bias"]).then_inc(reld, 16)
                    nc.scalar.dma_start(const1[:], a["const1"]).then_inc(reld, 16)
            nc.scalar.preload_act_table(ACT.Sqrt)
            for kv, name in enumerate(("cmp_pos_k", "cmp_pos_v")):
                for rep in range(2):
                    nc.scalar.dma_start(pos2[:, kv, rep, :], a[name][0]).then_inc(posd, 16)

            split = [0]

            def hi(v, slot, half, w, first_load):
                if isinstance(v, int) and v == 0:
                    act.wait_ge(sub0d, 16)
                else:
                    act.wait_ge(loaded[slot], first_load)
                if not (isinstance(v, int) and v < SUBS):
                    act.wait_ge(mm_done, v - SUBS + 1)
                k = (2 * slot + half) % SUBS
                nc.scalar.activation(wh[:, k, :, 0:w], raw[:, slot, 2 * half:2 * half + 2, 0:w], ACT.Copy).then_inc(hi_done, 1)

            def hi_to(v_end):
                while split[0] <= min(v_end, 2 * UNITS - 1):
                    v = split[0]
                    u = v // 2
                    hi(v, u % RAW, v % 2, width(v), 32 * (u // RAW + 1))
                    split[0] += 1

            chain = [0]

            def link(ins):
                chain[0] += 1
                ins.then_inc(act_c, 1)
                act.wait_ge(act_c, chain[0])

            def wait_block(b, t, v_last):
                if t == 0:
                    act.wait_ge(acc0_done, b + 1)
                else:
                    act.wait_ge(mm_done, v_last + 1)

            def round_hi(r, j):
                act.wait_ge(tp_done, 4 * r + j + 1)
                bank = quad[j]
                dst = memh if r == 0 else xh
                for kk in range(2):
                    k = 2 * j + kk
                    g = {0: k, 1: KD + k, 3: 2 * KD + k}.get(r)
                    scale = 0.5 if r == 2 else gcol[:, g:g + 1]
                    ins = nc.scalar.activation(dst[:, k, :], bank[:, 256 * kk:256 * kk + 256], ACT.Copy, scale=scale)
                ins.then_inc(th_done, 1)

            act.wait_ge(pre_dve, 2)
            for j in range(4):
                round_hi(0, j)
                hi_to(j)

            def roots(i):
                nc.scalar.activation(small[:, 2 * i:2 * i + 2], ssq[:, i, :], ACT.Sqrt, bias=eps[:], scale=1.0 / D).then_inc(root_done, 1)

            act.wait_ge(pre_dve, 3)
            for j in range(4):
                round_hi(1, j)
            hi_to(4)
            act.wait_ge(ssq_done, 2)
            roots(0)
            hi_to(5)
            for t in range(TILES):
                nc.scalar.activation(junk[:, 2 + t], xs[:, t], ACT.Square, accum_out=ssq[:, 1, t:t + 1]).then_inc(ssq_done, 1)
            act.wait_ge(ssq_done, 4)
            roots(1)
            nc.scalar.preload_act_table(ACT.Tanh)

            def evac_cols(b):
                v_last = 4 * b + 3
                hi_to(v_last + AHEAD)
                act.wait_ge(rstd_done, 1 if b == 0 else 2)
                wait_block(b, 0, v_last)
                if b == 0:
                    dst, i, w = kvm[:, 0, :], 0, SLICE
                else:
                    w = ATT_TAIL if b == 5 else SLICE
                    dst, i = pat[:, 0, SLICE * (b - 1):SLICE * (b - 1) + w], 1
                src = acc[:, b % 2, 0, 0:w]
                if b == B_ATT:
                    dst, src = pair_queries(dst, src)
                nc.scalar.activation(dst, src, ACT.Copy, scale=rstd[:, i, 0:1]).then_inc(ev[0], 1)

            def evac_qk(beta):
                act.wait_ge(qk_pe, beta + 1)
                nc.scalar.activation(qkt[:, 2 * beta:2 * beta + 2, :], sbank[:, beta % 2], ACT.Copy).then_inc(qk_ev[0], 1)

            evac_cols(0)
            hi_to(7)
            for i in (0, 2, 4):
                act.wait_ge(tb_pe, i + 1)
                nc.scalar.activation(tb[:, 2 * i:2 * i + 2, :], ptb[:], ACT.Copy).then_inc(tb_ev[0], 1)
                if i:
                    hi_to(7 + i // 2)
            act.wait_ge(tb_pe, 7)
            evac_cols(1)
            hi_to(12)
            evac_qk(0)
            evac_cols(2)
            evac_qk(2)
            evac_cols(3)
            evac_qk(4)
            hi_to(21)
            act.wait_ge(cmp_dve, 1)
            nc.scalar.activation(hx[:, 2, :], hx[:, 1, :], ACT.Tanh, scale=0.7978845608028654).then_inc(cmp_act, 1)
            evac_cols(4)
            act.wait_ge(ev[0], B_ATT + 3)
            act.wait_ge(ev[1], B_ATT + 3)
            nc.scalar.activation(gsig[:], pat[:, :, C_GN:C_GN + 3 * NSA_H], ACT.Tanh, scale=0.5).then_inc(cmp_act, 1)
            hi_to(24)
            evac_qk(6)
            evac_cols(5)
            act.wait_ge(cmp_dve, 4)
            nc.scalar.activation(xc[:, :, :, 0:NCMP], xc[:, :, :, 0:NCMP], ACT.Exp, scale=SCALE).then_inc(cmp_act, 1)

            def evac_gate(b):
                for t in range(TILES):
                    wait_block(b, t, 4 * b + 3)
                    c = SLICE * (b - B_GATE)
                    nc.scalar.activation(gates[:, t, c:c + SLICE], acc[:, b % 2, t], ACT.Tanh,
                                         scale=rstd[:, 4, t:t + 1]).then_inc(ev[t], 1)

            def evac_pt(n):
                act.wait_ge(t_done, t_count(n))
                if n >= 2:
                    act.wait_ge(pv_done, n - 1)
                w = 512 if jobs[n][0] == "mem" else 384
                nc.scalar.activation(pts[:, n % 2, 0:w], ptb[:, 0:w], ACT.Copy).then_inc(te_done, 1)

            def evac_o(n):
                if ends_pair(n):
                    act.wait_ge(pv_done, n + 1)
                    nc.scalar.activation(oh[:, pair_of(n), :], ob[:, 0:256], ACT.Copy).then_inc(oh_done, 1)

            for n in range(JOBS + 2):
                hi_to(V_GATE + n + AHEAD)
                if n < JOBS:
                    kind = jobs[n][0]
                    act.wait_ge(x_done, n + 1)
                    src = sbank if kind == "mem" else sx
                    if n >= 2:
                        act.wait_ge(t_done, t_count(n - 2))
                    for t in range(TILES):
                        lo, hic = prob_cols(kind, t)
                        ins = nc.scalar.activation(sx[:, n % 2, lo:hic], src[:, n % 2, lo:hic], ACT.Exp,
                                                   bias=jst[:, 1, n, t:t + 1], scale=SCALE,
                                                   accum_out=jst[:, 2, n, t:t + 1])
                    ins.then_inc(e_done, 1)
                    if n % 4 == 3:
                        evac_gate(B_GATE + n // 4)
                if n == 2:
                    act.wait_ge(t_done, 2)
                    nc.scalar.activation(pct[:], ptb[:], ACT.Copy).then_inc(te_done, 1)
                if 1 <= n <= JOBS:
                    evac_pt(n - 1)
                if n >= 2:
                    evac_o(n - 2)

            hi_to(V_NSA + 2 + AHEAD)
            for j in range(2):
                round_hi(2, j)
            hi_to(V_MIX + AHEAD)
            for j in range(2, 4):
                round_hi(2, j)
            nc.scalar.preload_act_table(ACT.Sqrt)

            def squares(i, n, b, v_last):
                for t in range(TILES):
                    wait_block(b, t, v_last)
                    nc.scalar.activation(tmp[:, t], acc[:, b % 2, t], ACT.Square, accum_out=part[:, i, n, t:t + 1]).then_inc(sq_done, 1)

            for n in range(2):
                v_last = V_MIX + 4 * n + 3
                hi_to(v_last + AHEAD)
                if n:
                    act.wait_ge(sq_done, 2)
                squares(0, n, B_MIX + n, v_last)
            act.wait_ge(sum_done, 1)
            roots(2)
            for j in range(4):
                round_hi(3, j)
            act.wait_ge(x1_done, 4)
            for t in range(TILES):
                nc.scalar.activation(yb[:, t], xs[:, t], ACT.Square, accum_out=ssq[:, 3, t:t + 1]).then_inc(ssq_done, 1)
            act.wait_ge(ssq_done, 6)
            roots(3)

            nc.scalar.preload_act_table(ACT.Silu)

            def ffn_hi(i, j, s):
                v = V_GU + AHEAD + s + 4 * i
                vj = AHEAD + s + 4 * j
                hi(v, (vj // 2) % RAW, vj % 2, SLICE, ((V_GU + vj) // 2 // RAW + 1) * 32 + (i - j) * 16)

            def ffn_ah(i):
                act.wait_ge(at_done, i + 1)
                nc.scalar.activation(ah[:, bass.ds(i * 2, 2), :], ptb[:], ACT.Copy).then_inc(ah_done, 1)

            def ffn_act(i, j, first):
                for s in range(4):
                    ffn_hi(i, j, s)
                    if s == 2 and not first:
                        ffn_ah(i - 1)
                for t in range(TILES):
                    if t == 0:
                        act.wait_ge(acc0_done, i + (B_GU + 1))
                    else:
                        act.wait_ge(mm_done, i * 4 + (V_GU + 4))
                    if not first:
                        act.wait_ge(prod_done, i * 2 + (t - 1))
                    nc.scalar.activation(silu[:, t], acc[:, j % 2, t, 0:GU_W], ACT.Silu, scale=rstd[:, 3, t:t + 1]).then_inc(silu_done, 1)

            act.wait_ge(rstd_done, 4)
            ffn_act(0, 0, True)
            with nc.scalar.Fori(0, (GU_BLOCKS - 1) // 2) as it:
                for j in range(2):
                    ffn_act(it * 2 + (1 + j), 1 - j, False)
            split[0] = V_GU + 4 * GU_BLOCKS + AHEAD
            hi_to(V_DOWN + 2 + AHEAD)
            ffn_ah(GU_BLOCKS - 1)
            nc.scalar.preload_act_table(ACT.Sqrt)
            for n in range(2):
                v_last = V_DOWN + 11 * n + 10
                hi_to(v_last + AHEAD)
                if n:
                    act.wait_ge(sq_done, 6)
                squares(1, n, B_DOWN + n, v_last)
            act.wait_ge(sum_done, 2)
            roots(4)

        @block.vector
        def _(dve):
            split = [0]

            def lo(v, slot, half, w):
                dve.wait_ge(hi_done, v + 1)
                k = (2 * slot + half) % SUBS
                nc.vector.tensor_tensor(wl[:, k, :, 0:w], raw[:, slot, 2 * half:2 * half + 2, 0:w],
                                        wh[:, k, :, 0:w].bitcast(F32), ALU.subtract).then_inc(lo_done, 1)

            def lo_to(v_end):
                while split[0] <= min(v_end, 2 * UNITS - 1):
                    v = split[0]
                    lo(v, v // 2 % RAW, v % 2, width(v))
                    split[0] += 1

            chain = [0]

            def link(ins):
                chain[0] += 1
                ins.then_inc(dve_c, 1)
                dve.wait_ge(dve_c, chain[0])

            def wait_block(b, t, v_last):
                if t == 0:
                    dve.wait_ge(acc0_done, b + 1)
                else:
                    dve.wait_ge(mm_done, v_last + 1)

            def round_lo(r, j):
                dve.wait_ge(th_done, 4 * r + j + 1)
                bank = quad[j]
                h, l = (memh, meml) if r == 0 else (xh, xl)
                for kk in range(2):
                    k = 2 * j + kk
                    g = {0: k, 1: KD + k, 3: 2 * KD + k}.get(r)
                    scale = 0.5 if r == 2 else gcol[:, g:g + 1]
                    ins = nc.vector.scalar_tensor_tensor(l[:, k, :], bank[:, 256 * kk:256 * kk + 256], scale,
                                                         h[:, k, :].bitcast(F32), ALU.mult, ALU.subtract)
                ins.then_inc(tl_done, 1)

            nc.vector.memset(eps[:], EPS).then_inc(pre_dve, 1)
            dve.wait_ge(pre_pe, 1)
            nc.vector.tensor_copy(gcol[:, 0:KD], acc[:, 1, 1, 0:KD]).then_inc(pre_dve, 1)

            def reciprocals(i, slot):
                nc.vector.reciprocal(rstd[:, slot, :], small[:, 2 * i:2 * i + 2]).then_inc(rstd_done, 1)

            for j in range(4):
                round_lo(0, j)
                lo_to(j)
                if j == 1:
                    dve.wait_ge(pre_pe, 2)
                    nc.vector.tensor_copy(gcol[:, KD:3 * KD], acc[:, 1, 1, P + KD:P + 3 * KD]).then_inc(pre_dve, 1)
                if j == 2:
                    dve.wait_ge(pre_pe, 3)
                    nc.vector.tensor_scalar(grow[:, 0:256], acc[0:BIAS_H, 1, 0, 0:256], 1.0 / SCALE, None, ALU.mult).then_inc(grow_done, 1)
                    nc.vector.memset(grow[:, 256:G_W], MASKED / SCALE).then_inc(grow_done, 1)
            dve.wait_ge(memd[0], 16)
            dve.wait_ge(memd[1], 16)
            for t in range(TILES):
                nc.vector.tensor_tensor_reduce(out=junk[:, t], in0=mems[:, t], in1=mems[:, t], scale=1.0, scalar=0.0, op0=ALU.mult,
                                               op1=ALU.add, accum_out=ssq[:, 0, t:t + 1]).then_inc(ssq_done, 1)
            for j in range(4):
                round_lo(1, j)
            dve.wait_ge(pre_pe, 4)
            nc.vector.tensor_copy(post[:], acc[:, 1, 1, 0:2 * CMP_LEN].rearrange("p (a j) -> p a j", a=2)).then_inc(pre_dve, 1)
            lo_to(4)
            dve.wait_ge(root_done, 1)
            reciprocals(0, 0)
            lo_to(5)
            dve.wait_ge(rstd_done, 1)

            def evac_cols(b):
                v_last = 4 * b + 3
                lo_to(v_last + AHEAD)
                wait_block(b, 1, v_last)
                if b == 0:
                    dst, i, w = kvm[:, 1, :], 0, SLICE
                else:
                    w = ATT_TAIL if b == 5 else SLICE
                    dst, i = pat[:, 1, SLICE * (b - 1):SLICE * (b - 1) + w], 1
                src = acc[:, b % 2, 1, 0:w]
                if b == B_ATT:
                    dst, src = pair_queries(dst, src)
                nc.vector.tensor_scalar(dst, src, rstd[:, i, 1:2], None, ALU.mult).then_inc(ev[1], 1)

            def evac_qk(beta):
                dve.wait_ge(qk_pe, beta + 1)
                nc.vector.tensor_copy(qkt[:, 2 * beta:2 * beta + 2, :], sbank[:, beta % 2].rearrange("p (a n) -> p a n", a=2)).then_inc(qk_ev[1], 1)

            evac_cols(0)
            dve.wait_ge(root_done, 2)
            reciprocals(1, 1)
            dve.wait_ge(rstd_done, 2)
            link(nc.vector.tensor_scalar(rstd[:, 4, :], rstd[:, 1, :], 0.5, None, ALU.mult))
            lo_to(7)
            for i in (1, 3, 5):
                dve.wait_ge(tb_pe, i + 1)
                nc.vector.tensor_copy(tb[:, 2 * i:2 * i + 2, :], ob[:].rearrange("p (a n) -> p a n", a=2)).then_inc(tb_ev[1], 1)
                if i > 1:
                    lo_to(7 + i // 2)
            dve.wait_ge(tb_pe, 7)
            nc.vector.tensor_copy(tbc[:, :, :, 0:NCMP], sbank[:, 0, 0:256].rearrange("p (t h c) -> p t h c", t=2, h=NSA_H)[:, :, :, 0:NCMP]).then_inc(tb_ev[1], 1)
            evac_cols(1)
            lo_to(13)
            evac_qk(1)
            evac_cols(2)
            lo_to(16)
            evac_qk(3)
            dve.wait_ge(qk_ev[1], 2)
            for kv in range(2):
                for g in range(GROUPS):
                    for jj in range(2):
                        src = qkt[HD * g:HD * g + HD, QK_KC + kv, jj:jj + 1]
                        pos = post[HD * g:HD * g + HD, kv, jj:jj + 1]
                        ins = nc.vector.tensor_tensor(
                            gcmp[HD * jj:HD * jj + HD, kv, :, NCMP * g:NCMP * g + NCMP],
                            bass.AP(src.tensor, src.offset, [src.ap[0], [2, PAIRS], [CMP_STRIDE, NCMP]]),
                            bass.AP(pos.tensor, pos.offset, [pos.ap[0], [2, PAIRS], [0, NCMP]]), ALU.add)
            ins.then_inc(cmp_g, 1)
            evac_cols(3)
            lo_to(21)
            dve.wait_ge(cmp_pe, 1)
            link(nc.vector.tensor_copy(hx[:, 0, :], ob[:, 0:4 * NCMP]))
            link(nc.vector.tensor_tensor(hx[:, 1, :], hx[:, 0, :], hx[:, 0, :], ALU.mult))
            link(nc.vector.tensor_scalar(hx[:, 1, :], hx[:, 1, :], 0.044715, 1.0, ALU.mult, ALU.add))
            nc.vector.tensor_tensor(hx[:, 1, :], hx[:, 1, :], hx[:, 0, :], ALU.mult).then_inc(cmp_dve, 1)
            dve.wait_ge(cmp_act, 1)
            link(nc.vector.scalar_tensor_tensor(hx[:, 2, :], hx[:, 2, :], 1.0, hx[:, 0, :], ALU.add, ALU.mult))
            nc.vector.tensor_scalar(hidk[:], hx[:, 2, 0:2 * NCMP], 0.5, None, ALU.mult)
            dve.wait_ge(zeroed, 2)
            for i in range(HPG):
                ins = nc.vector.tensor_scalar(hidv[:, :, i, 0:NCMP],
                                              hx[:, 2, 2 * NCMP:4 * NCMP].rearrange("p (g c) -> p g c", g=GROUPS),
                                              0.5, None, ALU.mult)
            ins.then_inc(cmp_dve, 1)
            evac_cols(4)
            lo_to(23)
            dve.wait_ge(cmp_pe, 2)
            for g in range(GROUPS):
                nc.vector.tensor_copy(kct[HD * g:HD * g + HD, :], ob[HD * g:HD * g + HD, 64 + NCMP * g:64 + NCMP * g + NCMP])
            for i in range(HPG):
                ins = nc.vector.tensor_copy(vcz[32 * i:32 * i + 32, :, i, :],
                                            ob[32 * i:32 * i + 32, 128:256].rearrange("p (g d) -> p g d", g=GROUPS))
            ins.then_inc(cmp_dve, 1)
            dve.wait_ge(cmp_act, 2)
            link(nc.vector.tensor_scalar(gsig[:], gsig[:], 0.5, 0.5, ALU.mult, ALU.add))
            gview = gsig[:].rearrange("p t (h b) -> p t h b", b=3)
            evac_qk(5)
            evac_cols(5)
            x16 = xc[:].rearrange("p t h c -> p (t h) c")[:, :, 0:NCMP]
            dve.wait_ge(cmp_pe, 3)
            for g, bank in enumerate((ob, ptb)):
                hs = slice(HPG * g, HPG * g + HPG)
                ins = nc.vector.tensor_tensor(xc[:, :, hs, 0:NCMP],
                                              bank[:, 0:P].rearrange("p (t h c) -> p t h c", t=2, h=HPG)[:, :, :, 0:NCMP],
                                              tbc[:, :, hs, 0:NCMP], ALU.add)
            link(ins)
            link(nc.vector.tensor_reduce(cst[:, 0, :], x16, AX, ALU.max))
            m16 = cst[:, 0, :]
            nc.vector.tensor_tensor(x16, x16, bass.AP(m16.tensor, m16.offset, [m16.ap[0], [1, 16], [0, NCMP]]), ALU.subtract).then_inc(cmp_dve, 1)

            def merge(b):
                c = SLICE * (b % 2)
                branch = {B_MOBA: 1, B_MEM: 2, B_NSA: 0}[b - b % 2]
                v_last = V_MOBA + b - B_MOBA if b < B_NSA else V_NSA + 2 * (b - B_NSA) + 1
                lo_to(v_last + AHEAD)
                for t in range(TILES):
                    wait_block(b, t, v_last)
                    g = gates[:, t, D * branch + c:D * branch + c + SLICE]
                    dst = yb[:, t, c:c + SLICE] if b < B_MEM else tmp[:, t]
                    nc.vector.scalar_tensor_tensor(dst, g, 1.0, acc[:, b % 2, t], ALU.add, ALU.mult).then_inc(ev[t], 1)
                    if b >= B_MEM:
                        dve.wait_ge(ev[t], b + 1)
                        ins = nc.vector.tensor_tensor(yb[:, t, c:c + SLICE], yb[:, t, c:c + SLICE], tmp[:, t], ALU.add)
                        if b >= B_NSA:
                            ins.then_inc(y_done, 1)
                        else:
                            link(ins)

            for n in range(JOBS + 2):
                if n < JOBS:
                    kind, h, _qb, _qh, _kb, bh = jobs[n]
                    dve.wait_ge(s_done, n + 1)
                    if kind == "mem":
                        link(nc.vector.tensor_reduce(jst[:, 0, n, :], sbank[:, n % 2].rearrange("p (t k) -> p t k", t=2), AX, ALU.max))
                    else:
                        if n >= 2:
                            dve.wait_ge(t_done, t_count(n - 2))
                        for t in range(TILES):
                            c0, c1 = prob_cols(kind, t)
                            nc.vector.tensor_tensor(sx[:, n % 2, c0:c1], sbank[:, n % 2, c0:c1], tb[:, bh, 128 * (1 - t):256], ALU.add).then_inc(dve_c, 1)
                            chain[0] += 1
                        dve.wait_ge(dve_c, chain[0] - 1)
                        for t in range(TILES):
                            c0, c1 = prob_cols(kind, t)
                            if t == 1:
                                dve.wait_ge(dve_c, chain[0])
                            ins = nc.vector.reduce_max(jst[:, 0, n, t:t + 1], sx[:, n % 2, c0:c1], axis=AX)
                        link(ins)
                    nc.vector.tensor_scalar(jst[:, 1, n, :], jst[:, 0, n, :], -SCALE, None, ALU.mult).then_inc(x_done, 1)
                lo_to(V_GATE + n + AHEAD)
                if n == 0:
                    evac_qk(7)
                if n < JOBS:
                    dve.wait_ge(e_done, n + 1)
                    if kind in ("sel", "win"):
                        link(nc.vector.reciprocal(jst[:, 3, n, :], jst[:, 2, n, :]))
                        nc.vector.tensor_tensor(jst[:, 4, n, :], jst[:, 3, n, :], gview[:, :, h, 1 if kind == "sel" else 2], ALU.mult).then_inc(r_done, 1)
                    else:
                        nc.vector.reciprocal(jst[:, 4, n, :], jst[:, 2, n, :]).then_inc(r_done, 1)
                if n == 0:
                    dve.wait_ge(cmp_act, 3)
                    dve.wait_ge(zeroed, 3)
                    link(nc.vector.tensor_reduce(cst[:, 1, :], x16, AX, ALU.add))
                    link(nc.vector.reciprocal(cst[:, 2, :], cst[:, 1, :]))
                    link(nc.vector.tensor_tensor(cst[:, 3, :].rearrange("p (t h) -> p t h", t=2), cst[:, 2, :].rearrange("p (t h) -> p t h", t=2), gview[:, :, :, 0], ALU.mult))
                    for t in range(TILES):
                        f8 = cst[:, 3, NSA_H * t:NSA_H * t + NSA_H]
                        ins = nc.vector.scalar_tensor_tensor(
                            pcz[:, t].rearrange("p g i c -> p (g i) c")[:, :, 0:NCMP], xc[:, t, :, 0:NCMP], row_any[:, t:t + 1],
                            bass.AP(f8.tensor, f8.offset, [f8.ap[0], [1, NSA_H], [0, NCMP]]), ALU.mult, ALU.mult)
                    ins.then_inc(cmp_dve, 1)
                if n >= 2 and ends_pair(n - 2):
                    p = pair_of(n - 2)
                    dve.wait_ge(oh_done, p + 1)
                    nc.vector.tensor_tensor(ol[:, p, :], ob[:, 0:256], oh[:, p, :].bitcast(F32), ALU.subtract).then_inc(ol_done, 1)

                if n == JOBS:
                    merge(B_MOBA)
                    merge(B_MOBA + 1)

            merge(B_MEM)
            merge(B_MEM + 1)
            merge(B_NSA)
            lo_to(V_NSA + 2 + AHEAD)
            for j in range(2):
                round_lo(2, j)
            merge(B_NSA + 1)
            lo_to(V_MIX + AHEAD)
            for j in range(2, 4):
                round_lo(2, j)

            def gain_halves(i, b0, v_last):
                for n in range(2):
                    lo_to(v_last[n] + AHEAD)
                    for t in range(TILES):
                        dve.wait_ge(sq_done, 4 * i + 2 * n + t + 1)
                        nc.vector.tensor_tensor(yb[:, t, SLICE * n:SLICE * n + SLICE], acc[:, (b0 + n) % 2, t],
                                                gpost[:, SLICE * n:SLICE * n + SLICE], ALU.mult).then_inc(ev[t], 1)
                nc.vector.tensor_tensor(ssq[:, 2 * i + 2, :], part[:, i, 0, :], part[:, i, 1, :], ALU.add).then_inc(sum_done, 1)

            def residual(slot, signal):
                for n in range(2):
                    for t in range(TILES):
                        c = slice(SLICE * n, SLICE * n + SLICE)
                        dve.wait_ge(ev[t], ev_base[slot] + n + 1)
                        nc.vector.scalar_tensor_tensor(xs[:, t, c], yb[:, t, c], rstd[:, slot, t:t + 1], xs[:, t, c],
                                                       ALU.mult, ALU.add).then_inc(signal, 1)

            ev_base = {2: B_MIX, 5: B_MIX + 2}
            dve.wait_ge(gpostd, 16)
            gain_halves(0, B_MIX, [V_MIX + 3, V_MIX + 7])
            dve.wait_ge(root_done, 3)
            reciprocals(2, 2)
            dve.wait_ge(rstd_done, 3)
            residual(2, x1_done)
            for j in range(4):
                round_lo(3, j)
            dve.wait_ge(root_done, 4)
            reciprocals(3, 3)
            dve.wait_ge(rstd_done, 4)

            def ffn_lo(i, j, s):
                vj = AHEAD + s + 4 * j
                lo(V_GU + AHEAD + s + 4 * i, (vj // 2) % RAW, vj % 2, SLICE)

            def ffn_al(i):
                dve.wait_ge(ah_done, i + 1)
                nc.vector.tensor_tensor(al[:, bass.ds(i * 2, 2), :], ptb[:].rearrange("p (k n) -> p k n", k=2),
                                        ah[:, bass.ds(i * 2, 2), :].bitcast(F32), ALU.subtract).then_inc(al_done, 1)

            def ffn_dve(i, j, first):
                for s in range(4):
                    ffn_lo(i, j, s)
                    if s == 2 and not first:
                        ffn_al(i - 1)
                for t in range(TILES):
                    dve.wait_ge(silu_done, i * 2 + (t + 1))
                    if not first:
                        dve.wait_ge(at_done, i)
                    nc.vector.scalar_tensor_tensor(act_tok[:, t], acc[:, j % 2, t, GU_W:2 * GU_W], rstd[:, 3, t:t + 1],
                                                   silu[:, t], ALU.mult, ALU.mult).then_inc(prod_done, 1)

            ffn_dve(0, 0, True)
            with nc.vector.Fori(0, (GU_BLOCKS - 1) // 2) as it:
                for j in range(2):
                    ffn_dve(it * 2 + (1 + j), 1 - j, False)
            split[0] = V_GU + 4 * GU_BLOCKS + AHEAD
            lo_to(V_DOWN + 2 + AHEAD)
            ffn_al(GU_BLOCKS - 1)
            dve.wait_ge(gpostd, 32)
            gain_halves(1, B_DOWN, [V_DOWN + 10, V_DOWN + 21])
            dve.wait_ge(root_done, 5)
            reciprocals(4, 5)
            dve.wait_ge(rstd_done, 5)
            residual(5, fin_done)

        @block.tensor
        def _(pe):
            def product(bank, h, l, k, t, slot, s, w, first, last):
                c = slice(P * t, P * t + P)
                nc.tensor.matmul(bank[:, 0:w], h[:, k, c], wh[:, slot, s, 0:w], start=first, stop=False)
                nc.tensor.matmul(bank[:, 0:w], h[:, k, c], wl[:, slot, s, 0:w], start=False, stop=False)
                return nc.tensor.matmul(bank[:, 0:w], l[:, k, c], wh[:, slot, s, 0:w], start=False, stop=last)

            def sub(v, slot, parity, h, l, k0, w, first, last):
                pe.wait_ge(lo_done, v + 1)
                for t in range(TILES):
                    for s in range(2):
                        ins = product(acc[:, parity, t], h, l, k0 + s, t, slot, s, w,
                                      first and s == 0, last and s == 1)
                    if t == 0 and last:
                        ins.then_inc(acc0_done, 1)
                ins.then_inc(mm_done, 1)

            def free_acc(b, static=True):
                if static and b < 2:
                    return
                for t in range(TILES):
                    pe.wait_ge(ev[t], b - 1)

            def whole_block(b, v0, subs, h, l, k0=0, w=SLICE, ready=None, after=None):
                free_acc(b)
                for i in range(subs):
                    if ready is not None:
                        pe.wait_ge(tl_done, 4 * ready + i + 1)
                    sub(v0 + i, (v0 + i) % SUBS, b % 2, h, l, k0 + 2 * i, w, i == 0, i == subs - 1)
                    for work in (after or {}).get(i, ()):
                        work()

            def transpose_bank(r, j, src):
                bank = quad[j]
                for kk in range(2):
                    for t in range(TILES):
                        ins = nc.tensor.transpose(bank[:, 256 * kk + P * t:256 * kk + P * t + P],
                                                  src[:, t, P * (2 * j + kk):P * (2 * j + kk) + P], ident)
                ins.then_inc(tp_done, 1)

            pe.wait_ge(constd, 16)
            pe.wait_ge(memd[0], 16)
            transpose_bank(0, 0, mems)
            transpose_bank(0, 1, mems)
            pe.wait_ge(gaind[0], 16)
            nc.tensor.transpose(acc[:, 1, 1, 0:KD], grows[0:KD, :], ident[0:KD, 0:KD]).then_inc(pre_pe, 1)
            pe.wait_ge(memd[1], 16)
            transpose_bank(0, 2, mems)
            transpose_bank(0, 3, mems)

            def gains_and_bias_row():
                pe.wait_ge(gaind[1], 2 * 16)
                pe.wait_ge(pre_dve, 2)
                nc.tensor.transpose(acc[:, 1, 1, P:P + 3 * KD], grows[:], ident[0:3 * KD, 0:3 * KD]).then_inc(pre_pe, 1)
                pe.wait_ge(reld, 2 * 16)
                nc.tensor.matmul(acc[0:BIAS_H, 1, 0, :], rel[:], onehot, start=True, stop=True).then_inc(pre_pe, 1)

            def positions():
                pe.wait_ge(posd, 4 * 16)
                pe.wait_ge(pre_dve, 3)
                for kv in range(2):
                    ins = nc.tensor.transpose(acc[:, 1, 1, CMP_LEN * kv:CMP_LEN * kv + CMP_LEN],
                                              pos2[:, kv].rearrange("j r d -> j (r d)"), ident[0:CMP_LEN, 0:CMP_LEN])
                ins.then_inc(pre_pe, 1)

            def round_x():
                pe.wait_ge(xd, 16)
                for j in range(4):
                    pe.wait_ge(tl_done, j + 1)
                    transpose_bank(1, j, xs)

            def bias_tables(i):
                if i == 0:
                    pe.wait_ge(bp_d, 16)
                    pe.wait_ge(tl_done, 8)
                for i in (2 * i, 2 * i + 1):
                    if i >= 2:
                        pe.wait_ge(tb_ev[i % 2], i // 2)
                    dst = (ptb, ob)[i % 2]
                    nc.tensor.matmul(dst[:].rearrange("p (a n) -> p a n", a=2), flip, bp[:, 2 * i:2 * i + 2, 0:256],
                                     start=True, stop=True).then_inc(tb_pe, 1)

            def compressed_bias():
                for t in range(TILES):
                    off = 31 + P * (1 - t)
                    src = bp[:, 0:NSA_H, off:off + 1]
                    ins = nc.tensor.matmul(sbank[:, 0, P * t:P * t + P].rearrange("p (h c) -> p h c", h=NSA_H)[:, :, 0:NCMP], flip,
                                           bass.AP(src.tensor, src.offset, [src.ap[0], [BP_W, NSA_H], [CMP_STRIDE, NCMP]]),
                                           start=True, stop=True)
                ins.then_inc(tb_pe, 1)

            whole_block(B_MEMKV, 0, 4, memh, meml, ready=0,
                        after={0: [gains_and_bias_row], 1: [round_x], 3: [positions]})
            pe.wait_ge(pre_dve, 4)

            def qk_batch(beta, blocks_ready, sources):
                for t in range(TILES):
                    pe.wait_ge(ev[t], blocks_ready)
                if beta >= 2:
                    pe.wait_ge(qk_ev[beta % 2], beta // 2)
                if beta == 0:
                    pe.wait_ge(tb_ev[1], 4)
                for i, src in enumerate(sources):
                    for t in range(TILES):
                        ins = nc.tensor.transpose(sbank[:, beta % 2, 256 * i + P * t:256 * i + P * t + P], src(t), ident)
                ins.then_inc(qk_pe, 1)

            def col(c):
                return lambda t: pat[:, t, c:c + P]

            def compress_1():
                pe.wait_ge(cmp_g, 1)
                pe.wait_ge(cmpd, 5 * 16)
                for kv in range(2):
                    for j in range(PAIRS):
                        ins = nc.tensor.matmul(ob[:, 2 * NCMP * kv:2 * NCMP * (kv + 1)], w1[:, kv, j, :], gcmp[:, kv, j, :],
                                               start=(j == 0), stop=(j == PAIRS - 1))
                ins.then_inc(cmp_pe, 1)

            def compress_2():
                pe.wait_ge(cmp_dve, 2)
                nc.tensor.matmul(ob[:, 64:64 + 2 * NCMP], w2k[:].rearrange("p r d -> p (r d)"), hidk[:], start=True, stop=True)
                for g in range(GROUPS):
                    ins = nc.tensor.matmul(ob[:, 128 + HD * g:128 + HD * g + HD], hidv[:, g].rearrange("p i c -> p (i c)"), w2v[:],
                                           start=True, stop=True)
                ins.then_inc(cmp_pe, 1)

            def compressed_scores():
                pe.wait_ge(cmp_dve, 3)
                for h in range(NSA_H):
                    for t in range(TILES):
                        g = h // HPG
                        c = 16 * (HPG * t + h % HPG)
                        ins = nc.tensor.matmul((ob, ptb)[g][:, c:c + NCMP], qkt[HD * g:HD * g + HD, QK_Q + h % HPG, P * t:P * t + P],
                                               kct[HD * g:HD * g + HD, :], start=True, stop=True)
                ins.then_inc(cmp_pe, 1)

            whole_block(1, 4, 4, xh, xl, ready=1,
                        after={2: [lambda: bias_tables(0)],
                               3: [lambda: bias_tables(1), lambda: bias_tables(2), compressed_bias]})
            whole_block(2, 8, 4, xh, xl,
                        after={1: [lambda: qk_batch(0, 1, [lambda t: kvm[:, t, 0:P], lambda t: kvm[:, t, P:2 * P]])],
                               2: [lambda: qk_batch(1, 2, [col(0), col(P)])],
                               3: [lambda: qk_batch(2, 2, [col(2 * P), col(3 * P)])]})
            whole_block(3, 12, 4, xh, xl, after={1: [lambda: qk_batch(3, 3, [col(C_KC), col(C_VC)])]})
            whole_block(4, 16, 4, xh, xl, after={1: [lambda: qk_batch(4, 4, [col(C_KS), col(C_KW)])], 2: [compress_1]})
            whole_block(5, 20, 4, xh, xl, w=ATT_TAIL,
                        after={0: [compress_2], 1: [lambda: qk_batch(5, 5, [col(C_QM), col(C_QM + P)])],
                               2: [lambda: qk_batch(6, 5, [col(C_KM), col(C_KM + P)])], 3: [compressed_scores]})

            def scores(n):
                kind, h, qb, qh, kb, _bh = jobs[n]
                half = slice(HD * qh, HD * qh + HD)
                if n == 0:
                    pe.wait_ge(qk_ev[1], 3)
                    pe.wait_ge(qk_ev[0], 4)
                elif n == 1:
                    pe.wait_ge(qk_ev[1], 4)
                else:
                    pe.wait_ge(e_done, n - 1)
                for t in range(TILES):
                    c0, c1 = prob_cols(kind, t)
                    ins = nc.tensor.matmul(sbank[:, n % 2, c0:c1], qkt[half, qb, P * t:P * t + P], qkt[half, kb, 0:c1 - c0],
                                           start=True, stop=True)
                ins.then_inc(s_done, 1)

            def turn(n):
                kind = jobs[n][0]
                pe.wait_ge(p_done, n + 1)
                if n:
                    pe.wait_ge(te_done, t_count(n) - 1)
                else:
                    pe.wait_ge(cmp_dve, 4)
                pieces = [(0, 0), (P, P), (2 * P, 2 * P)] if kind != "mem" else [(0, 0), (2 * P, P), (P, 2 * P), (3 * P, 3 * P)]
                for src, dst in pieces:
                    ins = nc.tensor.transpose(ptb[:, dst:dst + P], sx[:, n % 2, src:src + P], ident)
                ins.then_inc(t_done, 1)

            def values(n):
                kind, h = jobs[n][0:2]
                starts = kind != "win"
                ends = kind != "sel"
                if n == 0:
                    pe.wait_ge(cmp_dve, 4)
                elif ends_pair(n - 1):
                    pe.wait_ge(ol_done, pair_of(n))
                dst = ob[HD * (h % 2):HD * (h % 2) + HD]
                if kind == "sel":
                    g = h // HPG
                    nc.tensor.matmul(dst[:, 0:256], vcz[:, g, h % HPG, :], pct[:, g, :], start=True, stop=False)
                    starts = False
                if kind == "moba":
                    v = [pat[:, t, C_VM + HD * h:C_VM + HD * h + HD] for t in range(2)]
                elif kind == "mem":
                    v = [kvm[:, t, 256 + HD * h:256 + HD * h + HD] for t in range(2)]
                else:
                    c = (C_VS if kind == "sel" else C_VW) + HD * (h // HPG)
                    v = [pat[:, t, c:c + HD] for t in range(2)]
                pe.wait_ge(te_done, t_count(n))
                nc.tensor.matmul(dst[:, 0:256], v[0], pts[:, n % 2, 0:256], start=starts, stop=False)
                c0 = 0 if kind == "mem" else P
                nc.tensor.matmul(dst[:, c0:256], v[1], pts[:, n % 2, 256:512 - c0], start=False, stop=ends).then_inc(pv_done, 1)

            for n in range(JOBS + 2):
                if n < JOBS:
                    scores(n)
                if n < JOBS:
                    if n % 4 == 0:
                        free_acc(B_GATE + n // 4)
                    sub(V_GATE + n, n % SUBS, (n // 4) % 2, xh, xl, 2 * (n % 4), SLICE, n % 4 == 0, n % 4 == 3)
                elif n == JOBS:
                    whole_block(B_MOBA, V_MOBA, 1, oh, ol, 0)
                    whole_block(B_MOBA + 1, V_MOBA + 1, 1, oh, ol, 0)
                else:
                    for i in range(2):
                        whole_block(B_MEM + i, V_MEM + i, 1, oh, ol, 2)
                if n == 0:
                    qk_batch(7, 6, [col(C_QX), col(C_QX + P)])
                if n == 2:
                    pe.wait_ge(cmp_dve, 5)
                    pe.wait_ge(te_done, 1)
                    for g in range(GROUPS):
                        for t in range(TILES):
                            ins = nc.tensor.transpose(ptb[:, 256 * g + P * t:256 * g + P * t + P],
                                                      pcz[:, t, g].rearrange("p i c -> p (i c)"), ident)
                    ins.then_inc(t_done, 1)
                if 1 <= n <= JOBS:
                    turn(n - 1)
                if n >= 2:
                    values(n - 2)
            def rounds(r, first, src, ready, count):
                for j in (first, first + 1):
                    pe.wait_ge(ready, count)
                    if r == 3:
                        pe.wait_ge(tl_done, 8 + j + 1)
                    transpose_bank(r, j, src)

            pe.wait_ge(ol_done, 8)
            whole_block(B_NSA, V_NSA, 2, oh, ol, 4)
            whole_block(B_NSA + 1, V_NSA + 2, 2, oh, ol, 4, after={0: [lambda: rounds(2, 0, yb, y_done, 2)]})
            whole_block(B_MIX, V_MIX, 4, xh, xl, ready=2, after={0: [lambda: rounds(2, 2, yb, y_done, 4)]})
            whole_block(B_MIX + 1, V_MIX + 4, 4, xh, xl)
            rounds(3, 0, xs, x1_done, 2)
            whole_block(B_GU, V_GU, 4, xh, xl, ready=3, after={1: [lambda: rounds(3, 2, xs, x1_done, 4)]})

            def ffn_body(i, j, first):
                if first:
                    free_acc(B_GU + 1)
                else:
                    pe.wait_ge(prod_done, i * 2 - 2)
                for s in range(4):
                    sub(i * 4 + (V_GU + s), s, j, xh, xl, 2 * s, SLICE, s == 0, s == 3)
                    if s == 1:
                        ffn_turn_at(i)

            def ffn_turn_at(i):
                pe.wait_ge(prod_done, i * 2)
                pe.wait_ge(al_done, i - 1) if not isinstance(i, int) or i > 1 else None
                for kk in range(2):
                    for t in range(TILES):
                        ins = nc.tensor.transpose(ptb[:, 256 * kk + P * t:256 * kk + P * t + P],
                                                  act_tok[:, t, P * kk:P * kk + P], ident)
                ins.then_inc(at_done, 1)

            ffn_body(1, 1, True)
            ffn_body(2, 0, False)
            with nc.tensor.Fori(0, (GU_BLOCKS - 3) // 2) as it:
                for j in range(2):
                    ffn_body(it * 2 + (3 + j), 1 - j, False)
            for n in range(2):
                pe.wait_ge(prod_done, 2 * (GU_BLOCKS - 1 + n))
                for i in range(11):
                    v = V_DOWN + 11 * n + i
                    sub(v, v % SUBS, (B_DOWN + n) % 2, ah, al, 2 * i, SLICE, i == 0, i == 10)
                    if n == 0 and i == 1:
                        ffn_turn_at(GU_BLOCKS)
                    if n == 0 and i == 8:
                        pe.wait_ge(al_done, GU_BLOCKS)


def bucket_onehot():
    import numpy as np
    dist = 255 - np.arange(G_W)
    exact = BUCKETS // 2
    safe = np.maximum(dist, 1).astype(np.float32)
    logd = np.log(safe / np.float32(exact)).astype(np.float32) / np.float32(np.log(MAX_DIST / exact))
    large = np.minimum(exact + (logd * np.float32(BUCKETS - exact)).astype(np.int32), BUCKETS - 1)
    bucket = np.where(dist < exact, np.maximum(dist, 0), large)
    hot = (bucket[None, :] == np.arange(BUCKETS)[:, None]) & (dist >= 0)[None, :]
    return hot.astype(np.float32)


NAMES = ["x", "mem", "rel_bias", "pre_mix_g", "mem_norm_g", "post_mix_g", "w_in", "cmp_pos_k", "cmp_w1_k", "cmp_w2_k",
         "cmp_pos_v", "cmp_w1_v", "cmp_w2_v", "w_mem_kv", "w_nsa_o", "w_moba_o", "w_mem_o", "w_mix_out",
         "pre_ffn_g", "post_ffn_g", "w_ffn_gate", "w_ffn_up", "w_ffn_down"]


def kernel(**inputs):
    import numpy as np
    import concourse.bacc as bacc
    from concourse.bass_utils import run_bass_kernel_spmd

    nc = bacc.Bacc("TRN2", target_bir_lowering=False, num_devices=1)
    arrays = {f"in_{n}": np.ascontiguousarray(inputs[n]) for n in NAMES}
    rows = np.arange(SEQ).reshape(TILES, P).T
    eye = np.eye(P, dtype=np.float32)
    sees_block = (rows >= CMP_LEN - 1).astype(np.float32)
    arrays["in_const0"] = np.concatenate([eye, sees_block], axis=1)
    hot = np.zeros((P, G_W), np.float32)
    hot[:BUCKETS] = bucket_onehot()
    arrays["in_const1"] = np.concatenate([eye[::-1], hot], axis=1)
    a = {n[3:]: nc.dram_tensor(n, v.shape, F32, kind="ExternalInput").ap() for n, v in arrays.items()}
    out = nc.dram_tensor("out_0", (1, SEQ, D), F32, kind="ExternalOutput").ap()
    g_scratch = nc.dram_tensor("g_scratch", (BIAS_H, G_W), F32, kind="Internal").ap()
    build_layer(nc, a, out, g_scratch)
    r = run_bass_kernel_spmd(nc, [arrays], core_ids=[0])
    return r.results[0]["out_0"]
```

```python
from contextlib import ExitStack

import concourse.bass as bass
from concourse import mybir

F32 = mybir.dt.float32
F32R = mybir.dt.float32r
ALU = mybir.AluOpType
ACT = mybir.ActivationFunctionType
AX = mybir.AxisListType.X

P = 128
SEQ = 256
TILES = SEQ // P
D = 1024
KD = D // P
HD = 64
SCALE = HD ** -0.5
NSA_H, GROUPS, HPG = 8, 2, 4
MOBA_H, MEM_H = 4, 4
BIAS_H = NSA_H + MOBA_H
CMP_LEN, CMP_STRIDE, CMP_HID = 32, 16, 128
NCMP = (SEQ - CMP_LEN) // CMP_STRIDE + 1
PAIRS = CMP_LEN // 2
BUCKETS, MAX_DIST = 32, 128
D_FF = 2816
KF = D_FF // P
EPS = 1e-6
MASKED = -1e30

C_Q, C_KC, C_VC, C_KS, C_VS, C_KW, C_VW, C_GN = 0, 512, 640, 768, 896, 1024, 1152, 1280
C_QM, C_KM, C_VM, C_QX, C_GATES = 1304, 1560, 1816, 2072, 2328
ATT_W = C_GATES

SLICE = 512
ATT_TAIL = ATT_W - 4 * SLICE
RAW, SUBS = 4, 4
AHEAD = SUBS - 1

B_MEMKV, B_ATT, B_GATE, B_MOBA, B_GATE_MEM, B_MEM, B_NSA, B_MIX, B_GU, B_DOWN = 0, 1, 6, 10, 12, 14, 16, 18, 20, 31
GU_BLOCKS, GU_W = 11, 256
U_GU, U_DOWN = 32, 54
UNITS = U_DOWN + 2 * KF // 4
V_GATE, V_MOBA, V_GATE_MEM, V_MEM, V_NSA, V_MIX, V_GU, V_DOWN = 24, 40, 42, 50, 52, 56, 2 * U_GU, 2 * U_DOWN

JOBS = 24

Q_NSA, Q_MOBA, Q_MEM, Q_HEADS = 0, 8, 12, 16
K_MEM, K_SEL, K_WIN, K_MOBA, K_HEADS = 0, 4, 6, 8, 12
QK_BATCHES = [("k", K_MEM, 2, 1), ("q", Q_NSA, 1, 4), ("q", Q_NSA + 2, 1, 4), ("compress", 0, 0, 0),
              ("k", K_SEL, 2, 1), ("q", Q_MOBA, 2, 1), ("k", K_MOBA, 2, 1), ("q", Q_MEM, 2, 1)]
QK_COMPRESS, QK_LAST = 3, 7

G_W, BP_W = 512, 384


def job_plan():
    jobs = []
    for m in range(MOBA_H):
        jobs.append(("moba", m, Q_MOBA + m, m % 2, K_MOBA + m, NSA_H + m))
    for m in range(MEM_H):
        jobs.append(("mem", m, Q_MEM + m, m % 2, K_MEM + m, None))
    for h in range(NSA_H):
        for kind, first in (("sel", K_SEL), ("win", K_WIN)):
            jobs.append((kind, h, Q_NSA + h, h // HPG, first + h // HPG, h))
    return jobs


def pair_of(job):
    return job // 2 if job < 8 else 4 + (job - 8) // 4


def ends_pair(job):
    return job % 2 == 1 if job < 8 else (job - 8) % 4 == 3


CMP_SLOT = 4


def t_count(job):
    return job + 1 if job < CMP_SLOT - 1 else job + 2


def look_ahead(n):
    return AHEAD - 1 if n < 6 else AHEAD


def build_layer(nc, a, out, g_scratch):
    jobs = job_plan()
    xf = a["x"][0].rearrange("(t p) d -> p t d", p=P)
    memf = a["mem"][0].rearrange("(t p) d -> p t d", p=P)
    outf = out[0].rearrange("(t p) d -> p t d", p=P)

    def rows(name):
        return a[name][0].rearrange("(k p) n -> p k n", p=P)

    w_in, w_memkv = rows("w_in"), rows("w_mem_kv")
    w_nsa, w_moba, w_mem, w_mix = rows("w_nsa_o"), rows("w_moba_o"), rows("w_mem_o"), rows("w_mix_out")
    w_gate, w_up, w_down = rows("w_ffn_gate"), rows("w_ffn_up"), rows("w_ffn_down")

    with ExitStack() as ctx:
        def sb(name, shape, dt=F32, stack=ctx):
            return stack.enter_context(nc.sbuf_tensor(name, shape, dt))

        def psum(name, shape):
            return ctx.enter_context(nc.psum_tensor(name, shape, F32))

        def sem(name):
            return ctx.enter_context(nc.semaphore(name))

        raw = sb("raw", [P, RAW, 4, SLICE])
        wh = sb("wh", [P, SUBS, 2, SLICE], F32R)
        wl = sb("wl", [P, SUBS, 2, SLICE], F32R)
        xh = sb("xh", [P, KD, SEQ], F32R)
        xl = sb("xl", [P, KD, SEQ], F32R)
        const0 = sb("const0", [P, P + TILES])
        ident, row_any = const0[:, 0:P], const0[:, P:P + TILES]
        gcol = sb("gcol", [P, 3 * KD])
        eps = sb("eps", [P, 1])
        ssq = sb("ssq", [P, 8, TILES])
        part = sb("part", [P, 2, 2, TILES])
        rstd = sb("rstd", [P, 8, TILES])
        small = sb("small", [P, 64])
        with ExitStack() as s:
            memh = sb("memh", [P, KD, SEQ], F32R, s)
            meml = sb("meml", [P, KD, SEQ], F32R, s)
            mems = sb("mems", [P, TILES, D], F32, s)
        with ExitStack() as s:
            gcmp = sb("gcmp", [P, 2, PAIRS, GROUPS * NCMP], F32, s)
        gates = sb("gates", [P, TILES, 3 * D])
        with ExitStack() as s:
            w1 = sb("w1", [P, 2, PAIRS, CMP_HID], F32, s)
        oh = sb("oh", [P, 8, SEQ], F32R)
        ol = sb("ol", [P, 8, SEQ], F32R)
        late = ExitStack()
        with ExitStack() as s:
            bp = sb("bp", [P, BIAS_H, BP_W], F32, s)
        with ExitStack() as s:
            pat = sb("pat", [P, TILES, 4 * SLICE], F32, s)
            pct = sb("pct", [P, GROUPS, SEQ], F32, s)
            kvm = sb("kvm", [P, TILES, 2 * 256], F32, s)
            with ExitStack() as early:
                junk = sb("junk", [P, 4, D], F32, early)
                x0 = sb("x0", [P, TILES, D], F32, early)
            qst = sb("qst", [P, Q_HEADS, SEQ], F32R, s)
            khh = sb("khh", [P, K_HEADS, SEQ], F32R, s)
            klo = sb("klo", [P, K_HEADS // 2, SEQ], F32R, s)
            tb = sb("tb", [P, BIAS_H, 256], F32, s)
            tbc = sb("tbc", [P, TILES, NSA_H, 16], F32, s)
            with ExitStack() as early:
                rel = sb("rel", [BUCKETS, BIAS_H], F32, early)
                const1 = sb("const1", [P, P + G_W], F32, early)
                grow = sb("grow", [BIAS_H, G_W], F32, early)
                pos2 = sb("pos2", [CMP_LEN, 2, 2, HD], F32, early)
                grows = sb("grows", [3 * KD, P], F32, early)
            with ExitStack() as early:
                kvc = sb("kvc", [P, 2, SEQ], F32, early)
            flip, onehot = const1[:, 0:P], const1[0:BUCKETS, P:P + G_W]
            sx = sb("sx", [P, 2, 512], F32, s)
            pts = sb("pts", [P, 2, 512], F32, s)
            post = sb("post", [P, 2, CMP_LEN], F32, s)
            pcz = sb("pcz", [P, TILES, GROUPS, HPG, 32], F32, s)
            w2k = sb("w2k", [CMP_HID, 2, HD], F32, s)
            w2v = sb("w2v", [CMP_HID, HD], F32, s)
            hx = sb("hx", [P, 3, 4 * NCMP], F32, s)
            hidk = sb("hidk", [P, GROUPS * NCMP], F32, s)
            hidv = sb("hidv", [P, GROUPS, HPG, 32], F32, s)
            ckeys = sb("ckeys", [P, GROUPS, 2, 16], F32R, s)
            vcz = sb("vcz", [P, GROUPS, HPG, HD], F32, s)
            xc = sb("xc", [P, TILES, NSA_H, 16], F32, s)
            cst = sb("cst", [P, 4, TILES * NSA_H], F32, s)
            gsig = sb("gsig", [P, TILES, 3 * NSA_H], F32, s)
            jst = sb("jst", [P, 5, JOBS, TILES], F32, s)
        with late:
            ah = sb("ah", [P, KF, SEQ], F32R, late)
            al = sb("al", [P, KF, SEQ], F32R, late)
            yb = sb("yb", [P, TILES, D], F32, late)
            tmp = sb("tmp", [P, TILES, SLICE], F32, late)
            silu = sb("silu", [P, TILES, GU_W], F32, late)
            act_tok = sb("act_tok", [P, TILES, GU_W], F32, late)
            xs = sb("xs", [P, TILES, D], F32, late)
            gpost = sb("gpost", [P, D], F32, late)

        acc = psum("acc", [P, 2, TILES, 512])
        sbank = psum("sbank", [P, 2, 512])
        ptb = psum("ptb", [P, 512])
        ob = psum("ob", [P, 512])
        quad = [sbank[:, 0], sbank[:, 1], ptb[:], ob[:]]

        loaded = [sem(f"loaded{i}") for i in range(RAW)]
        hi_done = sem("hi_done")
        lo_done = sem("lo_done")
        mm_done = sem("mm_done")
        acc0_done = sem("acc0_done")
        ev = [sem("ev0"), sem("ev1")]
        xd, xsd, memd = sem("xd"), sem("xsd"), [sem("memd0"), sem("memd1")]
        constd, const1d, gaind = sem("constd"), sem("const1d"), [sem("gaind0"), sem("gaind1")]
        sub0d, posd, reld, cmpd, gpostd = sem("sub0d"), sem("posd"), sem("reld"), sem("cmpd"), sem("gpostd")
        grow_done, g_stored, bp_d = sem("grow_done"), sem("g_stored"), sem("bp_d")
        out_d = sem("out_d")
        zeroed = sem("zeroed")
        dve_c = sem("dve_c")
        ssq_done, root_done, rstd_done = sem("ssq_done"), sem("root_done"), sem("rstd_done")
        tp_done, th_done, tl_done = sem("tp_done"), sem("th_done"), sem("tl_done")
        pre_pe, pre_dve = sem("pre_pe"), sem("pre_dve")
        tb_pe, tb_ev = sem("tb_pe"), [sem("tb_ev0"), sem("tb_ev1")]
        qk_pe, qk_hi, qk_ev = sem("qk_pe"), sem("qk_hi"), [sem("qk_ev0"), sem("qk_ev1")]
        cmp_g, cmp_pe, cmp_dve, cmp_act = sem("cmp_g"), sem("cmp_pe"), sem("cmp_dve"), sem("cmp_act")
        s_done, x_done, e_done, r_done, p_done = (sem("s_done"), sem("x_done"), sem("e_done"), sem("r_done"),
                                                  sem("p_done"))
        t_done, te_done, pv_done = sem("t_done"), sem("te_done"), sem("pv_done")
        oh_done, ol_done = sem("oh_done"), sem("ol_done")
        silu_done, prod_done, at_done, ah_done, al_done = (sem("silu_done"), sem("prod_done"), sem("at_done"),
                                                           sem("ah_done"), sem("al_done"))
        y_done, m_done = sem("y_done"), sem("m_done")
        x1_done, fin_done = [sem("x1_done0"), sem("x1_done1")], [sem("fin_done0"), sem("fin_done1")]
        sq_done, sum_done, scaled = sem("sq_done"), sem("sum_done"), sem("scaled")

        block = ctx.enter_context(nc.Block())

        def width(v):
            return ATT_TAIL if v // 4 == B_ATT + 4 else SLICE

        def pat_col(c):
            return c - SLICE if c >= SLICE else 3 * SLICE + c

        def prob_cols(kind, t):
            if kind == "mem":
                return 256 * t, 256 * t + 256
            return (0, 128) if t == 0 else (128, 384)

        def stacked(beta, side):
            kind, first, step, second = QK_BATCHES[beta]
            h0 = first + second * side
            return slice(h0, h0 + step + 1, step), slice(h0 // 2, h0 // 2 + 2)

        def qk_bank(beta):
            bank = ob[:] if beta == QK_LAST else sbank[:, beta % 2]
            return bank.rearrange("p (a n) -> p a n", a=2)

        def half_rows(side):
            return slice(HD * side, HD * side + HD)

        def pair_queries(dst, src):
            return (dst.rearrange("p (i g d) -> p g i d", g=GROUPS, i=HPG),
                    src.rearrange("p (g i d) -> p g i d", g=GROUPS, i=HPG))

        @block.sync
        def _(sp):
            def free_slot(u):
                if isinstance(u, int) and u < RAW:
                    return
                sp.wait_ge(lo_done, 2 * (u - RAW) + 2)

            def unit(u, slot, parts):
                free_slot(u)
                for dst, src in parts:
                    sp.dma_start(dst, src).then_inc(loaded[slot], 32 // len(parts))

            def plain(u, src, k0, c0, w=SLICE):
                unit(u, u % RAW, [(raw[:, u % RAW, :, 0:w], src[:, k0:k0 + 4, c0:c0 + w])])

            for c in range(2):
                sp.dma_start(mems[:, :, SLICE * c:SLICE * c + SLICE],
                        memf[:, :, SLICE * c:SLICE * c + SLICE]).then_inc(memd[c], 16)
                sub_load = sp.dma_start(raw[:, 0, 2 * c:2 * c + 2, :], w_memkv[:, 2 * c:2 * c + 2, 0:SLICE])
                if c == 0:
                    sub_load.then_inc(sub0d, 16)
                else:
                    sub_load.then_inc(loaded[0], 32)
            sp.dma_start(const1[:], a["const1"]).then_inc(const1d, 16)
            plain(1, w_memkv, 4, 0)
            sp.dma_start(x0[:], xf).then_inc(xd, 16)
            plain(2, w_in, 0, 0)
            plain(3, w_in, 4, 0)
            sp.wait_ge(grow_done, 2)
            sp.dma_start(g_scratch, grow[:]).then_inc(g_stored, 16)
            sp.wait_ge(g_stored, 16)
            sp.dma_start(bp[:], bass.AP(g_scratch.tensor, 0, [[1, P], [G_W, BIAS_H], [1, BP_W]])).then_inc(bp_d, 16)
            u = 4
            for b in range(1, 5):
                for half in range(2):
                    plain(u, w_in, 4 * half, SLICE * b, SLICE if b < 4 else ATT_TAIL)
                    u += 1
            for gate_blocks, w in (((0, 1, 2, 3), w_moba), ((4, 5), w_mem)):
                for b in gate_blocks:
                    for half in range(2):
                        plain(u, w_in, 4 * half, C_GATES + SLICE * b)
                        u += 1
                unit(u, u % RAW, [(raw[:, u % RAW, 2 * n:2 * n + 2, :], w[:, :, SLICE * n:SLICE * n + SLICE])
                                  for n in range(2)])
                u += 1
            for n in range(2):
                plain(u, w_nsa, 0, SLICE * n)
                u += 1
            for n in range(2):
                for half in range(2):
                    plain(u, w_mix, 4 * half, SLICE * n)
                    u += 1

            def gate_up(i, j):
                for half in range(2):
                    u, slot = U_GU + 2 * i + half, (2 * j + half) % RAW
                    unit(u, slot, [(raw[:, slot, :, GU_W * c:GU_W * c + GU_W],
                                    w[:, 4 * half:4 * half + 4, bass.ds(i * GU_W, GU_W)])
                                   for c, w in enumerate((w_gate, w_up))])

            gate_up(0, 0)
            with nc.sync.Fori(0, (GU_BLOCKS - 1) // 2) as it:
                for j in range(2):
                    gate_up(it * 2 + (1 + j), 1 - j)
            for j in range(2 * KF // 4):
                u = U_DOWN + j
                cut = []
                for c in (0, 2):
                    n, k = divmod(4 * j + c, KF)
                    cut.append((raw[:, u % RAW, c:c + 2, :], w_down[:, k:k + 2, SLICE * n:SLICE * n + SLICE]))
                unit(u, u % RAW, cut)
            for t in range(TILES):
                for n in range(2):
                    c = slice(SLICE * n, SLICE * n + SLICE)
                    sp.wait_ge(fin_done[n], t + 1)
                    sp.dma_start(outf[:, t, c], xs[:, t, c]).then_inc(out_d, 16)
            sp.wait_ge(out_d, 16 * 4)

        @block.gpsimd
        def _(pool):
            for i, name in enumerate(("pre_mix_g", "pre_ffn_g")):
                nc.gpsimd.dma_start(grows[KD * (i + 1):KD * (i + 2), :],
                        a[name][0].rearrange("(k p) -> k p", p=P)).then_inc(gaind[1], 16)
            nc.gpsimd.dma_start(rel[:], a["rel_bias"]).then_inc(reld, 16)
            for kv, name in enumerate(("cmp_pos_k", "cmp_pos_v")):
                for rep in range(2):
                    nc.gpsimd.dma_start(pos2[:, kv, rep, :], a[name][0]).then_inc(posd, 16)
            nc.gpsimd.memset(hidv[:], 0.0).then_inc(zeroed, 1)
            nc.gpsimd.memset(vcz[:], 0.0).then_inc(zeroed, 1)
            nc.gpsimd.memset(pcz[:], 0.0).then_inc(zeroed, 1)
            nc.gpsimd.memset(ckeys[:].bitcast(F32), 0.0).then_inc(zeroed, 1)
            pool.wait_ge(bp_d, 16)
            for kv, name in enumerate(("cmp_w1_k", "cmp_w1_v")):
                nc.gpsimd.dma_start(w1[:, kv], a[name][0].rearrange("(j p) n -> p j n", p=P)).then_inc(cmpd, 16)
            for rep in range(2):
                nc.gpsimd.dma_start(w2k[:, rep, :], a["cmp_w2_k"][0]).then_inc(cmpd, 16)
            nc.gpsimd.dma_start(w2v[:], a["cmp_w2_v"][0]).then_inc(cmpd, 16)
            for n, (kind, *_r) in enumerate(jobs):
                pool.wait_ge(r_done, n + 1)
                for t in range(TILES):
                    lo, hi = prob_cols(kind, t)
                    ins = nc.gpsimd.tensor_scalar(sx[:, n % 2, lo:hi], sx[:, n % 2, lo:hi], jst[:, 4, n, t:t + 1], 1.0,
                                                  ALU.mult, ALU.mult)
                ins.then_inc(p_done, 1)
            pool.wait_ge(pv_done, JOBS)
            nc.gpsimd.dma_start(xs[:], xf).then_inc(xsd, 16)
            nc.gpsimd.dma_start(gpost[:], bass.AP(a["post_mix_g"].tensor, 0, [[0, P], [1, D]])).then_inc(gpostd, 16)
            for n in range(2):
                for t in range(TILES):
                    pool.wait_ge(ev[t], B_MEM + n + 1)
                    c = slice(SLICE * n, SLICE * n + SLICE)
                    moba, mem = gates[:, t, D:2 * D], gates[:, t, 2 * D:3 * D]
                    nc.gpsimd.tensor_tensor(moba[:, c], moba[:, c], mem[:, c], ALU.add).then_inc(m_done, 1)

            def residual(t):
                y = yb[:, t, SLICE:D]
                pool.wait_ge(ev[t], B_MIX + 2)
                pool.wait_ge(rstd_done, 3 + t)
                nc.gpsimd.tensor_scalar(y, y, rstd[:, 2, t:t + 1], 1.0, ALU.mult, ALU.mult).then_inc(scaled, 1)
                pool.wait_ge(scaled, t + 1)
                nc.gpsimd.tensor_tensor(xs[:, t, SLICE:D], xs[:, t, SLICE:D], y, ALU.add).then_inc(x1_done[1], 1)

            pool.wait_ge(xsd, 16)
            for t in range(TILES):
                residual(t)
            nc.gpsimd.dma_start(gpost[:], bass.AP(a["post_ffn_g"].tensor, 0, [[0, P], [1, D]])).then_inc(gpostd, 16)

        @block.scalar
        def _(act):
            nc.scalar.dma_start(const0[:], a["const0"]).then_inc(constd, 16)
            nc.scalar.dma_start(grows[0:KD, :], a["mem_norm_g"][0].rearrange("(k p) -> k p", p=P)).then_inc(gaind[0], 16)
            nc.scalar.preload_act_table(ACT.Sqrt)

            split = [0]

            def hi(v, slot, half, w, first_load):
                if isinstance(v, int) and v == 0:
                    act.wait_ge(sub0d, 16)
                else:
                    act.wait_ge(loaded[slot], first_load)
                if not (isinstance(v, int) and v < SUBS):
                    act.wait_ge(mm_done, v - SUBS + 1)
                k = (2 * slot + half) % SUBS
                nc.scalar.activation(wh[:, k, :, 0:w], raw[:, slot, 2 * half:2 * half + 2, 0:w], ACT.Copy).then_inc(hi_done, 1)

            def hi_to(v_end):
                while split[0] <= min(v_end, 2 * UNITS - 1):
                    v = split[0]
                    u = v // 2
                    hi(v, u % RAW, v % 2, width(v), 32 * (u // RAW + 1))
                    split[0] += 1

            def wait_block(b, t, v_last):
                if t == 0:
                    act.wait_ge(acc0_done, b + 1)
                else:
                    act.wait_ge(mm_done, v_last + 1)

            def round_hi(r, j):
                act.wait_ge(tp_done, 4 * r + j + 1)
                bank = quad[j]
                dst = memh if r == 0 else xh
                if r == 3:
                    t, k0 = j // 2, 4 * (j % 2)
                    for kk in range(4):
                        g = 2 * KD + k0 + kk
                        ins = nc.scalar.activation(dst[:, k0 + kk, P * t:P * t + P], bank[:, P * kk:P * kk + P], ACT.Copy,
                                                   scale=gcol[:, g:g + 1])
                    ins.then_inc(th_done, 1)
                    return
                for kk in range(2):
                    k = 2 * j + kk
                    scale = 0.5 if r == 2 else gcol[:, KD * r + k:KD * r + k + 1]
                    ins = nc.scalar.activation(dst[:, k, :], bank[:, 256 * kk:256 * kk + 256], ACT.Copy, scale=scale)
                ins.then_inc(th_done, 1)

            hi_to(0)
            act.wait_ge(pre_dve, 2)
            for j in range(4):
                round_hi(0, j)
                hi_to(j)

            def roots(i, t0=0, t1=TILES):
                nc.scalar.activation(small[:, 2 * i + t0:2 * i + t1], ssq[:, i, t0:t1], ACT.Sqrt, bias=eps[:],
                                     scale=1.0 / D).then_inc(root_done, 1)

            act.wait_ge(pre_dve, 3)
            for j in range(4):
                round_hi(1, j)
            hi_to(4)
            act.wait_ge(ssq_done, 2)
            roots(0)
            hi_to(5)
            for t in range(TILES):
                nc.scalar.activation(junk[:, 2 + t], x0[:, t], ACT.Square, accum_out=ssq[:, 1, t:t + 1]).then_inc(ssq_done, 1)
            act.wait_ge(ssq_done, 4)
            roots(1)
            nc.scalar.preload_act_table(ACT.Tanh)

            def evac_cols(b):
                v_last = 4 * b + 3
                hi_to(v_last + (AHEAD if b < 5 else 1))
                act.wait_ge(rstd_done, 1 if b == 0 else 2)
                wait_block(b, 0, v_last)
                if b == 0:
                    dst, i, w = kvm[:, 0, :], 0, SLICE
                else:
                    w = ATT_TAIL if b == 5 else SLICE
                    dst, i = pat[:, 0, pat_col(SLICE * (b - 1)):pat_col(SLICE * (b - 1)) + w], 1
                src = acc[:, b % 2, 0, 0:w]
                if b == B_ATT:
                    dst, src = pair_queries(dst, src)
                nc.scalar.activation(dst, src, ACT.Copy, scale=rstd[:, i, 0:1]).then_inc(ev[0], 1)

            def high_qk(beta):
                act.wait_ge(qk_pe, beta + 1)
                bank = qk_bank(beta)
                for side in range(2):
                    heads, _pairs = stacked(beta, side)
                    if QK_BATCHES[beta][0] == "q":
                        ins = nc.scalar.activation(qst[half_rows(side), heads, :], bank[half_rows(side)], ACT.Copy)
                    else:
                        for dst_side in range(2):
                            ins = nc.scalar.activation(khh[half_rows(dst_side), heads, :], bank[half_rows(side)], ACT.Copy)
                ins.then_inc(qk_hi, 1)

            evac_cols(0)
            hi_to(7)
            for i in (0, 2, 4):
                if i:
                    hi_to(7 + i // 2)
                act.wait_ge(tb_pe, i + 1)
                nc.scalar.activation(tb[:, 2 * i:2 * i + 2, :], ptb[:], ACT.Copy).then_inc(tb_ev[0], 1)
            act.wait_ge(tb_pe, 7)
            evac_cols(1)
            hi_to(12)
            high_qk(0)
            hi_to(13)
            high_qk(1)
            evac_cols(2)
            high_qk(2)
            evac_cols(3)
            hi_to(20)
            high_qk(4)
            hi_to(21)
            act.wait_ge(cmp_dve, 1)
            nc.scalar.activation(hx[:, 2, :], hx[:, 1, :], ACT.Tanh, scale=0.7978845608028654).then_inc(cmp_act, 1)
            evac_cols(4)
            act.wait_ge(ev[0], B_ATT + 3)
            act.wait_ge(ev[1], B_ATT + 3)
            nc.scalar.activation(gsig[:], pat[:, :, pat_col(C_GN):pat_col(C_GN) + 3 * NSA_H], ACT.Tanh,
                    scale=0.5).then_inc(cmp_act, 1)
            high_qk(5)
            hi_to(24)
            high_qk(6)
            evac_cols(5)
            hi_to(V_GATE + AHEAD)
            act.wait_ge(cmp_dve, 4)
            nc.scalar.activation(xc[:, :, :, 0:NCMP], xc[:, :, :, 0:NCMP], ACT.Exp, scale=SCALE).then_inc(cmp_act, 1)

            def evac_gate(b, v_last):
                for t in range(TILES):
                    act.wait_ge(ev[t], b)
                    wait_block(b, t, v_last)
                    c = SLICE * (b - B_GATE) if b < B_MOBA else SLICE * (b - B_GATE_MEM + 4)
                    nc.scalar.activation(gates[:, t, c:c + SLICE], acc[:, b % 2, t], ACT.Tanh,
                                         scale=rstd[:, 4, t:t + 1]).then_inc(ev[t], 1)

            def evac_pt(n):
                act.wait_ge(t_done, t_count(n))
                if n >= 2:
                    act.wait_ge(pv_done, n - 1)
                w = 512 if jobs[n][0] == "mem" else 384
                nc.scalar.activation(pts[:, n % 2, 0:w], ptb[:, 0:w], ACT.Copy).then_inc(te_done, 1)

            def evac_o(n):
                if ends_pair(n):
                    act.wait_ge(pv_done, n + 1)
                    nc.scalar.activation(oh[:, pair_of(n), :], ob[:, 0:256], ACT.Copy).then_inc(oh_done, 1)

            for n in range(JOBS + 2):
                hi_to(V_GATE + n + AHEAD)
                if n == CMP_SLOT:
                    act.wait_ge(t_done, CMP_SLOT)
                    nc.scalar.activation(pct[:], ptb[:], ACT.Copy).then_inc(te_done, 1)
                if n < JOBS:
                    kind = jobs[n][0]
                    act.wait_ge(x_done, n + 1)
                    src = sbank if kind == "mem" else sx
                    if n >= 2:
                        act.wait_ge(t_done, t_count(n - 2))
                    for t in range(TILES):
                        lo, hic = prob_cols(kind, t)
                        ins = nc.scalar.activation(sx[:, n % 2, lo:hic], src[:, n % 2, lo:hic], ACT.Exp,
                                                   bias=jst[:, 1, n, t:t + 1], scale=SCALE,
                                                   accum_out=jst[:, 2, n, t:t + 1])
                    ins.then_inc(e_done, 1)
                if n == 0:
                    high_qk(QK_LAST)
                if 1 <= n <= JOBS:
                    evac_pt(n - 1)
                if n >= 2:
                    evac_o(n - 2)
                if n < 16 and n % 4 == 3:
                    evac_gate(B_GATE + n // 4, V_GATE + n)
                if n in (21, 25):
                    evac_gate(B_GATE_MEM + (n - 21) // 4, V_GATE + n)

            hi_to(V_NSA + 2 + AHEAD)
            for j in range(2):
                round_hi(2, j)
            hi_to(V_MIX + AHEAD)
            for j in range(2, 4):
                round_hi(2, j)
            nc.scalar.preload_act_table(ACT.Sqrt)

            def squares(i, n, t, b, v_last):
                wait_block(b, t, v_last)
                if n:
                    act.wait_ge(sq_done, 4 * i + 2)
                nc.scalar.activation(tmp[:, t], acc[:, b % 2, t], ACT.Square,
                        accum_out=part[:, i, n, t:t + 1]).then_inc(sq_done, 1)

            hi_to(V_MIX + 3 + AHEAD)
            for t in range(TILES):
                squares(0, 0, t, B_MIX, V_MIX + 3)
            hi_to(V_MIX + 7)
            squares(0, 1, 0, B_MIX + 1, V_MIX + 7)
            act.wait_ge(sum_done, 1)
            roots(2, 0, 1)
            hi_to(V_GU + 1)
            round_hi(3, 0)
            round_hi(3, 1)
            squares(0, 1, 1, B_MIX + 1, V_MIX + 7)
            hi_to(V_GU + 2)
            act.wait_ge(sum_done, 2)
            roots(2, 1, 2)
            hi_to(V_GU + 3)
            for j in (2, 3):
                round_hi(3, j)
            hi_to(V_GU + AHEAD + 3)
            for n in range(2):
                act.wait_ge(x1_done[n], 2)
            for t in range(TILES):
                nc.scalar.activation(yb[:, t], xs[:, t], ACT.Square, accum_out=ssq[:, 3, t:t + 1]).then_inc(ssq_done, 1)
            act.wait_ge(ssq_done, 6)
            roots(3)

            nc.scalar.preload_act_table(ACT.Silu)

            def ffn_hi(i, j, s):
                v = V_GU + AHEAD + s + 4 * i
                vj = AHEAD + s + 4 * j
                hi(v, (vj // 2) % RAW, vj % 2, SLICE, ((V_GU + vj) // 2 // RAW + 1) * 32 + (i - j) * 16)

            def ffn_ah(i):
                act.wait_ge(at_done, i + 1)
                nc.scalar.activation(ah[:, bass.ds(i * 2, 2), :], ptb[:], ACT.Copy).then_inc(ah_done, 1)

            def ffn_act(i, j, first):
                for s in range(4):
                    if not first:
                        ffn_hi(i, j, s)
                    if s == 2 and not first:
                        ffn_ah(i - 1)
                for t in range(TILES):
                    if t == 0:
                        act.wait_ge(acc0_done, i + (B_GU + 1))
                    else:
                        act.wait_ge(mm_done, i * 4 + (V_GU + 4))
                    if not first:
                        act.wait_ge(prod_done, i * 2 + (t - 1))
                    nc.scalar.activation(silu[:, t], acc[:, j % 2, t, 0:GU_W], ACT.Silu,
                            scale=rstd[:, 3, t:t + 1]).then_inc(silu_done, 1)

            act.wait_ge(rstd_done, 5)
            ffn_act(0, 0, True)
            with nc.scalar.Fori(0, (GU_BLOCKS - 1) // 2) as it:
                for j in range(2):
                    ffn_act(it * 2 + (1 + j), 1 - j, False)
            split[0] = V_GU + 4 * GU_BLOCKS + AHEAD
            hi_to(V_DOWN + 2 + AHEAD)
            ffn_ah(GU_BLOCKS - 1)
            nc.scalar.preload_act_table(ACT.Sqrt)
            for n in range(2):
                v_last = V_DOWN + 11 * n + 10
                hi_to(v_last + AHEAD)
                for t in range(TILES):
                    squares(1, n, t, B_DOWN + n, v_last)
                    if n:
                        act.wait_ge(sum_done, 3 + t)
                        roots(4, t, t + 1)

        @block.vector
        def _(dve):
            split = [0]

            def lo(v, slot, half, w):
                dve.wait_ge(hi_done, v + 1)
                k = (2 * slot + half) % SUBS
                nc.vector.tensor_tensor(wl[:, k, :, 0:w], raw[:, slot, 2 * half:2 * half + 2, 0:w],
                                        wh[:, k, :, 0:w].bitcast(F32), ALU.subtract).then_inc(lo_done, 1)

            def lo_to(v_end):
                while split[0] <= min(v_end, 2 * UNITS - 1):
                    v = split[0]
                    lo(v, v // 2 % RAW, v % 2, width(v))
                    split[0] += 1

            chain = [0]

            def link(ins):
                chain[0] += 1
                ins.then_inc(dve_c, 1)
                dve.wait_ge(dve_c, chain[0])

            def wait_block(b, t, v_last):
                if t == 0:
                    dve.wait_ge(acc0_done, b + 1)
                else:
                    dve.wait_ge(mm_done, v_last + 1)

            def round_lo(r, j):
                dve.wait_ge(th_done, 4 * r + j + 1)
                bank = quad[j]
                h, l = (memh, meml) if r == 0 else (xh, xl)
                if r == 3:
                    t, k0 = j // 2, 4 * (j % 2)
                    for kk in range(4):
                        k = k0 + kk
                        ins = nc.vector.scalar_tensor_tensor(l[:, k, P * t:P * t + P], bank[:, P * kk:P * kk + P],
                                                             gcol[:, 2 * KD + k:2 * KD + k + 1],
                                                             h[:, k, P * t:P * t + P].bitcast(F32), ALU.mult, ALU.subtract)
                    ins.then_inc(tl_done, 1)
                    return
                for kk in range(2):
                    k = 2 * j + kk
                    scale = 0.5 if r == 2 else gcol[:, KD * r + k:KD * r + k + 1]
                    ins = nc.vector.scalar_tensor_tensor(l[:, k, :], bank[:, 256 * kk:256 * kk + 256], scale,
                                                         h[:, k, :].bitcast(F32), ALU.mult, ALU.subtract)
                ins.then_inc(tl_done, 1)

            nc.vector.memset(eps[:], EPS).then_inc(pre_dve, 1)
            dve.wait_ge(pre_pe, 1)
            nc.vector.tensor_copy(gcol[:, 0:KD], acc[:, 1, 1, 0:KD]).then_inc(pre_dve, 1)

            def reciprocals(i, slot):
                nc.vector.reciprocal(rstd[:, slot, :], small[:, 2 * i:2 * i + 2]).then_inc(rstd_done, 1)

            lo_to(0)
            for j in range(4):
                round_lo(0, j)
                lo_to(j)
                if j == 2:
                    dve.wait_ge(pre_pe, 2)
                    nc.vector.tensor_copy(gcol[:, KD:3 * KD], acc[:, 1, 1, P + KD:P + 3 * KD]).then_inc(pre_dve, 1)
                    dve.wait_ge(pre_pe, 3)
                    nc.vector.tensor_scalar(grow[:, 0:256], acc[0:BIAS_H, 1, 0, 0:256], 1.0 / SCALE, None,
                                            ALU.mult).then_inc(grow_done, 1)
                    nc.vector.memset(grow[:, 256:G_W], MASKED / SCALE).then_inc(grow_done, 1)
            dve.wait_ge(memd[0], 16)
            dve.wait_ge(memd[1], 16)
            for t in range(TILES):
                round_lo(1, t)
                nc.vector.tensor_tensor_reduce(out=junk[:, t], in0=mems[:, t], in1=mems[:, t], scale=1.0, scalar=0.0, op0=ALU.mult,
                                               op1=ALU.add, accum_out=ssq[:, 0, t:t + 1]).then_inc(ssq_done, 1)
            lo_to(4)
            for j in (2, 3):
                round_lo(1, j)
            dve.wait_ge(root_done, 1)
            reciprocals(0, 0)
            lo_to(5)
            dve.wait_ge(rstd_done, 1)

            def evac_cols(b):
                v_last = 4 * b + 3
                lo_to(v_last + (AHEAD if b < 5 else 1))
                wait_block(b, 1, v_last)
                if b == 0:
                    dst, i, w = kvm[:, 1, :], 0, SLICE
                else:
                    w = ATT_TAIL if b == 5 else SLICE
                    dst, i = pat[:, 1, pat_col(SLICE * (b - 1)):pat_col(SLICE * (b - 1)) + w], 1
                src = acc[:, b % 2, 1, 0:w]
                if b == B_ATT:
                    dst, src = pair_queries(dst, src)
                nc.vector.tensor_scalar(dst, src, rstd[:, i, 1:2], None, ALU.mult).then_inc(ev[1], 1)

            def low_qk(beta):
                bank = qk_bank(beta)
                if beta == QK_COMPRESS:
                    dve.wait_ge(qk_pe, beta + 1)
                    nc.vector.tensor_copy(kvc[:], bank).then_inc(qk_ev[1], 1)
                    return
                dve.wait_ge(qk_hi, beta + 1 if beta < QK_COMPRESS else beta)
                for side in range(2):
                    rows = half_rows(side)
                    heads, pairs = stacked(beta, side)
                    if QK_BATCHES[beta][0] == "q":
                        high, dst = qst[rows, heads, :], qst[half_rows(1 - side), heads, :]
                    else:
                        high, dst = khh[rows, heads, :], klo[rows, pairs, :]
                    ins = nc.vector.tensor_tensor(dst, bank[rows], high.bitcast(F32), ALU.subtract)
                ins.then_inc(qk_ev[beta % 2], 1)

            evac_cols(0)
            dve.wait_ge(root_done, 2)
            reciprocals(1, 1)
            dve.wait_ge(rstd_done, 2)
            link(nc.vector.tensor_scalar(rstd[:, 4, :], rstd[:, 1, :], 0.5, None, ALU.mult))
            dve.wait_ge(pre_pe, 4)
            nc.vector.tensor_copy(post[:], ptb[:, 0:2 * CMP_LEN].rearrange("p (a j) -> p a j", a=2)).then_inc(pre_dve, 1)
            lo_to(7)
            for i in (1, 3, 5):
                if i > 1:
                    lo_to(7 + i // 2)
                dve.wait_ge(tb_pe, i + 1)
                nc.vector.tensor_copy(tb[:, 2 * i:2 * i + 2, :], ob[:].rearrange("p (a n) -> p a n", a=2)).then_inc(tb_ev[1], 1)
            dve.wait_ge(tb_pe, 7)
            nc.vector.tensor_copy(tbc[:, :, :, 0:NCMP],
                    sbank[:, 0, 0:256].rearrange("p (t h c) -> p t h c", t=2, h=NSA_H)[:, :, :, 0:NCMP]).then_inc(tb_ev[1], 1)
            evac_cols(1)
            lo_to(12)
            low_qk(0)
            lo_to(13)
            low_qk(1)
            evac_cols(2)
            low_qk(2)
            lo_to(16)
            low_qk(3)
            dve.wait_ge(qk_ev[1], 2)
            for kv in range(2):
                for g in range(GROUPS):
                    for jj in range(2):
                        src = kvc[HD * g:HD * g + HD, kv, jj:jj + 1]
                        pos = post[HD * g:HD * g + HD, kv, jj:jj + 1]
                        ins = nc.vector.tensor_tensor(
                            gcmp[HD * jj:HD * jj + HD, kv, :, NCMP * g:NCMP * g + NCMP],
                            bass.AP(src.tensor, src.offset, [src.ap[0], [2, PAIRS], [CMP_STRIDE, NCMP]]),
                            bass.AP(pos.tensor, pos.offset, [pos.ap[0], [2, PAIRS], [0, NCMP]]), ALU.add)
            ins.then_inc(cmp_g, 1)
            evac_cols(3)
            lo_to(20)
            low_qk(4)
            lo_to(21)
            dve.wait_ge(cmp_pe, 1)
            link(nc.vector.tensor_copy(hx[:, 0, :], ob[:, 0:4 * NCMP]))
            link(nc.vector.tensor_tensor(hx[:, 1, :], hx[:, 0, :], hx[:, 0, :], ALU.mult))
            link(nc.vector.tensor_scalar(hx[:, 1, :], hx[:, 1, :], 0.044715, 1.0, ALU.mult, ALU.add))
            nc.vector.tensor_tensor(hx[:, 1, :], hx[:, 1, :], hx[:, 0, :], ALU.mult).then_inc(cmp_dve, 1)
            dve.wait_ge(cmp_act, 1)
            link(nc.vector.scalar_tensor_tensor(hx[:, 2, :], hx[:, 2, :], 1.0, hx[:, 0, :], ALU.add, ALU.mult))
            nc.vector.tensor_scalar(hidk[:], hx[:, 2, 0:2 * NCMP], 0.5, None, ALU.mult)
            dve.wait_ge(zeroed, 4)
            for i in range(HPG):
                ins = nc.vector.tensor_scalar(hidv[:, :, i, 0:NCMP],
                                              hx[:, 2, 2 * NCMP:4 * NCMP].rearrange("p (g c) -> p g c", g=GROUPS),
                                              0.5, None, ALU.mult)
            ins.then_inc(cmp_dve, 1)
            evac_cols(4)
            dve.wait_ge(cmp_pe, 2)
            for g in range(GROUPS):
                keys = ob[half_rows(g), 64 + NCMP * g:64 + NCMP * g + NCMP]
                nc.vector.tensor_copy(ckeys[half_rows(1 - g), g, 0, 0:NCMP], keys)
                link(nc.vector.tensor_copy(ckeys[half_rows(g), g, 0, 0:NCMP], keys))
                nc.vector.tensor_tensor(ckeys[half_rows(g), g, 1, 0:NCMP], keys, ckeys[half_rows(g), g, 0, 0:NCMP].bitcast(F32),
                                        ALU.subtract)
            for i in range(HPG):
                ins = nc.vector.tensor_copy(vcz[32 * i:32 * i + 32, :, i, :],
                                            ob[32 * i:32 * i + 32, 128:256].rearrange("p (g d) -> p g d", g=GROUPS))
            ins.then_inc(cmp_dve, 1)
            dve.wait_ge(cmp_act, 2)
            link(nc.vector.tensor_scalar(gsig[:], gsig[:], 0.5, 0.5, ALU.mult, ALU.add))
            gview = gsig[:].rearrange("p t (h b) -> p t h b", b=3)
            low_qk(5)
            lo_to(24)
            low_qk(6)
            evac_cols(5)
            lo_to(V_GATE + 1)
            x16 = xc[:].rearrange("p t h c -> p (t h) c")[:, :, 0:NCMP]
            dve.wait_ge(cmp_pe, 3)
            for half, other in ((1, tbc), (0, xc)):
                for g, bank in enumerate((ob, ptb)):
                    hs = slice(HPG * g, HPG * g + HPG)
                    products = bank[:, 0:2 * P].rearrange("p (t h a c) -> p a t h c", t=2, h=HPG, a=2)
                    ins = nc.vector.tensor_tensor(xc[:, :, hs, 0:NCMP], products[:, half, :, :, 0:NCMP],
                                                  other[:, :, hs, 0:NCMP], ALU.add)
                link(ins)
            link(nc.vector.tensor_reduce(cst[:, 0, :], x16, AX, ALU.max))
            m16 = cst[:, 0, :]
            nc.vector.tensor_tensor(x16, x16, bass.AP(m16.tensor, m16.offset, [m16.ap[0], [1, 16], [0, NCMP]]),
                    ALU.subtract).then_inc(cmp_dve, 1)

            def merge(b):
                c = SLICE * (b % 2)
                branch = {B_MOBA: 1, B_MEM: 2, B_NSA: 0}[b - b % 2]
                v_last = {B_MOBA: V_MOBA, B_MEM: V_MEM}[b - b % 2] + b % 2 if b < B_NSA else V_NSA + 2 * (b - B_NSA) + 1
                lo_to(v_last + AHEAD)
                for t in range(TILES):
                    if b >= B_MEM:
                        dve.wait_ge(ev[t], b)
                    wait_block(b, t, v_last)
                    g = gates[:, t, D * branch + c:D * branch + c + SLICE]
                    nc.vector.scalar_tensor_tensor(g, g, 1.0, acc[:, b % 2, t], ALU.add, ALU.mult).then_inc(ev[t], 1)
                    if b >= B_NSA:
                        dve.wait_ge(ev[t], b + 1)
                        dve.wait_ge(m_done, 2 * (b - B_NSA) + t + 1)
                        nc.vector.tensor_tensor(yb[:, t, c:c + SLICE], g, gates[:, t, D + c:D + c + SLICE],
                                ALU.add).then_inc(y_done, 1)

            for n in range(JOBS + 2):
                if n < JOBS:
                    kind, h, _qb, _qh, _kb, bh = jobs[n]
                    dve.wait_ge(s_done, n + 1)
                    if kind == "mem":
                        link(nc.vector.tensor_reduce(jst[:, 0, n, :], sbank[:, n % 2].rearrange("p (t k) -> p t k", t=2), AX, ALU.max))
                    else:
                        if n >= 2:
                            dve.wait_ge(t_done, t_count(n - 2))
                        for t in range(TILES):
                            c0, c1 = prob_cols(kind, t)
                            nc.vector.tensor_tensor(sx[:, n % 2, c0:c1], sbank[:, n % 2, c0:c1], tb[:, bh, 128 * (1 - t):256],
                                    ALU.add).then_inc(dve_c, 1)
                            chain[0] += 1
                        dve.wait_ge(dve_c, chain[0] - 1)
                        for t in range(TILES):
                            c0, c1 = prob_cols(kind, t)
                            if t == 1:
                                dve.wait_ge(dve_c, chain[0])
                            ins = nc.vector.reduce_max(jst[:, 0, n, t:t + 1], sx[:, n % 2, c0:c1], axis=AX)
                        link(ins)
                    nc.vector.tensor_scalar(jst[:, 1, n, :], jst[:, 0, n, :], -SCALE, None, ALU.mult).then_inc(x_done, 1)
                if n in (17, 18):
                    merge(B_MOBA + n - 17)
                if n == 1:
                    low_qk(QK_LAST)
                lo_to(V_GATE + n + look_ahead(n))
                if n < JOBS:
                    dve.wait_ge(e_done, n + 1)
                    if kind in ("sel", "win"):
                        link(nc.vector.reciprocal(jst[:, 3, n, :], jst[:, 2, n, :]))
                        nc.vector.tensor_tensor(jst[:, 4, n, :], jst[:, 3, n, :], gview[:, :, h, 1 if kind == "sel" else 2],
                                ALU.mult).then_inc(r_done, 1)
                    else:
                        nc.vector.reciprocal(jst[:, 4, n, :], jst[:, 2, n, :]).then_inc(r_done, 1)
                if n == CMP_SLOT - 2:
                    dve.wait_ge(cmp_act, 3)
                    link(nc.vector.tensor_reduce(cst[:, 1, :], x16, AX, ALU.add))
                    link(nc.vector.reciprocal(cst[:, 2, :], cst[:, 1, :]))
                    link(nc.vector.tensor_tensor(cst[:, 3, :].rearrange("p (t h) -> p t h", t=2), cst[:, 2, :].rearrange("p (t h) -> p t h", t=2), gview[:, :, :, 0], ALU.mult))
                    for t in range(TILES):
                        f8 = cst[:, 3, NSA_H * t:NSA_H * t + NSA_H]
                        ins = nc.vector.scalar_tensor_tensor(
                            pcz[:, t].rearrange("p g i c -> p (g i) c")[:, :, 0:NCMP], xc[:, t, :, 0:NCMP], row_any[:, t:t + 1],
                            bass.AP(f8.tensor, f8.offset, [f8.ap[0], [1, NSA_H], [0, NCMP]]), ALU.mult, ALU.mult)
                    ins.then_inc(cmp_dve, 1)
                if n >= 2 and ends_pair(n - 2):
                    p = pair_of(n - 2)
                    dve.wait_ge(oh_done, p + 1)
                    nc.vector.tensor_tensor(ol[:, p, :], ob[:, 0:256], oh[:, p, :].bitcast(F32),
                            ALU.subtract).then_inc(ol_done, 1)

            merge(B_MEM)
            merge(B_MEM + 1)
            merge(B_NSA)
            lo_to(V_NSA + 2 + AHEAD)
            for j in range(2):
                round_lo(2, j)
            merge(B_NSA + 1)
            lo_to(V_MIX + AHEAD)
            for j in range(2, 4):
                round_lo(2, j)

            def gain(i, n, t, b0):
                dve.wait_ge(sq_done, 4 * i + 2 * n + t + 1)
                nc.vector.tensor_tensor(yb[:, t, SLICE * n:SLICE * n + SLICE], acc[:, (b0 + n) % 2, t],
                                        gpost[:, SLICE * n:SLICE * n + SLICE], ALU.mult).then_inc(ev[t], 1)

            def sum_halves(i, t):
                dve.wait_ge(sq_done, 4 * i + 2 + t + 1)
                nc.vector.tensor_tensor(ssq[:, 2 * i + 2, t:t + 1], part[:, i, 0, t:t + 1], part[:, i, 1, t:t + 1],
                                        ALU.add).then_inc(sum_done, 1)

            def finish(i, t, root_count, slot, signal):
                dve.wait_ge(root_done, root_count)
                c = 2 * (2 * i + 2) + t
                nc.vector.reciprocal(rstd[:, slot, t:t + 1], small[:, c:c + 1]).then_inc(rstd_done, 1)
                dve.wait_ge(rstd_done, root_count)
                for n in range(1 + i):
                    cols = slice(SLICE * n, SLICE * n + SLICE)
                    dve.wait_ge(ev[t], B_MIX + 1 + 2 * i + n)
                    nc.vector.scalar_tensor_tensor(xs[:, t, cols], yb[:, t, cols], rstd[:, slot, t:t + 1], xs[:, t, cols],
                                                   ALU.mult, ALU.add).then_inc(signal[n], 1)

            dve.wait_ge(gpostd, 16)
            dve.wait_ge(xsd, 16)
            lo_to(V_MIX + 3 + AHEAD)
            for t in range(TILES):
                gain(0, 0, t, B_MIX)
            lo_to(V_MIX + 7)
            sum_halves(0, 0)
            gain(0, 1, 0, B_MIX)
            finish(0, 0, 3, 2, x1_done)
            lo_to(V_GU + 1)
            round_lo(3, 0)
            round_lo(3, 1)
            sum_halves(0, 1)
            gain(0, 1, 1, B_MIX)
            lo_to(V_GU + 2)
            finish(0, 1, 4, 2, x1_done)
            lo_to(V_GU + 3)
            for j in (2, 3):
                round_lo(3, j)
            lo_to(V_GU + AHEAD + 3)
            dve.wait_ge(root_done, 5)
            reciprocals(3, 3)
            dve.wait_ge(rstd_done, 5)

            def ffn_lo(i, j, s):
                vj = AHEAD + s + 4 * j
                lo(V_GU + AHEAD + s + 4 * i, (vj // 2) % RAW, vj % 2, SLICE)

            def ffn_al(i):
                dve.wait_ge(ah_done, i + 1)
                nc.vector.tensor_tensor(al[:, bass.ds(i * 2, 2), :], ptb[:].rearrange("p (k n) -> p k n", k=2),
                                        ah[:, bass.ds(i * 2, 2), :].bitcast(F32), ALU.subtract).then_inc(al_done, 1)

            def ffn_dve(i, j, first):
                for s in range(4):
                    if not first:
                        ffn_lo(i, j, s)
                    if s == 2 and not first:
                        ffn_al(i - 1)
                for t in range(TILES):
                    dve.wait_ge(silu_done, i * 2 + (t + 1))
                    if not first:
                        dve.wait_ge(at_done, i)
                    nc.vector.scalar_tensor_tensor(act_tok[:, t], acc[:, j % 2, t, GU_W:2 * GU_W], rstd[:, 3, t:t + 1],
                                                   silu[:, t], ALU.mult, ALU.mult).then_inc(prod_done, 1)

            ffn_dve(0, 0, True)
            with nc.vector.Fori(0, (GU_BLOCKS - 1) // 2) as it:
                for j in range(2):
                    ffn_dve(it * 2 + (1 + j), 1 - j, False)
            split[0] = V_GU + 4 * GU_BLOCKS + AHEAD
            lo_to(V_DOWN + 2 + AHEAD)
            ffn_al(GU_BLOCKS - 1)
            dve.wait_ge(gpostd, 32)
            lo_to(V_DOWN + 10 + AHEAD)
            for t in range(TILES):
                gain(1, 0, t, B_DOWN)
            lo_to(V_DOWN + 21)
            for t in range(TILES):
                sum_halves(1, t)
                gain(1, 1, t, B_DOWN)
                finish(1, t, 6 + t, 5, fin_done)

        @block.tensor
        def _(pe):
            def product(bank, h, l, k, t, slot, s, w, first, last):
                c = slice(P * t, P * t + P)
                nc.tensor.matmul(bank[:, 0:w], h[:, k, c], wh[:, slot, s, 0:w], start=first, stop=False)
                nc.tensor.matmul(bank[:, 0:w], h[:, k, c], wl[:, slot, s, 0:w], start=False, stop=False)
                return nc.tensor.matmul(bank[:, 0:w], l[:, k, c], wh[:, slot, s, 0:w], start=False, stop=last)

            def sub(v, slot, parity, h, l, k0, w, first, last):
                pe.wait_ge(lo_done, v + 1)
                for t in range(TILES):
                    for s in range(2):
                        ins = product(acc[:, parity, t], h, l, k0 + s, t, slot, s, w,
                                      first and s == 0, last and s == 1)
                    if t == 0 and last:
                        ins.then_inc(acc0_done, 1)
                ins.then_inc(mm_done, 1)

            def free_acc(b):
                if b < 2:
                    return
                for t in range(TILES):
                    pe.wait_ge(ev[t], b - 1)

            def whole_block(b, v0, subs, h, l, k0=0, w=SLICE, ready=None, after=None):
                free_acc(b)
                for i in range(subs):
                    if ready is not None:
                        pe.wait_ge(tl_done, 4 * ready + i + 1)
                    sub(v0 + i, (v0 + i) % SUBS, b % 2, h, l, k0 + 2 * i, w, i == 0, i == subs - 1)
                    for work in (after or {}).get(i, ()):
                        work()

            def by_tiles(b, v0, subs, h, l, k0, ready=None, after=None, first=True):
                for t in range(TILES):
                    for i in range(subs):
                        v = v0 + i
                        if t == 0:
                            pe.wait_ge(lo_done, v + 1)
                        if ready is not None and i % 2 == 0:
                            pe.wait_ge(tl_done, ready + 2 * t + i // 2 + 1)
                        for s in range(2):
                            ins = product(acc[:, b % 2, t], h, l, k0 + 2 * i + s, t, v % SUBS, s, SLICE,
                                          first and i == 0 and s == 0, i == subs - 1 and s == 1)
                        if t == 1:
                            ins.then_inc(mm_done, 1)
                        elif i == subs - 1:
                            ins.then_inc(acc0_done, 1)
                        for work in (after or {}).get((t, i), ()):
                            work()

            def transpose_bank(r, j, src):
                bank = quad[j]
                if r == 3:
                    t, k0 = j // 2, 4 * (j % 2)
                    for kk in range(4):
                        ins = nc.tensor.transpose(bank[:, P * kk:P * kk + P], src[:, t, P * (k0 + kk):P * (k0 + kk) + P], ident)
                    ins.then_inc(tp_done, 1)
                    return
                for kk in range(2):
                    for t in range(TILES):
                        ins = nc.tensor.transpose(bank[:, 256 * kk + P * t:256 * kk + P * t + P],
                                                  src[:, t, P * (2 * j + kk):P * (2 * j + kk) + P], ident)
                ins.then_inc(tp_done, 1)

            pe.wait_ge(constd, 16)
            pe.wait_ge(memd[0], 16)
            transpose_bank(0, 0, mems)
            transpose_bank(0, 1, mems)
            pe.wait_ge(gaind[0], 16)
            nc.tensor.transpose(acc[:, 1, 1, 0:KD], grows[0:KD, :], ident[0:KD, 0:KD]).then_inc(pre_pe, 1)
            pe.wait_ge(memd[1], 16)
            transpose_bank(0, 2, mems)
            transpose_bank(0, 3, mems)

            def gains_and_bias_row():
                pe.wait_ge(gaind[1], 2 * 16)
                pe.wait_ge(pre_dve, 2)
                nc.tensor.transpose(acc[:, 1, 1, P:P + 3 * KD], grows[:], ident[0:3 * KD, 0:3 * KD]).then_inc(pre_pe, 1)
                pe.wait_ge(reld, 16)
                pe.wait_ge(const1d, 16)
                nc.tensor.matmul(acc[0:BIAS_H, 1, 0, :], rel[:], onehot, start=True, stop=True).then_inc(pre_pe, 1)

            def positions():
                pe.wait_ge(posd, 4 * 16)
                pe.wait_ge(tl_done, 7)
                for kv in range(2):
                    ins = nc.tensor.transpose(ptb[:, CMP_LEN * kv:CMP_LEN * kv + CMP_LEN],
                                              pos2[:, kv].rearrange("j r d -> j (r d)"), ident[0:CMP_LEN, 0:CMP_LEN])
                ins.then_inc(pre_pe, 1)

            def round_x():
                pe.wait_ge(xd, 16)
                for j in range(4):
                    pe.wait_ge(tl_done, j + 1)
                    transpose_bank(1, j, x0)

            def bias_tables(i):
                if i == 0:
                    pe.wait_ge(bp_d, 16)
                    pe.wait_ge(tl_done, 8)
                    pe.wait_ge(pre_dve, 4)
                for i in (2 * i, 2 * i + 1):
                    if i >= 2:
                        pe.wait_ge(tb_ev[i % 2], i // 2)
                    dst = (ptb, ob)[i % 2]
                    nc.tensor.matmul(dst[:].rearrange("p (a n) -> p a n", a=2), flip, bp[:, 2 * i:2 * i + 2, 0:256],
                                     start=True, stop=True).then_inc(tb_pe, 1)

            def compressed_bias():
                for t in range(TILES):
                    off = 31 + P * (1 - t)
                    src = bp[:, 0:NSA_H, off:off + 1]
                    ins = nc.tensor.matmul(sbank[:, 0, P * t:P * t + P].rearrange("p (h c) -> p h c", h=NSA_H)[:, :, 0:NCMP], flip,
                                           bass.AP(src.tensor, src.offset, [src.ap[0], [BP_W, NSA_H], [CMP_STRIDE, NCMP]]),
                                           start=True, stop=True)
                ins.then_inc(tb_pe, 1)

            whole_block(B_MEMKV, 0, 4, memh, meml, ready=0,
                        after={0: [gains_and_bias_row], 1: [round_x]})
            pe.wait_ge(pre_dve, 3)
            pe.wait_ge(grow_done, 1)

            def qk_batch(beta, blocks_ready, sources):
                for t in range(TILES):
                    pe.wait_ge(ev[t], blocks_ready)
                if beta >= 2:
                    pe.wait_ge(qk_ev[beta % 2], beta // 2)
                if beta == 0:
                    pe.wait_ge(tb_ev[1], 4)
                if beta == QK_LAST:
                    pe.wait_ge(cmp_dve, 4)
                for i, src in enumerate(sources):
                    for t in range(TILES):
                        ins = nc.tensor.transpose(qk_bank(beta)[:, i, P * t:P * t + P], src(t), ident)
                ins.then_inc(qk_pe, 1)

            def col(c):
                c = pat_col(c)
                return lambda t: pat[:, t, c:c + P]

            def compress_1(part):
                if part == 0:
                    pe.wait_ge(cmp_g, 1)
                    pe.wait_ge(cmpd, 5 * 16)
                steps = [(kv, j) for kv in range(2) for j in range(PAIRS)]
                for kv, j in steps[11 * part:11 * part + 11]:
                    ins = nc.tensor.matmul(ob[:, 2 * NCMP * kv:2 * NCMP * (kv + 1)], w1[:, kv, j, :], gcmp[:, kv, j, :],
                                           start=(j == 0), stop=(j == PAIRS - 1))
                if part == 2:
                    ins.then_inc(cmp_pe, 1)

            def compress_2():
                pe.wait_ge(cmp_dve, 2)
                nc.tensor.matmul(ob[:, 64:64 + 2 * NCMP], w2k[:].rearrange("p r d -> p (r d)"), hidk[:], start=True, stop=True)
                for g in range(GROUPS):
                    ins = nc.tensor.matmul(ob[:, 128 + HD * g:128 + HD * g + HD], hidv[:, g].rearrange("p i c -> p (i c)"), w2v[:],
                                           start=True, stop=True)
                ins.then_inc(cmp_pe, 1)

            def logits(dst, q, side, t, high, low):
                cols = slice(P * t, P * t + P)
                nc.tensor.matmul(dst, qst[:, q, cols], high, start=True, stop=False)
                return nc.tensor.matmul(dst, qst[half_rows(side), q, cols], low, start=False, stop=True)

            def compressed_scores(g):
                pe.wait_ge(cmp_dve, 3)
                for h in range(HPG * g, HPG * g + HPG):
                    for t in range(TILES):
                        c = 32 * (HPG * t + h % HPG)
                        ins = nc.tensor.matmul((ob, ptb)[g][:, c:c + 32], qst[:, Q_NSA + h, P * t:P * t + P],
                                               ckeys[:, g].rearrange("p a c -> p (a c)"), start=True, stop=True)
                ins.then_inc(cmp_pe, 1)

            whole_block(1, 4, 4, xh, xl, ready=1,
                        after={0: [positions], 2: [lambda: bias_tables(0)], 3: [lambda: bias_tables(1)]})
            whole_block(2, 8, 4, xh, xl,
                        after={0: [lambda: bias_tables(2), compressed_bias],
                               1: [lambda: qk_batch(0, 1, [lambda t: kvm[:, t, 0:P], lambda t: kvm[:, t, P:2 * P]])],
                               2: [lambda: qk_batch(1, 2, [col(C_Q), col(C_Q + P)])],
                               3: [lambda: qk_batch(2, 2, [col(C_Q + 2 * P), col(C_Q + 3 * P)])]})
            whole_block(3, 12, 4, xh, xl, after={1: [lambda: qk_batch(3, 3, [col(C_KC), col(C_VC)])]})
            whole_block(4, 16, 4, xh, xl, after={0: [lambda: compress_1(0)],
                                                 1: [lambda: compress_1(1), lambda: qk_batch(4, 4, [col(C_KS), col(C_KW)])],
                                                 2: [lambda: compress_1(2)], 3: [compress_2]})
            whole_block(5, 20, 4, xh, xl, w=ATT_TAIL,
                        after={1: [lambda: qk_batch(5, 5, [col(C_QM), col(C_QM + P)]),
                                   lambda: qk_batch(6, 5, [col(C_KM), col(C_KM + P)])],
                               2: [lambda: compressed_scores(0), lambda: compressed_scores(1)]})

            def scores(n):
                kind, h, q, side, k, _bh = jobs[n]
                if n == 0:
                    pe.wait_ge(qk_ev[1], 3)
                    pe.wait_ge(qk_ev[0], 4)
                elif n >= 2:
                    pe.wait_ge(e_done, n - 1)
                for t in range(TILES):
                    c0, c1 = prob_cols(kind, t)
                    ins = logits(sbank[:, n % 2, c0:c1], q, side, t, khh[:, k, 0:c1 - c0], klo[half_rows(side), k // 2, 0:c1 - c0])
                ins.then_inc(s_done, 1)

            def turn(n):
                kind = jobs[n][0]
                pe.wait_ge(p_done, n + 1)
                if n:
                    pe.wait_ge(te_done, t_count(n) - 1)
                else:
                    pe.wait_ge(cmp_dve, 4)
                pieces = [(0, 0), (P, P), (2 * P, 2 * P)] if kind != "mem" else [(0, 0), (2 * P, P), (P, 2 * P), (3 * P, 3 * P)]
                for src, dst in pieces:
                    ins = nc.tensor.transpose(ptb[:, dst:dst + P], sx[:, n % 2, src:src + P], ident)
                ins.then_inc(t_done, 1)

            def values(n):
                kind, h = jobs[n][0:2]
                starts = kind != "win"
                ends = kind != "sel"
                if n == 0:
                    pe.wait_ge(qk_ev[1], 4)
                elif ends_pair(n - 1):
                    pe.wait_ge(ol_done, pair_of(n))
                dst = ob[HD * (h % 2):HD * (h % 2) + HD]
                if kind == "sel":
                    g = h // HPG
                    nc.tensor.matmul(dst[:, 0:256], vcz[:, g, h % HPG, :], pct[:, g, :], start=True, stop=False)
                    starts = False
                if kind == "moba":
                    c = pat_col(C_VM + HD * h)
                    v = [pat[:, t, c:c + HD] for t in range(2)]
                elif kind == "mem":
                    v = [kvm[:, t, 256 + HD * h:256 + HD * h + HD] for t in range(2)]
                else:
                    c = pat_col((C_VS if kind == "sel" else C_VW) + HD * (h // HPG))
                    v = [pat[:, t, c:c + HD] for t in range(2)]
                pe.wait_ge(te_done, t_count(n))
                nc.tensor.matmul(dst[:, 0:256], v[0], pts[:, n % 2, 0:256], start=starts, stop=False)
                c0 = 0 if kind == "mem" else P
                nc.tensor.matmul(dst[:, c0:256], v[1], pts[:, n % 2, 256:512 - c0], start=False, stop=ends).then_inc(pv_done, 1)

            for n in range(JOBS + 2):
                if n < JOBS:
                    scores(n)
                if n == CMP_SLOT:
                    pe.wait_ge(cmp_dve, 5)
                    pe.wait_ge(te_done, CMP_SLOT - 1)
                    for g in range(GROUPS):
                        for t in range(TILES):
                            ins = nc.tensor.transpose(ptb[:, 256 * g + P * t:256 * g + P * t + P],
                                                      pcz[:, t, g].rearrange("p i c -> p (i c)"), ident)
                    ins.then_inc(t_done, 1)
                if n in (16, 17):
                    pe.wait_ge(ol_done, 2)
                    whole_block(B_MOBA + n - 16, V_GATE + n, 1, oh, ol, 0)
                else:
                    b, i = divmod(n, 4) if n < 16 else divmod(n - 18, 4)
                    b += B_GATE if n < 16 else B_GATE_MEM
                    if i == 0:
                        free_acc(b)
                    sub(V_GATE + n, n % SUBS, b % 2, xh, xl, 2 * i, SLICE, i == 0, i == 3)
                if n == 0:
                    qk_batch(QK_LAST, 6, [col(C_QX), col(C_QX + P)])
                if 1 <= n <= JOBS:
                    turn(n - 1)
                if n >= 2:
                    values(n - 2)

            def merged_banks(first, count):
                pe.wait_ge(y_done, count)
                for j in (first, first + 1):
                    transpose_bank(2, j, yb)

            def new_x_banks(t):
                for n in range(2):
                    pe.wait_ge(x1_done[n], t + 1)
                    pe.wait_ge(tl_done, 8 + 2 * t + n + 1)
                    transpose_bank(3, 2 * t + n, xs)

            pe.wait_ge(ol_done, 4)
            for i in range(2):
                whole_block(B_MEM + i, V_MEM + i, 1, oh, ol, 2)
            for n in range(2):
                v, b = V_NSA + 2 * n, B_NSA + n
                free_acc(b)
                sub(v, v % SUBS, b % 2, oh, ol, 4, SLICE, True, False)
                if n == 0:
                    pe.wait_ge(ol_done, 8)
                else:
                    merged_banks(0, 2)
                sub(v + 1, (v + 1) % SUBS, b % 2, oh, ol, 6, SLICE, False, True)
            whole_block(B_MIX, V_MIX, 4, xh, xl, ready=2, after={0: [lambda: merged_banks(2, 4)]})
            free_acc(B_MIX + 1)
            by_tiles(B_MIX + 1, V_MIX + 4, 4, xh, xl, 0, after={(1, 2): [lambda: new_x_banks(0)]})
            free_acc(B_GU)
            by_tiles(B_GU, V_GU, 4, xh, xl, 0, ready=12, after={(0, 2): [lambda: new_x_banks(1)]})

            def ffn_body(i, j, first):
                if first:
                    free_acc(B_GU + 1)
                else:
                    pe.wait_ge(prod_done, i * 2 - 2)
                for s in range(4):
                    sub(i * 4 + (V_GU + s), s, j, xh, xl, 2 * s, SLICE, s == 0, s == 3)
                    if s == 1:
                        ffn_turn_at(i)

            def ffn_turn_at(i):
                pe.wait_ge(prod_done, i * 2)
                if not isinstance(i, int) or i > 1:
                    pe.wait_ge(al_done, i - 1)
                for kk in range(2):
                    for t in range(TILES):
                        ins = nc.tensor.transpose(ptb[:, 256 * kk + P * t:256 * kk + P * t + P],
                                                  act_tok[:, t, P * kk:P * kk + P], ident)
                ins.then_inc(at_done, 1)

            ffn_body(1, 1, True)
            ffn_body(2, 0, False)
            with nc.tensor.Fori(0, (GU_BLOCKS - 3) // 2) as it:
                for j in range(2):
                    ffn_body(it * 2 + (3 + j), 1 - j, False)
            for n in range(2):
                pe.wait_ge(prod_done, 2 * (GU_BLOCKS - 1 + n))
                for i in range(11 if n == 0 else 8):
                    v = V_DOWN + 11 * n + i
                    sub(v, v % SUBS, (B_DOWN + n) % 2, ah, al, 2 * i, SLICE, i == 0, i == 10)
                    if n == 0 and i == 1:
                        ffn_turn_at(GU_BLOCKS)
                    if n == 0 and i == 8:
                        pe.wait_ge(al_done, GU_BLOCKS)
            by_tiles(B_DOWN + 1, V_DOWN + 19, 3, ah, al, 16, first=False)


def bucket_onehot():
    import numpy as np
    dist = 255 - np.arange(G_W)
    exact = BUCKETS // 2
    safe = np.maximum(dist, 1).astype(np.float32)
    logd = np.log(safe / np.float32(exact)).astype(np.float32) / np.float32(np.log(MAX_DIST / exact))
    large = np.minimum(exact + (logd * np.float32(BUCKETS - exact)).astype(np.int32), BUCKETS - 1)
    bucket = np.where(dist < exact, np.maximum(dist, 0), large)
    hot = (bucket[None, :] == np.arange(BUCKETS)[:, None]) & (dist >= 0)[None, :]
    return hot.astype(np.float32)


NAMES = ["x", "mem", "rel_bias", "pre_mix_g", "mem_norm_g", "post_mix_g", "w_in", "cmp_pos_k", "cmp_w1_k", "cmp_w2_k",
         "cmp_pos_v", "cmp_w1_v", "cmp_w2_v", "w_mem_kv", "w_nsa_o", "w_moba_o", "w_mem_o", "w_mix_out",
         "pre_ffn_g", "post_ffn_g", "w_ffn_gate", "w_ffn_up", "w_ffn_down"]


def kernel(**inputs):
    import numpy as np
    import concourse.bacc as bacc
    from concourse.bass_utils import run_bass_kernel_spmd

    nc = bacc.Bacc("TRN2", target_bir_lowering=False, num_devices=1)
    arrays = {f"in_{n}": np.ascontiguousarray(inputs[n]) for n in NAMES}
    rows = np.arange(SEQ).reshape(TILES, P).T
    eye = np.eye(P, dtype=np.float32)
    sees_block = (rows >= CMP_LEN - 1).astype(np.float32)
    arrays["in_const0"] = np.concatenate([eye, sees_block], axis=1)
    hot = np.zeros((P, G_W), np.float32)
    hot[:BUCKETS] = bucket_onehot()
    arrays["in_const1"] = np.concatenate([eye[::-1], hot], axis=1)
    a = {n[3:]: nc.dram_tensor(n, v.shape, F32, kind="ExternalInput").ap() for n, v in arrays.items()}
    out = nc.dram_tensor("out_0", (1, SEQ, D), F32, kind="ExternalOutput").ap()
    g_scratch = nc.dram_tensor("g_scratch", (BIAS_H, G_W), F32, kind="Internal").ap()
    build_layer(nc, a, out, g_scratch)
    r = run_bass_kernel_spmd(nc, [arrays], core_ids=[0])
    return r.results[0]["out_0"]
```
